# Optimizing a Trainium2 kernel written in Bass

```python
import jax, jax.numpy as jnp
from jax import lax
import numpy as np

D_MODEL = 1024
BATCH = 1
SEQ = 256
DEPTH = 2

PLE_DIM = 256
SC_WIDTH = 512
SC_KERNEL = 3
N_HEADS = 8
QK_NOPE = 64
QK_ROPE = 32
V_HEAD = 64
Q_LORA = 768
KV_LORA = 256
ROPE_THETA = 10000.0
Q_BLOCK = 128
CONF_WIDTH = 512
CONF_KERNEL = 31
N_GROUPS = 4
EXPERTS_PER_GROUP = 8
N_EXPERTS = N_GROUPS * EXPERTS_PER_GROUP
TOP_K = 2
EXPERT_HIDDEN = 256
EPS = 1e-6

SPLIT_SIZES = (D_MODEL, D_MODEL, D_MODEL,
               SC_WIDTH, SC_WIDTH, SC_WIDTH,
               Q_LORA, KV_LORA, QK_ROPE,
               CONF_WIDTH, CONF_WIDTH)
IN_COLS = 3 * D_MODEL + 3 * SC_WIDTH + Q_LORA + KV_LORA + QK_ROPE + 2 * CONF_WIDTH

kernel_name = 'hybrid_gated_sconv_mla_conformer_hmoe'

def rms_norm(x, g):
    x32 = x.astype(jnp.float32)
    y = x32 * lax.rsqrt(jnp.mean(x32 * x32, axis=-1, keepdims=True) + EPS) * g.astype(jnp.float32)
    return y.astype(x.dtype)

def layer_norm(x, g, b):
    x32 = x.astype(jnp.float32)
    mu = jnp.mean(x32, axis=-1, keepdims=True)
    xc = x32 - mu
    var = jnp.mean(xc * xc, axis=-1, keepdims=True)
    y = xc * lax.rsqrt(var + EPS) * g.astype(jnp.float32) + b.astype(jnp.float32)
    return y.astype(x.dtype)

def causal_depthwise_conv(x, w):
    k, c = w.shape
    return lax.conv_general_dilated(x, w[:, None, :], window_strides=(1,), padding=[(k - 1, 0)],
                                    dimension_numbers=('NWC', 'WIO', 'NWC'), feature_group_count=c)

def rope_cos_sin(positions, dim):
    inv_freq = ROPE_THETA ** (-jnp.arange(0, dim, 2, dtype=jnp.float32) / dim)
    ang = positions.astype(jnp.float32)[..., None] * inv_freq
    return jnp.cos(ang), jnp.sin(ang)

def apply_rope(x, cos, sin):
    half = x.shape[-1] // 2
    x1, x2 = x[..., :half], x[..., half:]
    c, s = cos.astype(x.dtype), sin.astype(x.dtype)
    return jnp.concatenate([x1 * c - x2 * s, x1 * s + x2 * c], axis=-1)

def mla_attention(q_nope, q_rope, k_nope, k_rope, v):
    b, s, h, _ = q_nope.shape
    nblk = s // Q_BLOCK
    scale = (QK_NOPE + QK_ROPE) ** -0.5
    k_idx = jnp.arange(s)

    def to_blocks(t):
        return jnp.moveaxis(t.reshape(b, nblk, Q_BLOCK, *t.shape[2:]), 1, 0)

    def one_block(args):
        qn, qr, blk = args
        sc = (jnp.einsum('bqhd,bkhd->bhqk', qn, k_nope)
              + jnp.einsum('bqhr,bkr->bhqk', qr, k_rope)).astype(jnp.float32) * scale
        q_idx = blk * Q_BLOCK + jnp.arange(Q_BLOCK)
        causal = q_idx[:, None] >= k_idx[None, :]
        sc = jnp.where(causal, sc, -jnp.inf)
        pr = jax.nn.softmax(sc, axis=-1).astype(v.dtype)
        return jnp.einsum('bhqk,bkhd->bqhd', pr, v)

    out = lax.map(one_block, (to_blocks(q_nope), to_blocks(q_rope), jnp.arange(nblk)))
    return jnp.moveaxis(out, 0, 1).reshape(b, s, h * V_HEAD)

def mixer_block(xn, cos, sin, w_in, conv_a_w, w_out_a, q_norm_g, w_uq, kv_norm_g, w_ukv, w_out_b,
                conv_c_w, ln_c_g, ln_c_b, w_out_c, w_o):
    b, s, _ = xn.shape
    proj = xn @ w_in
    points, acc = [], 0
    for size in SPLIT_SIZES[:-1]:
        acc += size
        points.append(acc)
    (gate_a, gate_b, gate_c, sc_b, sc_c, sc_u, q_lat, kv_lat, k_rope_raw,
     glu_val, glu_gate) = jnp.split(proj, points, axis=-1)

    y_a = (sc_b * causal_depthwise_conv(sc_c * sc_u, conv_a_w)) @ w_out_a

    q = (rms_norm(q_lat, q_norm_g) @ w_uq).reshape(b, s, N_HEADS, QK_NOPE + QK_ROPE)
    q_nope = q[..., :QK_NOPE]
    q_rope = apply_rope(q[..., QK_NOPE:], cos[:, :, None, :], sin[:, :, None, :])
    kv = (rms_norm(kv_lat, kv_norm_g) @ w_ukv).reshape(b, s, N_HEADS, QK_NOPE + V_HEAD)
    k_nope, v = kv[..., :QK_NOPE], kv[..., QK_NOPE:]
    k_rope = apply_rope(k_rope_raw, cos, sin)
    y_b = mla_attention(q_nope, q_rope, k_nope, k_rope, v) @ w_out_b

    u = glu_val * jax.nn.sigmoid(glu_gate)
    u = causal_depthwise_conv(u, conv_c_w)
    u = jax.nn.silu(layer_norm(u, ln_c_g, ln_c_b))
    y_c = u @ w_out_c

    merged = (jax.nn.sigmoid(gate_a) * y_a + jax.nn.sigmoid(gate_b) * y_b
              + jax.nn.sigmoid(gate_c) * y_c)
    return merged @ w_o

def hier_moe(xn, w_rg, b_rg, w_re, b_re, w_gate, w_up, w_down):
    b, s, _ = xn.shape
    grp_logits = (xn @ w_rg).astype(jnp.float32) + b_rg.astype(jnp.float32)
    pg = jax.nn.softmax(grp_logits, axis=-1)
    g_sel = jnp.argmax(grp_logits, axis=-1)
    g_onehot = jax.nn.one_hot(g_sel, N_GROUPS, dtype=jnp.float32)
    p_sel = jnp.max(pg, axis=-1, keepdims=True)
    exp_logits = ((xn @ w_re).astype(jnp.float32) + b_re.astype(jnp.float32)).reshape(
        b, s, N_GROUPS, EXPERTS_PER_GROUP)
    exp_sel = jnp.sum(exp_logits * g_onehot[..., None], axis=2)
    pe = jax.nn.softmax(exp_sel, axis=-1)
    top_w, top_i = lax.top_k(pe, TOP_K)
    top_w = top_w / jnp.sum(top_w, axis=-1, keepdims=True) * p_sel
    comb_in = jnp.sum(jax.nn.one_hot(top_i, EXPERTS_PER_GROUP, dtype=jnp.float32) * top_w[..., None], axis=-2)
    comb = (g_onehot[..., None] * comb_in[:, :, None, :]).astype(xn.dtype)
    y = jnp.zeros_like(xn)
    for g in range(N_GROUPS):
        sl = slice(g * EXPERTS_PER_GROUP, (g + 1) * EXPERTS_PER_GROUP)
        hg = jnp.einsum('bsd,edf->bsef', xn, w_gate[sl])
        hu = jnp.einsum('bsd,edf->bsef', xn, w_up[sl])
        hh = jax.nn.silu(hg) * hu * comb[:, :, g, :, None]
        y = y + jnp.einsum('bsef,efd->bsd', hh, w_down[sl])
    return y

def setup_inputs(seed: int = 0) -> dict:
    key = jax.random.key(seed)
    ks = iter(jax.random.split(key, 40))

    def w(shape, fan_in):
        return jax.random.normal(next(ks), shape, jnp.float32) * fan_in ** -0.5

    def gain(shape):
        return 1.0 + 0.02 * jax.random.normal(next(ks), shape, jnp.float32)

    def small(shape, scale):
        return scale * jax.random.normal(next(ks), shape, jnp.float32)

    L = DEPTH
    x = jax.random.normal(next(ks), (BATCH, SEQ, D_MODEL), jnp.float32)
    p = jax.random.normal(next(ks), (DEPTH, BATCH, SEQ, PLE_DIM), jnp.float32)
    start = jax.random.randint(next(ks), (BATCH, 1), 0, 1024, dtype=jnp.int32)
    positions = start + jnp.arange(SEQ, dtype=jnp.int32)[None, :]
    return {
        'x': x, 'p': p, 'positions': positions,
        'ln_mix_g': gain((L, D_MODEL)),
        'w_in': w((L, D_MODEL, IN_COLS), D_MODEL),
        'conv_a_w': w((L, SC_KERNEL, SC_WIDTH), SC_KERNEL),
        'w_out_a': w((L, SC_WIDTH, D_MODEL), SC_WIDTH),
        'q_norm_g': gain((L, Q_LORA)),
        'w_uq': w((L, Q_LORA, N_HEADS * (QK_NOPE + QK_ROPE)), Q_LORA),
        'kv_norm_g': gain((L, KV_LORA)),
        'w_ukv': w((L, KV_LORA, N_HEADS * (QK_NOPE + V_HEAD)), KV_LORA),
        'w_out_b': w((L, N_HEADS * V_HEAD, D_MODEL), N_HEADS * V_HEAD),
        'conv_c_w': w((L, CONF_KERNEL, CONF_WIDTH), CONF_KERNEL),
        'ln_c_g': gain((L, CONF_WIDTH)),
        'ln_c_b': small((L, CONF_WIDTH), 0.02),
        'w_out_c': w((L, CONF_WIDTH, D_MODEL), CONF_WIDTH),
        'w_o': w((L, D_MODEL, D_MODEL), D_MODEL),
        'ln_ffn_g': gain((L, D_MODEL)),
        'w_route_grp': w((L, D_MODEL, N_GROUPS), D_MODEL),
        'b_route_grp': small((L, N_GROUPS), 0.01),
        'w_route_exp': w((L, D_MODEL, N_EXPERTS), D_MODEL),
        'b_route_exp': small((L, N_EXPERTS), 0.01),
        'w_exp_gate': w((L, N_EXPERTS, D_MODEL, EXPERT_HIDDEN), D_MODEL),
        'w_exp_up': w((L, N_EXPERTS, D_MODEL, EXPERT_HIDDEN), D_MODEL),
        'w_exp_down': w((L, N_EXPERTS, EXPERT_HIDDEN, D_MODEL), EXPERT_HIDDEN),
        'ln_ple_g': gain((L, D_MODEL)),
        'w_ple_gate': w((L, D_MODEL, D_MODEL), D_MODEL),
        'w_ple': w((L, PLE_DIM, D_MODEL), PLE_DIM),
        'final_norm_g': gain((D_MODEL,)),
    }

def reference(x, p, positions, ln_mix_g, w_in, conv_a_w, w_out_a, q_norm_g, w_uq, kv_norm_g, w_ukv,
              w_out_b, conv_c_w, ln_c_g, ln_c_b, w_out_c, w_o, ln_ffn_g, w_route_grp, b_route_grp,
              w_route_exp, b_route_exp, w_exp_gate, w_exp_up, w_exp_down, ln_ple_g, w_ple_gate, w_ple,
              final_norm_g):
    cos, sin = rope_cos_sin(positions, QK_ROPE)
    for i in range(DEPTH):
        h = rms_norm(x, ln_mix_g[i])
        x = x + mixer_block(h, cos, sin, w_in[i], conv_a_w[i], w_out_a[i], q_norm_g[i], w_uq[i],
                            kv_norm_g[i], w_ukv[i], w_out_b[i], conv_c_w[i], ln_c_g[i], ln_c_b[i],
                            w_out_c[i], w_o[i])
        h = rms_norm(x, ln_ffn_g[i])
        x = x + hier_moe(h, w_route_grp[i], b_route_grp[i], w_route_exp[i], b_route_exp[i],
                         w_exp_gate[i], w_exp_up[i], w_exp_down[i])
        h = rms_norm(x, ln_ple_g[i])
        x = x + jax.nn.sigmoid(h @ w_ple_gate[i]) * (p[i] @ w_ple[i])
    return rms_norm(x, final_norm_g)


_drawn_inputs = setup_inputs


def setup_inputs(seed=0):
    import zlib

    import numpy as np

    out = dict(_drawn_inputs(seed))
    spreads = {}
    factors = {'q_norm_g': 5.089,
     'kv_norm_g': 5.167,
     'ln_c_b': 2.747,
     'b_route_grp': 10.537,
     'b_route_exp': 3.945,
     'ln_ple_g': 18.69,
     'final_norm_g': 20.603,
     'ln_c_g': 3.553}
    for name, (base, spread) in spreads.items():
        noise = np.random.default_rng([zlib.crc32(name.encode()), seed]).standard_normal(out[name].shape)
        drawn = base * np.exp(spread * noise) if base else spread * noise
        out[name] = __import__('jax').numpy.asarray(drawn.astype(out[name].dtype))
    for name, factor in factors.items():
        out[name] = (out[name] * factor).astype(out[name].dtype)
    return out
```

```python
import concourse.bass as bass
from concourse import mybir
from contextlib import ExitStack

F32 = mybir.dt.float32
I32 = mybir.dt.int32
ALU = mybir.AluOpType
ACT = mybir.ActivationFunctionType
AX = mybir.AxisListType

P = 128
DEPTH, S, D = 2, 256, 1024
DC, TC = D // P, S // P
SC, SCC = 512, 4
KA, KC = 3, 31
HEADS, NOPE, ROPE, VH = 8, 64, 32, 64
QK = NOPE + ROPE
QL, KVL = 768, 256
NG, EPG, NE, FH = 4, 8, 32, 256
PAIRS = 2 * S
WIN = 64
WIDE = S // WIN
SLOTS = PAIRS + WIN
EPS = 1e-6
SCALE = float(QK) ** -0.5
BIG = 1e30
OFF_SC = 3 * D
OFF_Q = OFF_SC + 3 * SC
OFF_KV = OFF_Q + QL
OFF_KR = OFF_KV + KVL
OFF_GV = OFF_KR + ROPE
OFF_GG = OFF_GV + SC
INV_2PI = 0.15915494309189535
ROUND = 1.5 * 2.0 ** 23
TWO_PI = (6.28125, 0.001934051513671875, 1.255665914356996e-06)
PI_IN = 3.1415925
HALF_PI = 1.5707963267948966
ROPE_STEPS = 10

C_ID, C_UP, C_CAUSAL, C_ROT, C_FREQ, C_IOTA = 0, P, 2 * P, 3 * P, 3 * P + QK, 3 * P + QK + 1
C_COLS = C_IOTA + PAIRS

VEC = {}
_at = 0
for _name, _n in (("mix", DC), ("q", QL // P), ("kv", KVL // P), ("lng", SCC), ("lnb", SCC),
                  ("ffn", DC), ("ple", DC), ("ca", KA * SCC)):
    VEC[_name] = _at
    _at += _n
VROWS = _at
CROWS = KC * SCC

RING = 3
SLOT = 2048
CHUNKS = (["kv"] + [f"q{i}" for i in range(3)] + ["ukv"] + [f"uq{i}" for i in range(4)]
          + ["gg0", "gv0", "gg1", "gv1"] + ["c0", "u0", "b0", "c1", "u1", "b1"]
          + [f"{x}{m}" for m in range(4) for x in ("ga", "gb", "gc", "yab", "yc")]
          + [f"wo{m}" for m in range(4)] + ["pp"] + [f"pg{m}" for m in range(4)])
CI = {c: i for i, c in enumerate(CHUNKS)}
NC = len(CHUNKS)
assert NC % RING == 0

FILL = ["c0", "u0", "b0", "c1", "u1", "b1"]
UNITS = (["kv", "kr", "q0", "q1", "q2", "rotk", "kn0", "kn1", "kn2", "kn3", "v0", "v1",
          "uq0", "uq1", "rot0", "uq2", "rot1", "uq3", "rot2", "gg0", "rot3", "gv0", "gg1", "gv1"]
         + FILL
         + [f"{x}{m}" for m in range(4) for x in ("ga", "gb", "gc", "ya", "yb", "yc")]
         + [f"wo{m}" for m in range(4)] + ["lg", "rank"] + [f"cb{m}" for m in range(4)]
         + ["pp0", "pp1", "pg0", "pp2", "pg1", "pp3", "pg2", "pg3"])
UI = {u: i for i, u in enumerate(UNITS)}
NU = len(UNITS)
BANKS = 3


def chunk_of(unit):
    if unit in CI:
        return unit
    if unit[:2] == "kn" or unit in ("v0", "v1"):
        return "ukv"
    if unit[:2] in ("ya", "yb"):
        return "yab" + unit[2:]
    if unit[:2] == "pp":
        return "pp"
    return None


LAST_UNIT = {}
for _u in UNITS:
    if chunk_of(_u):
        LAST_UNIT[chunk_of(_u)] = UI[_u]

NORMS = ["mix", "kv", "q", "lnm", "lnv", "ffn", "ple"]
POWS = ["mix", "kv", "q", "lnv", "ffn", "ple"]
SQUARES = ([f"mix{i}" for i in range(4)] + ["kv", "q0", "q1", "q2", "lnv"]
           + [f"ffn{i}" for i in range(4)] + [f"ple{i}" for i in range(4)])


def after(events, name):
    return events.index(name) + 1


def program(nc, x, p, positions, ln_mix_g, w_in, conv_a_w, w_out_a, q_norm_g, w_uq, kv_norm_g, w_ukv,
            w_out_b, conv_c_w, ln_c_g, ln_c_b, w_out_c, w_o, ln_ffn_g, w_route_grp, b_route_grp,
            w_route_exp, b_route_exp, w_exp_gate, w_exp_up, w_exp_down, ln_ple_g, w_ple_gate, w_ple,
            final_norm_g, consts, out, windows=WIN):
    ctx = ExitStack()
    with ctx:
        def sb(name, shape, dt=F32):
            return ctx.enter_context(nc.sbuf_tensor(name, shape, dt))

        def sem(name):
            return ctx.enter_context(nc.semaphore(name))

        ring = sb("ring", [P, RING, SLOT])
        ering = sb("ering", [P, 4, 3, SLOT])
        xT = sb("xT", [P, DC, S])
        hT = sb("hT", [P, DC, S])
        cst = sb("cst", [P, C_COLS])
        ones = sb("ones", [P, P])
        mhalf = sb("mhalf", [P, 2])
        last_act = sb("last_act", [P, 1])
        last_dve = sb("last_dve", [P, 1])
        cosT = sb("cosT", [QK, S])
        sinT = sb("sinT", [QK, S])
        bc = sb("bc", [P, S])
        bcs = sb("bcs", [P, S])
        diag = sb("diag", [P, 2, P])
        col = sb("col", [P, len(NORMS), 2, 2])
        vrow = sb("vrow", [VROWS, P])
        crow = sb("crow", [CROWS, P])
        vecT = sb("vecT", [P, VROWS])
        convT = sb("convT", [P, CROWS])
        w_rt = sb("w_rt", [P, DC, NG + NE])
        b_rt = sb("b_rt", [P, TC, NG + NE])
        w_kr = sb("w_kr", [P, DC, QK])
        prow = sb("prow", [P, TC, S])
        pT = sb("pT", [P, 2, S])
        starts = sb("starts", [1, WIDE * NE], I32)
        most = sb("most", [1, 1], I32)
        mx = sb("mx", [P, 2, 2, 3])
        work = sb("work", [P, 12928])
        ps = ctx.enter_context(nc.psum_tensor("ps", [P, 8, 512], F32))

        ident = cst[:, C_ID:C_ID + P]
        upper = cst[:, C_UP:C_UP + P]
        causal = cst[:, C_CAUSAL:C_CAUSAL + P]
        rot = cst[0:QK, C_ROT:C_ROT + QK]
        freq = cst[NOPE:QK, C_FREQ:C_FREQ + 1]
        iota = cst[:, C_IOTA:C_IOTA + PAIRS]

        def area(at, *dims):
            n = 1
            for d in dims:
                n *= d
            v = work[:, at:at + n]
            if len(dims) == 2:
                return v.rearrange("p (a b) -> p a b", a=dims[0])
            if len(dims) == 3:
                return v.rearrange("p (a b c) -> p a b c", a=dims[0], b=dims[1])
            return v

        qn = area(0, 6, S)
        kvn = area(1536, 2, S)
        scu = area(0, SCC, S + KA - 1)
        ya = area(1032, SCC, S)
        qT = area(2056, HEADS, S)
        sq_q = area(2056, 6, S)
        sq_kv = area(2056 + 1536, 2, S)
        merged = area(2056, DC, S)
        kT = area(4104, HEADS, S)
        sq_x = area(4104, DC, S)
        v = area(6152, TC, SC)
        attnT = area(7176, SCC, S)
        rtmp = area(7176, 2, 2, S)
        probs = area(8200, 2, 384)
        probsT = area(8200 + 768, 2, 384)
        upad = area(9736, SCC, S + KC - 1)
        conv = area(10880, SCC, S)
        kr = area(10880, 2, S)
        tmp = area(11904, 2, 512)
        sq_ln = area(11904, SCC, S)
        glu_t = [area(11904, 2, 512), area(8200, 2, 512)]
        gate_t = [area(8200, 3, 512), area(4104, 3, 512)]
        ys = area(0, DC, SLOTS)
        h_tok = area(0, TC, D)
        sel = area(2048, TC, PAIRS)
        sel_t = area(3072, TC, PAIRS)
        xs = area(4608, DC, SLOTS)
        gw = area(9216, TC, PAIRS)
        xw = area(10240, 2, DC, WIN)
        hhT = area(11264, 2, 2 * WIN)
        hflat = hT[0:WIN, :, :].rearrange("p c n -> p (c n)")
        yrow = hflat[:, 0:D]
        sg = hflat[:, D:D + 2 * FH].rearrange("p (b n) -> p b n", b=2)
        hh = hflat[:, D + 2 * FH:D + 4 * FH].rearrange("p (b n) -> p b n", b=2)
        y_tok = area(4608, 4, D)
        gwT = area(11776, 4, S)
        route_at = [10240]

        def rt(n):
            route_at[0] += 2 * n
            assert route_at[0] <= 12928
            return area(route_at[0] - 2 * n, 2, n)

        logit, gmax, geq, gval, gmin, gone, gpen = rt(NG + NE), rt(1), rt(NG), rt(NG), rt(1), rt(NG), rt(NG)
        masked, masked2 = rt(NE), rt(NE)
        top, teq, tval, tmin = [rt(1), rt(1)], [rt(NE), rt(NE)], [rt(NE), rt(NE)], [rt(1), rt(1)]
        one = [rt(NE), rt(NE)]
        chosen = rt(NE)
        expd, gsum, dplus, weight = rt(NG + 1), rt(1), rt(1), [rt(1), rt(1)]
        ranks = area(route_at[0], 3 * NE)
        route_at[0] += 3 * NE
        prefix = [rt(24), rt(24)]
        prefix = [f.rearrange("p a b -> p (a b)") for f in prefix]
        base, prod, pos = rt(NE), [rt(NE), rt(NE)], [rt(1), rt(1)]
        off = rt(NE // 2).rearrange("p a b -> p (a b)")
        sq_p = area(0, DC, S)
        ple_t = [area(2048, 512), area(2560, 512)]
        ppt = [area(3072, 512), area(3584, 512)]
        xin = area(0, TC, D)
        gfull = area(8192, D)
        xout = area(9216, TC, D)
        ang = area(8192, 4, S)

        init_loaded = sem("init_loaded")
        small_loaded = sem("small_loaded")
        route_loaded = sem("route_loaded")
        wait_carried = sem("wait_carried")
        chunk_loaded = [sem(f"chunk_loaded{i}") for i in range(RING)]
        gu_loaded = [sem(f"gu_loaded{i}") for i in range(4)]
        down_loaded = [sem(f"down_loaded{i}") for i in range(4)]
        unit_ready = sem("unit_ready")
        gu_ready = sem("gu_ready")
        down_ready = sem("down_ready")
        layer_over = sem("layer_over")
        x_tr = sem("x_tr")
        x_in = sem("x_in")
        rope_step = sem("rope_step")
        rope_sin = sem("rope_sin")
        const_set = sem("const_set")
        out_stored = sem("out_stored")
        zeroed = []

        def lsem(name):
            zeroed.append(sem(name))
            return zeroed[-1]

        evacuated = [lsem(f"evacuated{i}") for i in range(BANKS)]
        vec_tr = lsem("vec_tr")
        vec_ready = lsem("vec_ready")
        h_ready = lsem("h_ready")
        sq_ready = lsem("sq_ready")
        stat_ready = lsem("stat_ready")
        ms_ready = lsem("ms_ready")
        pow_ready = lsem("pow_ready")
        diag_ready = lsem("diag_ready")
        bcast_ready = lsem("bcast_ready")
        bcast_used = lsem("bcast_used")
        dve_step = lsem("dve_step")
        mean_ready = lsem("mean_ready")
        mask_step = lsem("mask_step")
        short_step = lsem("short_step")
        kvn_ready = lsem("kvn_ready")
        qn_ready = lsem("qn_ready")
        k_ready = lsem("k_ready")
        q_cos = lsem("q_cos")
        q_ready = lsem("q_ready")
        glu_sig = lsem("glu_sig")
        u_ready = lsem("u_ready")
        pad_zero = lsem("pad_zero")
        conv_step = lsem("conv_step")
        score_ready = lsem("score_ready")
        max_ready = lsem("max_ready")
        exp_ready = lsem("exp_ready")
        recip_ready = lsem("recip_ready")
        probs_ready = lsem("probs_ready")
        pT_psum = lsem("pT_psum")
        pT_ready = lsem("pT_ready")
        pv_ready = lsem("pv_ready")
        attn_ready = lsem("attn_ready")
        scu_ready = lsem("scu_ready")
        ya_ready = lsem("ya_ready")
        xc_ready = lsem("xc_ready")
        ln_step = lsem("ln_step")
        ln_sig = lsem("ln_sig")
        yc_ready = lsem("yc_ready")
        gate_sig = lsem("gate_sig")
        merge_step = lsem("merge_step")
        merged_ready = lsem("merged_ready")
        tok_psum = lsem("tok_psum")
        tok_read = [lsem("tok_read_act"), lsem("tok_read_dve")]
        onehot_ready = lsem("onehot_ready")
        top_diff = lsem("top_diff")
        top_exp = lsem("top_exp")
        sel_ready = lsem("sel_ready")
        gw_ready = lsem("gw_ready")
        starts_ready = lsem("starts_ready")
        gather_psum = lsem("gather_psum")
        xs_read = [lsem("xs_read_act"), lsem("xs_read_dve")]
        xs_pad = lsem("xs_pad")
        xw_ready = lsem("xw_ready")
        wide_gu = lsem("wide_gu")
        wide_down = lsem("wide_down")
        sg_ready = lsem("sg_ready")
        hh_part = lsem("hh_part")
        hh_ready = lsem("hh_ready")
        hh_tr = lsem("hh_tr")
        hhT_ready = lsem("hhT_ready")
        yrow_ready = [lsem("yrow_ready_act"), lsem("yrow_ready_dve")]
        yT_psum = lsem("yT_psum")
        ys_ready = lsem("ys_ready")
        gwT_psum = lsem("gwT_psum")
        gwT_ready = lsem("gwT_ready")
        ytok_psum = lsem("ytok_psum")
        ytok_read = [lsem("ytok_read_act"), lsem("ytok_read_dve")]
        pT_tr = lsem("pT_tr")
        p_ready = lsem("p_ready")
        psig_ready = lsem("psig_ready")
        pmul_ready = lsem("pmul_ready")
        engines_done = lsem("engines_done")

        def begin(eng, layers):
            eng.wait_ge(layer_over, layers)
            eng.sem_inc(wait_carried, 1)

        def unit_value(l, name):
            return NU * (l + 1) + UI[name] + 1

        def wait_unit(eng, l, name):
            eng.wait_ge(unit_ready, unit_value(l, name))

        def bank(name):
            return ps[:, UI[name] % BANKS, :]

        def wait_evacuated(eng, name):
            eng.wait_ge(evacuated[UI[name] % BANKS], UI[name] // BANKS + 1)

        def evacuates(instruction, name):
            instruction.then_inc(evacuated[UI[name] % BANKS], 1)

        def two(ap):
            return ap.rearrange("p (a b) -> p a b", a=2)

        def bc2(n=2):
            return bc[:, :].unsqueeze(1).to_broadcast([P, n, S])

        def vcol(name, i):
            return vecT[:, VEC[name] + i:VEC[name] + i + 1]

        block = ctx.enter_context(nc.Block())

        @block.sync
        def _(sp):
            sp.dma_start(xin, x[0].rearrange("(t q) d -> q t d", q=P)).then_inc(init_loaded, 16)
            sp.dma_start(cst[:, :], consts[:, :]).then_inc(init_loaded, 16)
            sp.dma_start(ang[NOPE:QK, 0, :].bitcast(I32), positions[0].partition_broadcast(ROPE)).then_inc(init_loaded, 16)
            sp.sem_inc(unit_ready, NU)
            sp.sem_inc(gu_ready, NE)
            sp.sem_inc(down_ready, NE)

            gate_flat = w_exp_gate.rearrange("l e d f -> (l e) d f")
            up_flat = w_exp_up.rearrange("l e d f -> (l e) d f")
            down_flat = w_exp_down.rearrange("l e f d -> (l e) f d")

            def cols(w, at, n):
                return w[:, at:at + n].rearrange("(c q) n -> q c n", q=P)

            def source(l, name):
                kind, m = name.rstrip("0123456789"), name[len(name.rstrip("0123456789")):]
                m = int(m) if m else 0
                if kind in ("ga", "gb", "gc"):
                    return [cols(w_in[l], "abc".index(kind[1]) * D + 256 * m, 256)]
                if kind in ("b", "c", "u"):
                    return [cols(w_in[l], OFF_SC + "bcu".index(kind) * SC + 256 * m, 256)]
                if kind == "q":
                    return [cols(w_in[l], OFF_Q + 256 * m, 256)]
                if kind == "kv":
                    return [cols(w_in[l], OFF_KV, 256)]
                if kind == "gv":
                    return [cols(w_in[l], OFF_GV + 256 * m, 256)]
                if kind == "gg":
                    return [cols(w_in[l], OFF_GG + 256 * m, 256)]
                if kind == "ukv":
                    return [cols(w_ukv[l], 0, HEADS * (NOPE + VH))]
                if kind == "uq":
                    return [cols(w_uq[l], 2 * QK * m, 2 * QK)]
                if kind == "yab":
                    return [cols(w_out_a[l], 256 * m, 256), cols(w_out_b[l], 256 * m, 256)]
                if kind == "yc":
                    return [cols(w_out_c[l], 256 * m, 256)]
                if kind == "wo":
                    return [cols(w_o[l], 256 * m, 256)]
                if kind == "pp":
                    return [cols(w_ple[l], 0, D)]
                return [cols(w_ple_gate[l], 256 * m, 256)]

            def load_chunk(l, name):
                n = CI[name]
                if n >= RING:
                    sp.wait_ge(unit_ready, NU * (l + 1) + LAST_UNIT[CHUNKS[n - RING]] + 1)
                else:
                    sp.wait_ge(unit_ready, NU * l + LAST_UNIT[CHUNKS[n - RING]] + 1)
                sp.sem_inc(wait_carried, 1)
                at = 0
                parts = source(l, name)
                for i, src in enumerate(parts):
                    k, w = src.shape[1], src.shape[2]
                    dst = ring[:, n % RING, at:at + k * w].rearrange("p (k n) -> p k n", k=k)
                    at += k * w
                    sp.dma_start(dst, src).then_inc(chunk_loaded[n % RING], 16)

            def load_expert(l, e, s):
                sp.wait_ge(gu_ready, NE * (l + 1) + e - 3)
                sp.dma_start(ering[:, s, 0, :], gate_flat[l * NE + e].rearrange("(q c) f -> q (c f)", q=P)).then_inc(gu_loaded[s], 16)
                sp.dma_start(ering[:, s, 1, :], up_flat[l * NE + e].rearrange("(q c) f -> q (c f)", q=P)).then_inc(gu_loaded[s], 16)
                sp.wait_ge(down_ready, NE * (l + 1) + e - 3)
                sp.dma_start(ering[:, s, 2, :].rearrange("p (c d) -> p c d", c=2),
                             down_flat[l * NE + e].rearrange("(c q) d -> q c d", q=P)).then_inc(down_loaded[s], 16)

            with sp.Fori(0, DEPTH) as l:
                load_chunk(l, CHUNKS[0])
                sp.wait_ge(unit_ready, NU * l + UI["pp0"] + 1)
                sp.sem_inc(wait_carried, 1)
                for name, w in (("mix", ln_mix_g), ("q", q_norm_g), ("kv", kv_norm_g), ("lng", ln_c_g),
                                ("lnb", ln_c_b), ("ffn", ln_ffn_g), ("ple", ln_ple_g)):
                    n = w.shape[1] // P
                    sp.dma_start(vrow[VEC[name]:VEC[name] + n, :], w[l].rearrange("(c q) -> c q", q=P)).then_inc(small_loaded, 16)
                sp.dma_start(vrow[VEC["ca"]:VEC["ca"] + KA * SCC, :], conv_a_w[l].rearrange("k (c q) -> (k c) q", q=P)).then_inc(small_loaded, 16)
                sp.dma_start(crow[:, :], conv_c_w[l].rearrange("k (c q) -> (k c) q", q=P)).then_inc(small_loaded, 16)
                sp.dma_start(w_kr[:, :, :], cols(w_in[l], OFF_KR - NOPE, QK)).then_inc(small_loaded, 16)
                for c in CHUNKS[1:4]:
                    load_chunk(l, c)
                sp.dma_start(w_rt[:, :, 0:NG], cols(w_route_grp[l], 0, NG)).then_inc(route_loaded, 16)
                sp.dma_start(w_rt[:, :, NG:NG + NE], cols(w_route_exp[l], 0, NE)).then_inc(route_loaded, 16)
                for t in range(TC):
                    sp.dma_start(b_rt[:, t, 0:NG], b_route_grp[l].partition_broadcast(P)).then_inc(route_loaded, 16)
                    sp.dma_start(b_rt[:, t, NG:NG + NE], b_route_exp[l].partition_broadcast(P)).then_inc(route_loaded, 16)
                sp.dma_start(prow[:, :, :], p[l, 0].rearrange("(t q) d -> q t d", q=P)).then_inc(route_loaded, 16)
                for c in CHUNKS[4:16]:
                    load_chunk(l, c)
                for s in range(4):
                    load_expert(l, s, s)
                    for c in CHUNKS[16 + s:17 + s]:
                        load_chunk(l, c)
                for c in CHUNKS[20:CI["wo3"] + RING]:
                    load_chunk(l, c)
                with sp.Fori(1, NE // 4) as it:
                    for s in range(4):
                        load_expert(l, it * 4 + s, s)
                for c in CHUNKS[CI["wo3"] + RING:]:
                    load_chunk(l, c)
            sp.wait_ge(layer_over, DEPTH + 1)
            sp.dma_start(gfull, final_norm_g.partition_broadcast(P)).then_inc(init_loaded, 16)
            for t in range(TC):
                sp.wait_ge(pmul_ready, t + 1)
                sp.dma_start(out[0, t * P:(t + 1) * P, :], xout[:, t, :]).then_inc(out_stored, 16)
            sp.wait_ge(out_stored, 16 * TC)

        SMALL = 10
        ROUTES = 2 + 2 * TC + 1

        def wait_last_ys(eng, most_reg, windows, ys_sem):
            with eng.If(most_reg > windows):
                eng.wait_ge(ys_sem, WIDE * NE)
            with eng.Else():
                eng.wait_ge(ys_sem, NE)

        def expert_of(w, i, per):
            return w if per == 1 else (w - i % per) // per

        def windows_of(eng, per, step):
            n = 4 * per
            for i in range(n):
                step(0, i, i, True, False)
            with eng.Fori(1, NE // 4) as it:
                for i in range(n):
                    step(it, it * n + i, i, False, False)
            for i in (n, n + 1):
                step(NE // 4 - 1, (NE // 4 - 1) * n + i, i, False, True)

        def wait_gate_up(eng, l, w, i, per):
            if i % per == per - 1:
                eng.wait_ge(gu_ready, NE * (l + 1) + expert_of(w, i, per) + 1)
            else:
                eng.wait_ge(wide_gu, expert_of(w, i, per) * (per - 1) + i % per + 1)

        def wait_down(eng, l, w, i, per):
            if i % per == per - 1:
                eng.wait_ge(down_ready, NE * (l + 1) + expert_of(w, i, per) + 1)
            else:
                eng.wait_ge(wide_down, expert_of(w, i, per) * (per - 1) + i % per + 1)

        @block.tensor
        def _(pe):
            def mm(o, lhsT, rhs, first, last):
                return nc.tensor.matmul(o, lhsT, rhs, start=first, stop=last)

            def tr(o, i, n=P):
                return nc.tensor.transpose(o, i, ident[0:n, 0:n])

            pe.wait_ge(init_loaded, 48)
            for c in range(DC):
                for t in range(TC):
                    last = tr(ps[:, c // 2, (c % 2) * S + t * P:(c % 2) * S + (t + 1) * P], xin[:, t, c * P:(c + 1) * P])
                if c % 2:
                    last.then_inc(x_tr, 1)

            def stat(name, tiles, squares):
                n = len(tiles)
                if name != NORMS[0]:
                    pe.wait_ge(bcast_used, after(NORMS, name) - 1)
                for t in range(TC):
                    for c in range(n):
                        if t == 0 and squares[c] is not None:
                            pe.wait_ge(*squares[c])
                        last = mm(ps[:, 3, t:t + 1], tiles[c][:, t * P:(t + 1) * P], ones[:, 0:1], c == 0, c == n - 1)
                last.then_inc(stat_ready, 1)

            def bcast(name):
                pe.wait_ge(diag_ready, after(NORMS, name))
                for t in range(TC):
                    last = mm(ps[:, 3, S + t * P:S + (t + 1) * P], ones[:, :], diag[:, t, :], True, True)
                last.then_inc(bcast_ready, 1)

            def sq_events(name, n):
                return [(sq_ready, after(SQUARES, f"{name}{c // 2}")) for c in range(n)]

            with pe.Fori(0, DEPTH) as l:
                begin(pe, l + 1)

                def wait_chunk(name):
                    n = CI[name]
                    slot = n % RING
                    upto = sum(2 if c[:3] == "yab" else 1 for c in CHUNKS[slot:n + 1:RING])
                    whole = sum(2 if c[:3] == "yab" else 1 for c in CHUNKS[slot::RING])
                    pe.wait_ge(chunk_loaded[slot], l * (16 * whole) + 16 * upto)

                def free_bank(name):
                    if UI[name] >= BANKS:
                        wait_evacuated(pe, UNITS[UI[name] - BANKS])

                def project(name, rhs, k, waits=(), at=0, width=256):
                    wait_chunk(chunk_of(name))
                    free_bank(name)
                    w = ring[:, CI[chunk_of(name)] % RING, at:at + k * width].rearrange("p (k n) -> p k n", k=k)
                    for m in range(2):
                        for c in range(k):
                            if m == 0 and waits:
                                if waits[c] is not None:
                                    pe.wait_ge(*waits[c])
                            last = mm(two(bank(name))[:, m, :], w[:, c, m * P:(m + 1) * P], rhs[:, c, :], c == 0, c == k - 1)
                    last.then_inc(unit_ready, 1)

                def h_events(name):
                    return [(h_ready, DC * ["mix", "ffn", "ple"].index(name) + c + 1) for c in range(DC)]

                pe.wait_ge(small_loaded, l * (16 * SMALL) + 16 * SMALL)
                tr(ps[:, 6, 0:CROWS], crow[:, :], CROWS).then_inc(vec_tr, 1)
                tr(ps[:, 7, 0:VROWS], vrow[:, :], VROWS).then_inc(vec_tr, 1)
                stat("mix", [sq_x[:, c, :] for c in range(DC)], sq_events("mix", DC))
                project("kv", hT, DC, h_events("mix"))
                for c in range(DC):
                    last = mm(bank("kr")[0:QK, 0:S], w_kr[:, c, :], hT[:, c, :], c == 0, c == DC - 1)
                last.then_inc(unit_ready, 1)
                bcast("mix")
                project("q0", hT, DC)
                project("q1", hT, DC)
                stat("kv", [sq_kv[:, c, :] for c in range(2)], [(sq_ready, after(SQUARES, "kv"))] * 2)
                project("q2", hT, DC)
                bcast("kv")
                free_bank("rotk")
                wait_evacuated(pe, "kr")
                mm(bank("rotk")[0:QK, 0:S], rot, kr[0:QK, 0, :], True, True).then_inc(unit_ready, 1)
                wait_chunk("ukv")
                ukv = ring[:, CI["ukv"] % RING, :].rearrange("p (k h n) -> p k h n", k=2, h=HEADS)
                pe.wait_ge(kvn_ready, 2)
                for i in range(4):
                    free_bank(f"kn{i}")
                    for j in range(2):
                        for c in range(2):
                            last = mm(two(bank(f"kn{i}"))[0:NOPE, j, :], ukv[:, c, 2 * i + j, 0:NOPE], kvn[:, c, :], c == 0, c == 1)
                    last.then_inc(unit_ready, 1)
                for t in range(TC):
                    free_bank(f"v{t}")
                    for c in range(2):
                        last = mm(bank(f"v{t}").rearrange("p (h n) -> p h n", h=HEADS), kvn[:, c, t * P:(t + 1) * P],
                                  ukv[:, c, :, NOPE:NOPE + VH], c == 0, c == 1)
                    last.then_inc(unit_ready, 1)
                stat("q", [sq_q[:, c, :] for c in range(6)], sq_events("q", 6))
                bcast("q")

                def queries(i):
                    wait_chunk(f"uq{i}")
                    free_bank(f"uq{i}")
                    w = ring[:, CI[f"uq{i}"] % RING, 0:6 * 2 * QK].rearrange("p (k n) -> p k n", k=6)
                    for j in range(2):
                        for c in range(6):
                            if i == 0 and j == 0:
                                pe.wait_ge(qn_ready, c + 1)
                            last = mm(two(bank(f"uq{i}"))[0:QK, j, :], w[:, c, j * QK:(j + 1) * QK], qn[:, c, :], c == 0, c == 5)
                    last.then_inc(unit_ready, 1)

                def rotate(i):
                    wait_evacuated(pe, f"uq{i}")
                    free_bank(f"rot{i}")
                    mm(bank(f"rot{i}")[0:QK, :], rot, qT[0:QK, 2 * i:2 * i + 2, :], True, True).then_inc(unit_ready, 1)

                queries(0)
                queries(1)
                rotate(0)
                queries(2)
                rotate(1)
                queries(3)
                rotate(2)
                project("gg0", hT, DC)
                rotate(3)
                project("gv0", hT, DC)
                project("gg1", hT, DC)
                project("gv1", hT, DC)

                def scores(h):
                    pe.wait_ge(q_ready, h // 2 + 1)
                    if h == 0:
                        pe.wait_ge(k_ready, 1)
                        for i in range(4):
                            wait_evacuated(pe, f"kn{i}")
                    if h >= 2:
                        pe.wait_ge(exp_ready, 2 * (h - 1))
                    mm(ps[:, 4 + h % 2, 0:P], qT[0:QK, h, 0:P], kT[0:QK, h, 0:P], True, True)
                    mm(ps[:, 4 + h % 2, P:3 * P], qT[0:QK, h, P:S], kT[0:QK, h, :], True, True).then_inc(score_ready, 1)

                def transpose_probs(h):
                    pe.wait_ge(probs_ready, 2 * (h + 1))
                    if h >= 1:
                        pe.wait_ge(pT_ready, h)
                    for i in range(3):
                        last = tr(ps[:, 6, i * P:(i + 1) * P], probs[:, h % 2, i * P:(i + 1) * P])
                    last.then_inc(pT_psum, 1)

                def weigh_values(h):
                    pe.wait_ge(pT_ready, h + 1)
                    if h == 0:
                        wait_evacuated(pe, "v0")
                        wait_evacuated(pe, "v1")
                    if h >= 1:
                        pe.wait_ge(attn_ready, h)
                    o = ps[:, 7, 0:S]
                    mm(o, v[:, 0, (h // 2) * P:(h // 2 + 1) * P], probsT[:, h % 2, 0:S], True, False)
                    mm(o[:, P:S], v[:, 1, (h // 2) * P:(h // 2 + 1) * P], probsT[:, h % 2, S:3 * P], False, True).then_inc(pv_ready, 1)

                scores(0)
                scores(1)
                for h in range(HEADS):
                    transpose_probs(h)
                    if h + 2 < HEADS:
                        scores(h + 2)
                    if h < len(FILL):
                        project(FILL[h], hT, DC)
                    weigh_values(h)

                for m in range(4):
                    project(f"ga{m}", hT, DC)
                    if m == 0:
                        stat("lnm", [conv[:, c, :] for c in range(SCC)], [(conv_step, KC * SCC)] + [None] * 3)
                    project(f"gb{m}", hT, DC)
                    if m == 0:
                        bcast("lnm")
                    project(f"gc{m}", hT, DC)
                    if m == 0:
                        pe.wait_ge(ya_ready, 2)
                    project(f"ya{m}", ya, SCC)
                    if m == 0:
                        stat("lnv", [sq_ln[:, c, :] for c in range(SCC)], [(sq_ready, after(SQUARES, "lnv"))] + [None] * 3)
                        pe.wait_ge(attn_ready, HEADS)
                    project(f"yb{m}", attnT, SCC, at=SLOT // 2)
                    if m == 0:
                        bcast("lnv")
                    project(f"yc{m}", conv, SCC, [(yc_ready, c + 1) for c in range(SCC)])
                for m in range(4):
                    project(f"wo{m}", merged, DC, [(merged_ready, c // 2 + 1) for c in range(DC)])

                stat("ffn", [sq_x[:, c, :] for c in range(DC)], sq_events("ffn", DC))
                bcast("ffn")
                free_bank("lg")
                pe.wait_ge(route_loaded, l * (16 * ROUTES) + 16 * ROUTES)
                lgp = bank("lg")[:, 0:TC * (NG + NE)].rearrange("p (t n) -> p t n", t=TC)
                for t in range(TC):
                    for c in range(DC):
                        if t == 0:
                            pe.wait_ge(h_ready, DC + c + 1)
                        last = mm(lgp[:, t, :], hT[:, c, t * P:(t + 1) * P], w_rt[:, c, :], c == 0, c == DC - 1)
                last.then_inc(unit_ready, 1)
                for i in range(4):
                    for j in range(4):
                        t, c = i // 2, (i % 2) * 4 + j
                        last = tr(ps[:, 4 + i, j * P:(j + 1) * P], hT[:, c, t * P:(t + 1) * P])
                    last.then_inc(tok_psum, 1)
                free_bank("rank")
                pe.wait_ge(onehot_ready, 1)
                a0, a1 = chosen[:, 0, :], chosen[:, 1, :]
                rk = bank("rank")
                mm(rk[:, 0:NE], upper, a0, True, True)
                mm(rk[:, NE:2 * NE], ones[:, :], a0, True, False)
                mm(rk[:, NE:2 * NE], upper, a1, False, True)
                mm(rk[:, 2 * NE:3 * NE], ones[:, :], a0, True, False)
                mm(rk[:, 2 * NE:3 * NE], ones[:, :], a1, False, True).then_inc(unit_ready, 1)
                pe.wait_ge(tok_read[0], 2)
                pe.wait_ge(tok_read[1], 2)
                for c in range(DC):
                    for t in range(TC):
                        if c == 0:
                            pe.wait_ge(sel_ready, t + 1)
                        if t == 0 and c >= 4:
                            pe.wait_ge(xs_read[c % 2], (c - 4) // 2 + 1)
                        last = mm(ps[:, 4 + c % 4, :], h_tok[:, t, :].rearrange("p (q c) -> p c q", c=DC)[:, c, :],
                                  sel[:, t, :], t == 0, t == TC - 1)
                    last.then_inc(gather_psum, 1)

                def experts(per):
                    def gate_up(it, w, i, first):
                        s, b = (i // per) % 4, i % 2
                        if i % per == 0:
                            pe.wait_ge(gu_loaded[s], l * (32 * NE // 4) + it * 32 + 32)
                        pe.wait_ge(xw_ready, w + 1)
                        if not (first and i < 2):
                            pe.wait_ge(hh_ready, w - 1)
                        for c in range(DC):
                            last = mm(two(ps[0:WIN, b, :]), xw[:, b, c, :], ering[:, s, 0:2, c * FH:(c + 1) * FH], c == 0, c == DC - 1)
                        last.then_inc(gu_ready if i % per == per - 1 else wide_gu, 1)

                    def turn_hidden(it, w, i):
                        b = i % 2
                        pe.wait_ge(hh_ready, w + 1)
                        pe.sem_inc(wait_carried, 1)
                        for c in range(2):
                            last = tr(ps[:, 4 + b, c * WIN:(c + 1) * WIN], hh[:, b, c * P:(c + 1) * P], WIN)
                        last.then_inc(hh_tr, 1)

                    def down(it, w, i):
                        s, b = (i // per) % 4, i % 2
                        if i % per == 0:
                            pe.wait_ge(down_loaded[s], l * (16 * NE // 4) + it * 16 + 16)
                        pe.wait_ge(hhT_ready, w + 1)
                        wd = ering[:, s, 2, :].rearrange("p (c n) -> p c n", c=2)
                        for half in range(2):
                            for c in range(2):
                                last = mm(ps[0:WIN, 6 + half, :], hhT[:, b, c * WIN:(c + 1) * WIN], wd[:, c, half * 512:(half + 1) * 512], c == 0, c == 1)
                        last.then_inc(down_ready if i % per == per - 1 else wide_down, 1)

                    def turn_out(it, w, i, first):
                        b = i % 2
                        for half in range(2):
                            pe.wait_ge(yrow_ready[half], w + 1)
                        if not (first and i < 2):
                            pe.wait_ge(ys_ready, w - 1)
                        pe.sem_inc(wait_carried, 1)
                        for c in range(DC):
                            last = tr(ps[:, 2 + b, c * WIN:(c + 1) * WIN], yrow[:, c * P:(c + 1) * P], WIN)
                        last.then_inc(yT_psum, 1)

                    n = 4 * per

                    def step(it, w, i, first, ending):
                        if not ending:
                            gate_up(it, w, i, first)
                        if i <= n and not (first and i < 1):
                            turn_hidden(it, w - 1, (i - 1) % n)
                        if not (first and i < 2):
                            turn_out(it, w - 2, (i - 2) % n, first)
                        if i <= n and not (first and i < 1):
                            down(it - 1 if i == 0 else it, w - 1, (i - 1) % n)

                    windows_of(pe, per, step)

                wait_evacuated(pe, "rank")
                wait_evacuated(pe, "lg")
                pe.wait_ge(starts_ready, 2)
                most_pe = pe.value_load(most[0:1, 0:1], min_val=0, max_val=S)
                with pe.If(most_pe > windows):
                    experts(WIDE)
                with pe.Else():
                    experts(1)

                pe.wait_ge(gw_ready, 2)
                for t in range(TC):
                    for s in range(4):
                        b = 4 + t
                        last = tr(ps[:, b, s * P:(s + 1) * P], gw[:, t, s * P:(s + 1) * P])
                    last.then_inc(gwT_psum, 1)
                for s in range(4):
                    for half in range(2):
                        i = 2 * s + half
                        if i == 0:
                            wait_last_ys(pe, most_pe, windows, ys_ready)
                        if i >= 2:
                            pe.wait_ge(ytok_read[i % 2], (i - 2) // 2 + 1)
                        for j in range(4):
                            last = tr(ps[:, 6 + i % 2, j * P:(j + 1) * P], ys[:, half * 4 + j, s * P:(s + 1) * P])
                        last.then_inc(ytok_psum, 1)
                pe.wait_ge(gwT_ready, 2)
                pe.wait_ge(ytok_read[0], 4)
                pe.wait_ge(ytok_read[1], 4)
                for m in range(4):
                    free_bank(f"cb{m}")
                    for j in range(2):
                        for s in range(4):
                            last = mm(two(bank(f"cb{m}"))[:, j, :], y_tok[:, s, (2 * m + j) * P:(2 * m + j + 1) * P],
                                      gwT[:, s, :], s == 0, s == 3)
                    last.then_inc(unit_ready, 1)

                for i in range(2):
                    for t in range(TC):
                        last = tr(ps[:, 7, i * S + t * P:i * S + (t + 1) * P], prow[:, t, i * P:(i + 1) * P])
                last.then_inc(pT_tr, 1)
                pe.wait_ge(p_ready, 1)

                def embed(m):
                    wait_chunk("pp")
                    free_bank(f"pp{m}")
                    w = ring[:, CI["pp"] % RING, :].rearrange("p (k n) -> p k n", k=2)
                    for j in range(2):
                        for c in range(2):
                            last = mm(two(bank(f"pp{m}"))[:, j, :], w[:, c, (2 * m + j) * P:(2 * m + j + 1) * P],
                                      pT[:, c, :], c == 0, c == 1)
                    last.then_inc(unit_ready, 1)

                embed(0)
                embed(1)
                stat("ple", [sq_p[:, c, :] for c in range(DC)], sq_events("ple", DC))
                project("pg0", hT, DC, h_events("ple"))
                bcast("ple")
                for m in range(1, 4):
                    if m < 3:
                        embed(m + 1)
                    project(f"pg{m}", hT, DC)
                pe.wait_ge(bcast_used, len(NORMS))
                mm(ps[:, 3, 0:1], ones[:, :], ones[:, 0:1], True, True).then_inc(engines_done, 1)
            begin(pe, DEPTH + 1)
            stat("mix", [sq_x[:, c, :] for c in range(DC)], sq_events("mix", DC))
            for i in range(4):
                for j in range(4):
                    t, c = i // 2, (i % 2) * 4 + j
                    last = tr(ps[:, 4 + i, j * P:(j + 1) * P], xT[:, c, t * P:(t + 1) * P])
                last.then_inc(tok_psum, 1)

        @block.scalar
        def _(act):
            def copy(o, i):
                return nc.scalar.activation(o, i, ACT.Copy)

            def squares(name, dst, src, units):
                for i, unit in enumerate(units):
                    if unit:
                        wait_evacuated(act, unit)
                    nc.scalar.activation(dst[:, 2 * i:2 * i + 2, :], src[:, 2 * i:2 * i + 2, :], ACT.Square).then_inc(sq_ready, 1)

            for i in range(2):
                act.wait_ge(x_tr, 2 * i + 1)
                copy(xT[:, 4 * i:4 * i + 2, :], ps[:, 2 * i, :]).then_inc(x_in, 1)
            act.wait_ge(rope_step, ROPE_STEPS)
            act.wait_ge(init_loaded, 48)
            nc.scalar.activation(sinT[NOPE:QK, :], ang[NOPE:QK, 0, :], ACT.Sin).then_inc(rope_sin, 1)
            nc.scalar.activation(cosT[NOPE:QK, :], ang[NOPE:QK, 2, :], ACT.Sin).then_inc(rope_sin, 1)

            with act.Fori(0, DEPTH) as l:
                begin(act, l + 1)
                act.wait_ge(x_in, 4)
                squares("mix", sq_x, xT, [None] * 4)
                act.wait_ge(vec_tr, 1)
                copy(convT[:, :], ps[:, 6, 0:CROWS]).then_inc(vec_ready, 1)
                act.wait_ge(vec_tr, 2)
                copy(vecT[:, :], ps[:, 7, 0:VROWS]).then_inc(vec_ready, 1)
                squares("kv", sq_kv, two(tmp[:, 0, :]), ["kv"])
                squares("q", sq_q, qn, [f"q{i}" for i in range(3)])
                for i in range(4):
                    wait_unit(act, l, f"kn{i}")
                    evacuates(copy(kT[0:NOPE, 2 * i:2 * i + 2, :], two(bank(f"kn{i}"))[0:NOPE, :, :]), f"kn{i}")
                for t in range(TC):
                    wait_unit(act, l, f"v{t}")
                    evacuates(copy(v[:, t, :], bank(f"v{t}")), f"v{t}")
                for i in range(4):
                    wait_unit(act, l, f"uq{i}")
                    if i == 0:
                        act.wait_ge(stat_ready, after(NORMS, "q"))
                    evacuates(copy(qT[0:QK, 2 * i:2 * i + 2, :], two(bank(f"uq{i}"))[0:QK, :, :]), f"uq{i}")
                for i in range(2):
                    wait_evacuated(act, f"gg{i}")
                    nc.scalar.activation(glu_t[i][:, 0, :], glu_t[i][:, 0, :], ACT.Sigmoid).then_inc(glu_sig, 1)

                def exponentials(h):
                    act.wait_ge(max_ready, h + 1)
                    if h == 0:
                        act.wait_ge(u_ready, 2)
                    if h >= 2:
                        act.wait_ge(pT_psum, h - 1)
                    for i, (a, b) in enumerate(((0, P), (P, 3 * P))):
                        nc.scalar.activation(probs[:, h % 2, a:b], ps[:, 4 + h % 2, a:b], ACT.Exp,
                                             bias=mx[:, h % 2, i, 1:2], scale=SCALE,
                                             accum_out=mx[:, h % 2, i, 2:3]).then_inc(exp_ready, 1)

                def copy_transposed(h):
                    act.wait_ge(pT_psum, h + 1)
                    if h >= 2:
                        act.wait_ge(pv_ready, h - 1)
                    copy(probsT[:, h % 2, :], ps[:, 6, 0:3 * P]).then_inc(pT_ready, 1)

                def copy_attention(h):
                    act.wait_ge(pv_ready, h + 1)
                    r = (h % 2) * VH
                    if h == 0:
                        act.wait_ge(q_ready, 4)
                    copy(attnT[r:r + VH, h // 2, :], ps[r:r + VH, 7, 0:S]).then_inc(attn_ready, 1)

                exponentials(0)
                exponentials(1)
                for h in range(HEADS):
                    copy_transposed(h)
                    if h + 2 < HEADS:
                        exponentials(h + 2)
                    if h >= 1:
                        copy_attention(h - 1)
                copy_attention(HEADS - 1)

                def gate_sigmoids(m):
                    for i in range(3):
                        wait_evacuated(act, f"g{'abc'[i]}{m}")
                        nc.scalar.activation(gate_t[m % 2][:, i, :], gate_t[m % 2][:, i, :], ACT.Sigmoid).then_inc(gate_sig, 1)

                act.wait_ge(xc_ready, 1)
                nc.scalar.activation(sq_ln, conv, ACT.Square).then_inc(sq_ready, 1)
                gate_sigmoids(0)
                for c in range(SCC):
                    act.wait_ge(ln_step, c + 1)
                    nc.scalar.activation(sq_ln[:, c, :], conv[:, c, :], ACT.Sigmoid, bias=vcol("lnb", c)).then_inc(ln_sig, 1)
                for m in range(1, 4):
                    gate_sigmoids(m)
                act.wait_ge(merged_ready, 4)
                squares("ffn", sq_x, xT, [f"wo{m}" for m in range(4)])
                for i in (0, 2):
                    act.wait_ge(tok_psum, i + 1)
                    copy(h_tok[:, i // 2, (i % 2) * 512:(i % 2 + 1) * 512], ps[:, 4 + i, :]).then_inc(tok_read[0], 1)
                act.wait_ge(top_diff, 1)
                nc.scalar.activation(expd, expd, ACT.Exp).then_inc(top_exp, 1)
                for c in range(0, DC, 2):
                    act.wait_ge(gather_psum, c + 1)
                    copy(xs[:, c, 0:PAIRS], ps[:, 4 + c % 4, :]).then_inc(xs_read[0], 1)

                def experts(per):
                    def sigmoid(w, i):
                        wait_gate_up(act, l, w, i, per)
                        nc.scalar.activation(sg[:, i % 2, :], ps[0:WIN, i % 2, 0:FH], ACT.Sigmoid).then_inc(sg_ready, 1)

                    def place(w, i, first):
                        e, j = expert_of(w, i, per), i % per
                        at = act.value_load(starts[0:1, bass.ds(e + j * NE, 1)], min_val=0, max_val=PAIRS)
                        act.wait_ge(yT_psum, w + 1)
                        if not (first and i == 0):
                            act.wait_ge(ys_ready, w)
                        copy(ys[:, :, bass.ds(at, WIN)], ps[:, 2 + i % 2, :].rearrange("p (m n) -> p m n", m=DC)).then_inc(ys_ready, 1)

                    def take_rows(w, i):
                        wait_down(act, l, w, i, per)
                        copy(yrow[:, 0:512], ps[0:WIN, 6, :]).then_inc(yrow_ready[0], 1)

                    n = 4 * per

                    def step(it, w, i, first, ending):
                        if not ending:
                            sigmoid(w, i)
                        if not (first and i < 2):
                            place(w - 2, (i - 2) % n, first)
                        if i <= n and not (first and i < 1):
                            take_rows(w - 1, (i - 1) % n)

                    windows_of(act, per, step)

                act.wait_ge(starts_ready, 2)
                act.wait_ge(gather_psum, DC)
                most_act = act.value_load(most[0:1, 0:1], min_val=0, max_val=S)
                with act.If(most_act > windows):
                    experts(WIDE)
                with act.Else():
                    experts(1)
                for i in (0, 2, 4, 6):
                    act.wait_ge(ytok_psum, i + 1)
                    copy(y_tok[:, i // 2, 0:512], ps[:, 6, :]).then_inc(ytok_read[0], 1)
                act.wait_ge(pT_tr, 1)
                copy(pT[:, :, :], two(ps[:, 7, :])).then_inc(p_ready, 1)
                squares("ple", sq_p, xT, [f"cb{m}" for m in range(4)])

                def copy_embedding(m):
                    wait_unit(act, l, f"pp{m}")
                    if m >= 2:
                        act.wait_ge(pmul_ready, m - 1)
                    evacuates(copy(ppt[m % 2], bank(f"pp{m}")), f"pp{m}")

                def ple_sigmoid(m):
                    wait_evacuated(act, f"pg{m}")
                    last = nc.scalar.activation(ple_t[m % 2], ple_t[m % 2], ACT.Sigmoid)
                    last.then_inc(psig_ready, 1)

                copy_embedding(0)
                copy_embedding(1)
                for m in range(4):
                    ple_sigmoid(m)
                    if m < 2:
                        copy_embedding(m + 2)
                act.wait_ge(psig_ready, 4)
                copy(last_act[:, :], ones[:, 0:1]).then_inc(engines_done, 1)
            begin(act, DEPTH + 1)
            squares("mix", sq_x, xT, [None] * 4)


        @block.gpsimd
        def _(pool):
            nc.gpsimd.memset(ones[:, :], 1.0).then_inc(const_set, 1)
            nc.gpsimd.memset(mhalf[:, :], -0.5).then_inc(const_set, 1)
            pool.wait_ge(const_set, 2)
            pool.sem_inc(layer_over, 1)

            def power(name):
                i = NORMS.index(name)
                pool.wait_ge(ms_ready, after(POWS, name))
                nc.gpsimd.tensor_tensor(col[:, i, 1, :], col[:, i, 0, :], mhalf[:, :], ALU.pow).then_inc(pow_ready, 1)

            with pool.Fori(0, DEPTH) as l:
                nc.gpsimd.memset(upad[:, :, 0:KC - 1], 0.0).then_inc(pad_zero, 1)
                power("mix")
                power("kv")
                wait_evacuated(pool, "rotk")
                pool.wait_ge(rope_sin, 2)
                nc.gpsimd.tensor_tensor(kr[NOPE:QK, 0, :], kr[NOPE:QK, 0, :], cosT[NOPE:QK, :], ALU.mult).then_inc(q_cos, 1)
                pool.wait_ge(q_cos, 1)
                nc.gpsimd.tensor_tensor(kr[NOPE:QK, 0, :], kr[NOPE:QK, 0, :], kr[NOPE:QK, 1, :], ALU.add).then_inc(q_cos, 1)
                pool.wait_ge(q_cos, 2)
                nc.gpsimd.tensor_copy(kT[NOPE:QK, :, :], kr[NOPE:QK, 0, :].unsqueeze(1).to_broadcast([ROPE, HEADS, S])).then_inc(k_ready, 1)
                pool.wait_ge(k_ready, 1)
                power("q")
                for i in range(4):
                    q2 = qT[NOPE:QK, 2 * i:2 * i + 2, :]
                    wait_evacuated(pool, f"rot{i}")
                    nc.gpsimd.tensor_tensor(q2, q2, cosT[NOPE:QK, :].unsqueeze(1).to_broadcast([ROPE, 2, S]), ALU.mult).then_inc(q_cos, 1)
                    pool.wait_ge(q_cos, i + 3)
                    nc.gpsimd.tensor_tensor(q2, q2, rtmp[NOPE:QK, i % 2, :, :], ALU.add).then_inc(q_ready, 1)
                pool.wait_ge(q_ready, 4)
                for i in range(2):
                    pool.wait_ge(glu_sig, i + 1)
                    wait_evacuated(pool, f"gv{i}")
                    if i == 0:
                        pool.wait_ge(pad_zero, 1)
                    nc.gpsimd.tensor_tensor(upad[:, 2 * i:2 * i + 2, KC - 1:], two(glu_t[i][:, 1, :]), two(glu_t[i][:, 0, :]), ALU.mult).then_inc(u_ready, 1)
                wait_evacuated(pool, "uq3")
                nc.gpsimd.memset(scu[:, :, 0:KA - 1], 0.0).then_inc(pad_zero, 1)
                for h in range(HEADS):
                    pool.wait_ge(recip_ready, h + 1)
                    for i, (a, b) in enumerate(((0, P), (P, 3 * P))):
                        pool.wait_ge(exp_ready, 2 * (h + 1)) if i == 0 else None
                        nc.gpsimd.tensor_scalar(probs[:, h % 2, a:b], probs[:, h % 2, a:b], mx[:, h % 2, i, 0:1], None,
                                                ALU.mult).then_inc(probs_ready, 1)
                    if h in (1, 4):
                        i = h // 3
                        wait_evacuated(pool, f"u{i}")
                        half = scu[:, 2 * i:2 * i + 2, KA - 1:]
                        nc.gpsimd.tensor_tensor(half, half, two(tmp[:, 0, :]), ALU.mult).then_inc(scu_ready, 1)
                power("lnv")
                for m in range(4):
                    g = gate_t[m % 2]
                    wait_evacuated(pool, f"ya{m}")
                    wait_evacuated(pool, f"yb{m}")
                    nc.gpsimd.tensor_tensor(merged[:, 2 * m:2 * m + 2, :], two(g[:, 0, :]), two(g[:, 1, :]), ALU.add).then_inc(merge_step, 1)
                    pool.wait_ge(merge_step, m + 1)
                    wait_evacuated(pool, f"yc{m}")
                    nc.gpsimd.tensor_tensor(merged[:, 2 * m:2 * m + 2, :], merged[:, 2 * m:2 * m + 2, :], two(g[:, 2, :]), ALU.add).then_inc(merged_ready, 1)
                power("ffn")
                pool.wait_ge(stat_ready, after(NORMS, "ffn"))
                nc.gpsimd.memset(xs[:, :, PAIRS:SLOTS], 0.0).then_inc(xs_pad, 1)

                def experts(per):
                    with pool.Fori(0, NE // 4) as it:
                        for i, (s, j) in enumerate([(s, j) for s in range(4) for j in range(per)]):
                            e = it * 4 + s
                            at = pool.value_load(starts[0:1, bass.ds(e + j * NE, 1)], min_val=0, max_val=PAIRS)
                            if per == 1:
                                pool.wait_ge(gu_ready, NE * (l + 1) + e - 1)
                            elif j < 2:
                                pool.wait_ge(gu_ready, NE * (l + 1) + e)
                            else:
                                pool.wait_ge(wide_gu, e * (per - 1) + j - 1)
                            nc.gpsimd.tensor_copy(xw[:, i % 2, :, :], xs[:, :, bass.ds(at, WIN)]).then_inc(xw_ready, 1)

                pool.wait_ge(xs_read[0], 4)
                pool.wait_ge(xs_read[1], 4)
                pool.wait_ge(xs_pad, 1)
                pool.wait_ge(gw_ready, 2)
                pool.wait_ge(starts_ready, 2)
                most_pool = pool.value_load(most[0:1, 0:1], min_val=0, max_val=S)
                with pool.If(most_pool > windows):
                    experts(WIDE)
                with pool.Else():
                    experts(1)
                power("ple")
                for m in range(4):
                    pool.wait_ge(pmul_ready, m + 1)
                    x2 = xT[:, 2 * m:2 * m + 2, :]
                    if m == 0:
                        pool.wait_ge(h_ready, 3 * DC)
                        pool.wait_ge(sq_ready, len(SQUARES))
                    nc.gpsimd.tensor_tensor(x2, x2, two(ple_t[m % 2]), ALU.add).then_inc(merge_step, 1)
                pool.wait_ge(merge_step, 8)
                pool.wait_ge(engines_done, 3)
                pool.sem_clear(range(zeroed[0].num, zeroed[-1].num + 1))
                pool.sem_inc(layer_over, 1)
            power("mix")

        @block.vector
        def _(dve):
            TT, TS, STT = nc.vector.tensor_tensor, nc.vector.tensor_scalar, nc.vector.scalar_tensor_tensor
            for i in range(2):
                dve.wait_ge(x_tr, 2 * i + 2)
                nc.vector.tensor_copy(xT[:, 4 * i + 2:4 * i + 4, :], ps[:, 2 * i + 1, :]).then_inc(x_in, 1)

            rows = slice(NOPE, QK)
            n_rope = [0]

            def rstep(ins):
                n_rope[0] += 1
                ins.then_inc(rope_step, 1)
                dve.wait_ge(rope_step, n_rope[0])

            dve.wait_ge(init_loaded, 48)
            a0, a1, a2 = (ang[rows, i, :] for i in (1, 3, 2))
            A = ang[rows, 0, :]
            rstep(nc.vector.tensor_copy(a0, A.bitcast(I32)))
            rstep(TS(a0, a0, freq, None, ALU.mult))
            rstep(TS(a1, a0, INV_2PI, ROUND, ALU.mult, ALU.add))
            rstep(TS(a1, a1, ROUND, None, ALU.subtract))
            rstep(STT(a0, a1, -TWO_PI[0], a0, ALU.mult, ALU.add))
            rstep(STT(a0, a1, -TWO_PI[1], a0, ALU.mult, ALU.add))
            rstep(STT(a0, a1, -TWO_PI[2], a0, ALU.mult, ALU.add))
            rstep(TS(A, a0, PI_IN, -PI_IN, ALU.min, ALU.max))
            rstep(STT(a2, A, -1.0, A, ALU.mult, ALU.min))
            rstep(TS(a2, a2, HALF_PI, None, ALU.add))

            def mean(name, n):
                i = NORMS.index(name)
                dve.wait_ge(stat_ready, after(NORMS, name))
                if name == "lnm":
                    TS(col[:, i, 1, :], ps[:, 3, 0:TC], 1.0 / n, None, ALU.mult).then_inc(mean_ready, 1)
                else:
                    TS(col[:, i, 0, :], ps[:, 3, 0:TC], 1.0 / n, EPS, ALU.mult, ALU.add).then_inc(ms_ready, 1)

            def diagonal(name):
                i = NORMS.index(name)
                if name == "lnm":
                    dve.wait_ge(mean_ready, 1)
                else:
                    dve.wait_ge(pow_ready, after(POWS, name))
                TS(diag[:, 0, :], ident, col[:, i, 1, 0:1], None, ALU.mult)
                TS(diag[:, 1, :], ident, col[:, i, 1, 1:2], None, ALU.mult).then_inc(diag_ready, 1)

            def take_row(name, dst):
                dve.wait_ge(bcast_ready, after(NORMS, name))
                nc.vector.tensor_copy(dst[:, :], ps[:, 3, S:2 * S]).then_inc(bcast_used, 1)
                dve.wait_ge(bcast_used, after(NORMS, name))

            with dve.Fori(0, DEPTH) as l:
                begin(dve, l + 1)
                dve.wait_ge(x_in, 4)
                dve.wait_ge(vec_ready, 2)
                for c in range(DC):
                    TS(hT[:, c, :], xT[:, c, :], vcol("mix", c), None, ALU.mult).then_inc(h_ready, 1)

                def scale_out(name, dst, n=2):
                    wait_unit(dve, l, name)
                    evacuates(TT(dst, two(bank(name)), bc2(), ALU.mult), name)

                mean("mix", D)
                diagonal("mix")
                take_row("mix", bc)
                scale_out("kv", two(tmp[:, 0, :]))
                wait_unit(dve, l, "kr")
                evacuates(TT(kr[0:QK, 0, :], bank("kr")[0:QK, 0:S], bc[0:QK, :], ALU.mult), "kr")
                scale_out("q0", qn[:, 0:2, :])
                scale_out("q1", qn[:, 2:4, :])
                mean("kv", KVL)
                scale_out("q2", qn[:, 4:6, :])
                diagonal("kv")
                take_row("kv", bcs)
                for c in range(2):
                    STT(kvn[:, c, :], two(tmp[:, 0, :])[:, c, :], vcol("kv", c), bcs[:, :], ALU.mult, ALU.mult).then_inc(kvn_ready, 1)
                wait_unit(dve, l, "rotk")
                dve.wait_ge(rope_sin, 2)
                evacuates(TT(kr[NOPE:QK, 1, :], bank("rotk")[NOPE:QK, 0:S], sinT[NOPE:QK, :], ALU.mult), "rotk")
                mean("q", QL)
                diagonal("q")
                take_row("q", bcs)
                for c in range(6):
                    STT(qn[:, c, :], qn[:, c, :], vcol("q", c), bcs[:, :], ALU.mult, ALU.mult).then_inc(qn_ready, 1)

                def rotated(i):
                    wait_unit(dve, l, f"rot{i}")
                    if i >= 2:
                        dve.wait_ge(q_ready, i - 1)
                    evacuates(TT(rtmp[NOPE:QK, i % 2, :, :], two(bank(f"rot{i}"))[NOPE:QK, :, :],
                                 sinT[NOPE:QK, :].unsqueeze(1).to_broadcast([ROPE, 2, S]), ALU.mult), f"rot{i}")

                rotated(0)
                rotated(1)
                rotated(2)
                scale_out("gg0", two(glu_t[0][:, 0, :]))
                rotated(3)
                scale_out("gv0", two(glu_t[0][:, 1, :]))
                scale_out("gg1", two(glu_t[1][:, 0, :]))
                scale_out("gv1", two(glu_t[1][:, 1, :]))

                def maximum(h):
                    dve.wait_ge(score_ready, h + 1)
                    if h >= 2:
                        dve.wait_ge(probs_ready, 2 * (h - 1))
                    b = 4 + h % 2
                    edge = two(ps[:, b, :])[:, :, 0:P]
                    TT(edge, edge, causal.unsqueeze(1).to_broadcast([P, 2, P]), ALU.add).then_inc(mask_step, 1)
                    dve.wait_ge(mask_step, 2 * h + 1)
                    nc.vector.reduce_max(mx[:, h % 2, 0, 0:1], ps[:, b, 0:P], AX.X)
                    nc.vector.reduce_max(mx[:, h % 2, 1, 0:1], ps[:, b, P:3 * P], AX.X).then_inc(mask_step, 1)
                    dve.wait_ge(mask_step, 2 * h + 2)
                    TS(mx[:, h % 2, :, 1], mx[:, h % 2, :, 0], -SCALE, None, ALU.mult).then_inc(max_ready, 1)

                taps = [(k, c) for k in range(KC) for c in range(SCC)]

                def conv_taps(first, count):
                    for n in range(first, min(first + count, len(taps))):
                        k, c = taps[n]
                        w = convT[:, k * SCC + c:k * SCC + c + 1]
                        if k == 0:
                            TS(conv[:, c, :], upad[:, c, 0:S], w, None, ALU.mult).then_inc(conv_step, 1)
                        else:
                            dve.wait_ge(conv_step, n - SCC + 1)
                            STT(conv[:, c, :], upad[:, c, k:k + S], w, conv[:, c, :], ALU.mult, ALU.add).then_inc(conv_step, 1)

                def short_conv(i):
                    dve.wait_ge(scu_ready, i + 1)
                    t = two(tmp[:, 1, :])
                    for j in range(2):
                        c = 2 * i + j
                        TS(t[:, j, :], scu[:, c, 0:S], vcol("ca", c), None, ALU.mult).then_inc(short_step, 1)
                    for k in range(1, KA):
                        for j in range(2):
                            c = 2 * i + j
                            dve.wait_ge(short_step, 6 * i + 2 * (k - 1) + j + 1)
                            STT(t[:, j, :], scu[:, c, k:k + S], vcol("ca", k * SCC + c), t[:, j, :], ALU.mult, ALU.add).then_inc(short_step, 1)
                    dve.wait_ge(short_step, 6 * (i + 1))
                    y2 = ya[:, 2 * i:2 * i + 2, :]
                    TT(y2, y2, t, ALU.mult).then_inc(ya_ready, 1)

                maximum(0)
                maximum(1)
                dve.wait_ge(u_ready, 2)
                dve.wait_ge(k_ready, 1)
                PER_HEAD = -(-len(taps) // HEADS)
                for h in range(HEADS):
                    dve.wait_ge(exp_ready, 2 * (h + 1))
                    nc.vector.reciprocal(mx[:, h % 2, :, 0], mx[:, h % 2, :, 2]).then_inc(recip_ready, 1)
                    conv_taps(PER_HEAD * h, PER_HEAD)
                    if h + 2 < HEADS:
                        maximum(h + 2)
                    if h < len(FILL):
                        kind, i = FILL[h][0], h // 3
                        if h == 0:
                            dve.wait_ge(pad_zero, 2)
                        if kind == "c":
                            scale_out(FILL[h], scu[:, 2 * i:2 * i + 2, KA - 1:])
                        if kind == "u":
                            if i:
                                dve.wait_ge(scu_ready, 1)
                            scale_out(FILL[h], two(tmp[:, 0, :]))
                        if kind == "b":
                            scale_out(FILL[h], ya[:, 2 * i:2 * i + 2, :])
                            wait_evacuated(dve, FILL[h])
                            short_conv(i)

                def gate_out(x, m):
                    if m == 0:
                        dve.wait_ge(pv_ready, HEADS)
                    if m >= 2:
                        dve.wait_ge(merged_ready, m - 1)
                    scale_out(f"g{x}{m}", two(gate_t[m % 2][:, "abc".index(x), :]))

                def gate_mul(x, m):
                    wait_unit(dve, l, f"y{x}{m}")
                    i = "abc".index(x)
                    dve.wait_ge(gate_sig, 3 * m + i + 1)
                    g = gate_t[m % 2][:, i, :]
                    evacuates(TT(g, g, bank(f"y{x}{m}"), ALU.mult), f"y{x}{m}")

                for m in range(4):
                    gate_out("a", m)
                    if m == 0:
                        mean("lnm", SC)
                        diagonal("lnm")
                    gate_out("b", m)
                    if m == 0:
                        take_row("lnm", bcs)
                        TT(conv, conv, bcs[:, :].unsqueeze(1).to_broadcast([P, SCC, S]), ALU.subtract).then_inc(xc_ready, 1)
                    gate_out("c", m)
                    gate_mul("a", m)
                    if m == 0:
                        mean("lnv", SC)
                    gate_mul("b", m)
                    if m == 0:
                        diagonal("lnv")
                        take_row("lnv", bcs)
                        for c in range(SCC):
                            STT(conv[:, c, :], conv[:, c, :], vcol("lng", c), bcs[:, :], ALU.mult, ALU.mult).then_inc(ln_step, 1)
                        for c in range(SCC):
                            dve.wait_ge(ln_sig, c + 1)
                            STT(conv[:, c, :], conv[:, c, :], vcol("lnb", c), sq_ln[:, c, :], ALU.add, ALU.mult).then_inc(yc_ready, 1)
                    gate_mul("c", m)

                def add_to_x(unit, m):
                    wait_unit(dve, l, unit)
                    x2 = xT[:, 2 * m:2 * m + 2, :]
                    evacuates(TT(x2, two(bank(unit)), x2, ALU.add), unit)

                for m in range(4):
                    add_to_x(f"wo{m}", m)
                mean("ffn", D)
                diagonal("ffn")
                take_row("ffn", bcs)
                for c in range(DC):
                    STT(hT[:, c, :], xT[:, c, :], vcol("ffn", c), bcs[:, :], ALU.mult, ALU.mult).then_inc(h_ready, 1)

                n_step = [0]

                def step(ins):
                    n_step[0] += 1
                    ins.then_inc(dve_step, 1)
                    dve.wait_ge(dve_step, n_step[0])

                def b3(t, n):
                    return t.to_broadcast([P, TC, n])

                def io(n):
                    return iota[:, 0:n].unsqueeze(1).to_broadcast([P, TC, n])

                def first_of_max(x, n, mxt, eq, val, mn, hot):
                    step(nc.vector.reduce_max(mxt, x, AX.X))
                    step(TT(eq, x, b3(mxt, n), ALU.is_equal))
                    step(STT(val, eq, -float(PAIRS), io(n), ALU.mult, ALU.add))
                    step(nc.vector.tensor_reduce(mn, val, AX.X, ALU.min))
                    return TT(hot, val, b3(mn, n), ALU.is_equal)

                wait_unit(dve, l, "lg")
                lgp = bank("lg")[:, 0:TC * (NG + NE)].rearrange("p (t n) -> p t n", t=TC)
                evacuates(TT(logit, lgp, b_rt[:, :, :], ALU.add), "lg")
                wait_evacuated(dve, "lg")
                for i in (1, 3):
                    dve.wait_ge(tok_psum, i + 1)
                    nc.vector.tensor_copy(h_tok[:, i // 2, (i % 2) * 512:(i % 2 + 1) * 512], ps[:, 4 + i, :]).then_inc(tok_read[1], 1)
                step(first_of_max(logit[:, :, 0:NG], NG, gmax, geq, gval, gmin, gone))
                step(TS(gpen, gone, BIG, -BIG, ALU.mult, ALU.add))
                for t in range(TC):
                    last = TT(masked[:, t, :].rearrange("p (g e) -> p g e", g=NG), logit[:, t, NG:].rearrange("p (g e) -> p g e", g=NG),
                              gpen[:, t, :].unsqueeze(2).to_broadcast([P, NG, EPG]), ALU.add)
                step(last)
                step(first_of_max(masked, NE, top[0], teq[0], tval[0], tmin[0], one[0]))
                step(STT(masked2, one[0], -3.0 * BIG, masked, ALU.mult, ALU.add))
                step(first_of_max(masked2, NE, top[1], teq[1], tval[1], tmin[1], one[1]))
                TT(chosen, one[0], one[1], ALU.add).then_inc(onehot_ready, 1)
                TT(expd[:, :, 0:NG], logit[:, :, 0:NG], b3(gmax, NG), ALU.subtract)
                TT(expd[:, :, NG:NG + 1], top[1], top[0], ALU.subtract).then_inc(top_diff, 1)
                for f in prefix:
                    nc.vector.memset(f[:, 0:16], 0.0)
                wait_unit(dve, l, "rank")
                evacuates(nc.vector.tensor_copy(ranks, bank("rank")[:, 0:3 * NE]), "rank")
                wait_evacuated(dve, "rank")
                count = ranks[:, 2 * NE:3 * NE]
                step(nc.vector.tensor_copy(prefix[0][:, 16:48], count))
                for i, sh in enumerate((1, 2, 4, 8, 16)):
                    a, b = prefix[i % 2], prefix[(i + 1) % 2]
                    step(TT(b[:, 16:48], a[:, 16:48], a[:, 16 - sh:48 - sh], ALU.add))
                upto = prefix[1][:, 16:48]
                step(TT(off, upto, count, ALU.subtract))
                step(TT(base, ranks[:, 0:2 * NE].rearrange("p (t n) -> p t n", t=TC), off.unsqueeze(1).to_broadcast([P, TC, NE]), ALU.add))
                TT(prod[0], base, one[0], ALU.mult)
                step(TT(prod[1], base, one[1], ALU.mult))
                nc.vector.reduce_sum(pos[0], prod[0], AX.X)
                step(nc.vector.reduce_sum(pos[1], prod[1], AX.X))
                for t in range(TC):
                    step(TS(sel_t[:, t, :], iota, pos[0][:, t, :], None, ALU.is_equal))
                    STT(sel[:, t, :], iota, pos[1][:, t, :], sel_t[:, t, :], ALU.is_equal, ALU.add).then_inc(sel_ready, 1)
                for j in range(WIDE):
                    last = STT(starts[0:1, j * NE:(j + 1) * NE], off[0:1, :], float(j * WIN), upto[0:1, :], ALU.add, ALU.min)
                last.then_inc(starts_ready, 1)
                nc.vector.reduce_max(most[0:1, 0:1], count[0:1, :], AX.X).then_inc(starts_ready, 1)
                dve.wait_ge(top_exp, 1)
                nc.vector.reduce_sum(gsum, expd[:, :, 0:NG], AX.X)
                step(TS(dplus, expd[:, :, NG:NG + 1], 1.0, None, ALU.add))
                step(TT(gsum, gsum, dplus, ALU.mult))
                step(nc.vector.reciprocal(weight[0], gsum))
                step(TT(weight[1], weight[0], expd[:, :, NG:NG + 1], ALU.mult))
                dve.wait_ge(sel_ready, 2)
                for t in range(TC):
                    TS(gw[:, t, :], iota, pos[0][:, t, :], weight[0][:, t, :], ALU.is_equal, ALU.mult)
                    step(TS(sel_t[:, t, :], iota, pos[1][:, t, :], weight[1][:, t, :], ALU.is_equal, ALU.mult))
                    TT(gw[:, t, :], gw[:, t, :], sel_t[:, t, :], ALU.add).then_inc(gw_ready, 1)
                for c in range(1, DC, 2):
                    dve.wait_ge(gather_psum, c + 1)
                    nc.vector.tensor_copy(xs[:, c, 0:PAIRS], ps[:, 4 + c % 4, :]).then_inc(xs_read[1], 1)

                def experts(per):
                    def hidden(w, i):
                        b = i % 2
                        dve.wait_ge(sg_ready, w + 1)
                        TT(hh[:, b, :], sg[:, b, :], ps[0:WIN, b, 0:FH], ALU.mult).then_inc(hh_part, 1)
                        dve.wait_ge(hh_part, w + 1)
                        TT(hh[:, b, :], hh[:, b, :], ps[0:WIN, b, FH:2 * FH], ALU.mult).then_inc(hh_ready, 1)

                    def take_hidden(w, i):
                        dve.wait_ge(hh_tr, w + 1)
                        nc.vector.tensor_copy(hhT[:, i % 2, :], ps[:, 4 + i % 2, 0:2 * WIN]).then_inc(hhT_ready, 1)

                    def take_rows(w, i):
                        wait_down(dve, l, w, i, per)
                        nc.vector.tensor_copy(yrow[:, 512:1024], ps[0:WIN, 7, :]).then_inc(yrow_ready[1], 1)

                    n = 4 * per

                    def step(it, w, i, first, ending):
                        before = i <= n and not (first and i < 1)
                        if before:
                            take_hidden(w - 1, (i - 1) % n)
                        if not ending:
                            hidden(w, i)
                        if before:
                            take_rows(w - 1, (i - 1) % n)

                    windows_of(dve, per, step)

                dve.wait_ge(starts_ready, 2)
                most_dve = dve.value_load(most[0:1, 0:1], min_val=0, max_val=S)
                with dve.If(most_dve > windows):
                    experts(WIDE)
                with dve.Else():
                    experts(1)
                for t in range(TC):
                    dve.wait_ge(gwT_psum, t + 1)
                    nc.vector.tensor_copy(gwT[:, :, t * P:(t + 1) * P], ps[:, 4 + t, :].rearrange("p (s n) -> p s n", s=4)).then_inc(gwT_ready, 1)
                for i in (1, 3, 5, 7):
                    dve.wait_ge(ytok_psum, i + 1)
                    nc.vector.tensor_copy(y_tok[:, i // 2, 512:1024], ps[:, 7, :]).then_inc(ytok_read[1], 1)
                for m in range(4):
                    add_to_x(f"cb{m}", m)
                    wait_evacuated(dve, f"cb{m}")
                    for c in (2 * m, 2 * m + 1):
                        TS(hT[:, c, :], xT[:, c, :], vcol("ple", c), None, ALU.mult).then_inc(h_ready, 1)
                mean("ple", D)
                diagonal("ple")
                take_row("ple", bc)

                def ple_mul(m):
                    dve.wait_ge(psig_ready, m + 1)
                    wait_evacuated(dve, f"pp{m}")
                    TT(ple_t[m % 2], ple_t[m % 2], ppt[m % 2], ALU.mult).then_inc(pmul_ready, 1)

                for m in range(4):
                    if m >= 2:
                        dve.wait_ge(merge_step, 4 + m - 1)
                    scale_out(f"pg{m}", two(ple_t[m % 2]))
                    if m >= 1:
                        ple_mul(m - 1)
                ple_mul(3)
                nc.vector.tensor_copy(last_dve[:, :], ones[:, 0:1]).then_inc(engines_done, 1)
            begin(dve, DEPTH + 1)
            mean("mix", D)
            dve.wait_ge(pow_ready, 1)
            dve.wait_ge(init_loaded, 64)
            for t in range(TC):
                for half in range(2):
                    dve.wait_ge(tok_psum, 2 * t + half + 1)
                    last = STT(xout[:, t, half * 512:(half + 1) * 512], ps[:, 4 + 2 * t + half, :], col[:, 0, 1, t:t + 1],
                               gfull[:, half * 512:(half + 1) * 512], ALU.mult, ALU.mult)
                last.then_inc(pmul_ready, 1)


_INS = ["x", "p", "positions", "ln_mix_g", "w_in", "conv_a_w", "w_out_a", "q_norm_g", "w_uq", "kv_norm_g", "w_ukv",
        "w_out_b", "conv_c_w", "ln_c_g", "ln_c_b", "w_out_c", "w_o", "ln_ffn_g", "w_route_grp", "b_route_grp",
        "w_route_exp", "b_route_exp", "w_exp_gate", "w_exp_up", "w_exp_down", "ln_ple_g", "w_ple_gate", "w_ple",
        "final_norm_g"]


def constants():
    import numpy as np
    c = np.zeros((P, C_COLS), np.float32)
    c[:, C_ID:C_ID + P] = np.eye(P)
    c[:, C_UP:C_UP + P] = np.triu(np.ones((P, P)), 1)
    c[:, C_CAUSAL:C_CAUSAL + P] = np.where(np.tril(np.ones((P, P))) > 0, 0.0, -BIG)
    half = ROPE // 2
    for i in range(half):
        c[NOPE + half + i, C_ROT + NOPE + i] = -1.0
        c[NOPE + i, C_ROT + NOPE + half + i] = 1.0
        f = np.float32(10000.0) ** np.float32(-2.0 * i / ROPE)
        c[NOPE + i, C_FREQ] = c[NOPE + half + i, C_FREQ] = f
    c[:, C_IOTA:C_IOTA + PAIRS] = np.arange(PAIRS)
    return c


def kernel(**inputs):
    import numpy as _np
    import concourse.bacc as _bacc
    from concourse import mybir as _mybir
    from concourse.bass_utils import run_bass_kernel_spmd as _run

    nc = _bacc.Bacc("TRN2", target_bir_lowering=False, num_devices=1)
    arrays, args = {}, []
    for name in _INS:
        a = _np.ascontiguousarray(inputs[name])
        arrays[f"in_{name}_dram"] = a
        args.append(nc.dram_tensor(f"in_{name}_dram", a.shape, _mybir.dt.from_np(a.dtype), kind="ExternalInput").ap())
    c = constants()
    arrays["in_consts_dram"] = c
    args.append(nc.dram_tensor("in_consts_dram", c.shape, _mybir.dt.float32, kind="ExternalInput").ap())
    args.append(nc.dram_tensor("out_0_dram", (1, S, D), _mybir.dt.float32, kind="ExternalOutput").ap())
    program(nc, *args)
    r = _run(nc, [arrays], core_ids=[0])
    return r.results[0]["out_0_dram"]
```

```python
import concourse.bass as bass
from concourse import mybir
from contextlib import ExitStack

F32 = mybir.dt.float32
F32R = mybir.dt.float32r
I32 = mybir.dt.int32
ALU = mybir.AluOpType
ACT = mybir.ActivationFunctionType
AX = mybir.AxisListType

P = 128
DEPTH, S, D = 2, 256, 1024
DC, TC = D // P, S // P
SC, SCC = 512, 4
KA, KC = 3, 31
HEADS, NOPE, ROPE, VH = 8, 64, 32, 64
QK = NOPE + ROPE
QL, KVL = 768, 256
NG, EPG, NE, FH = 4, 8, 32, 256
PAIRS = 2 * S
WIN = 64
WIDE = S // WIN
SLOTS = PAIRS + WIN
ERING = 3
PIECES, KP = 4, 2
BODY = 2 * ERING
PEEL = NE % BODY
EPS = 1e-6
SCALE = float(QK) ** -0.5
BIG = 1e30
OFF_SC = 3 * D
OFF_Q = OFF_SC + 3 * SC
OFF_KV = OFF_Q + QL
OFF_KR = OFF_KV + KVL
OFF_GV = OFF_KR + ROPE
OFF_GG = OFF_GV + SC
INV_2PI = 0.15915494309189535
ROUND = 1.5 * 2.0 ** 23
TWO_PI = (6.28125, 0.001934051513671875, 1.255665914356996e-06)
PI_IN = 3.1415925
HALF_PI = 1.5707963267948966
ROPE_STEPS = 10

C_ID, C_UP, C_CAUSAL, C_ROT, C_FREQ, C_IOTA = 0, P, 2 * P, 3 * P, 3 * P + QK, 3 * P + QK + 1
C_COLS = C_IOTA + PAIRS

VEC = {}
_at = 0
for _name, _n in (("mix", DC), ("q", QL // P), ("kv", KVL // P), ("lng", SCC), ("lnb", SCC),
                  ("ffn", DC), ("ple", DC), ("ca", KA * SCC)):
    VEC[_name] = _at
    _at += _n
VROWS = _at
CROWS = KC * SCC

RING = 3
SLOT = 2048
CHUNKS = (["kv"] + [f"q{i}" for i in range(3)] + ["ukv"] + [f"uq{i}" for i in range(4)]
          + ["gg0", "gv0", "gg1", "gv1"] + ["c0", "u0", "b0", "c1", "u1", "b1"]
          + [f"{x}{m}" for m in range(4) for x in ("ga", "gb", "gc", "yab", "yc")]
          + [f"wo{m}" for m in range(4)] + ["pp"] + [f"pg{m}" for m in range(4)])
CI = {c: i for i, c in enumerate(CHUNKS)}
NC = len(CHUNKS)
assert NC % RING == 0

FILL = ["c0", "u0", "b0", "c1", "u1", "b1"]
UNITS = (["kv", "kr", "q0", "q1", "q2", "rotk", "kn0", "kn1", "kn2", "kn3", "v0", "v1",
          "uq0", "uq1", "rot0", "uq2", "rot1", "uq3", "rot2", "gg0", "rot3", "gv0", "gg1", "gv1"]
         + FILL
         + [f"{x}{m}" for m in range(4) for x in ("ga", "gb", "gc", "ya", "yb", "yc")]
         + [f"wo{m}" for m in range(4)] + ["lg", "rank"] + [f"cb{m}" for m in range(4)]
         + ["pp0", "pp1", "pg0", "pp2", "pg1", "pp3", "pg2", "pg3"])
UI = {u: i for i, u in enumerate(UNITS)}
NU = len(UNITS)
BANKS = 3


def chunk_of(unit):
    if unit in CI:
        return unit
    if unit[:2] == "kn" or unit in ("v0", "v1"):
        return "ukv"
    if unit[:2] in ("ya", "yb"):
        return "yab" + unit[2:]
    if unit[:2] == "pp":
        return "pp"
    return None


LAST_UNIT = {}
for _u in UNITS:
    if chunk_of(_u):
        LAST_UNIT[chunk_of(_u)] = UI[_u]

NORMS = ["mix", "kv", "q", "lnm", "lnv", "ffn", "ple"]
POWS = ["mix", "kv", "q", "lnv", "ffn", "ple"]
SQUARES = ([f"mix{i}" for i in range(4)] + ["kv", "q0", "q1", "q2", "lnv"]
           + [f"ffn{i}" for i in range(4)] + [f"ple{i}" for i in range(4)])


def after(events, name):
    return events.index(name) + 1


def program(nc, x, p, positions, ln_mix_g, w_in, conv_a_w, w_out_a, q_norm_g, w_uq, kv_norm_g, w_ukv,
            w_out_b, conv_c_w, ln_c_g, ln_c_b, w_out_c, w_o, ln_ffn_g, w_route_grp, b_route_grp,
            w_route_exp, b_route_exp, w_exp_gate, w_exp_up, w_exp_down, ln_ple_g, w_ple_gate, w_ple,
            final_norm_g, consts, out, windows=WIN):
    ctx = ExitStack()
    with ctx:
        def sb(name, shape, dt=F32):
            return ctx.enter_context(nc.sbuf_tensor(name, shape, dt))

        def sem(name):
            return ctx.enter_context(nc.semaphore(name))

        ring = sb("ring", [P, RING, SLOT])
        gu_ring = sb("gu_ring", [P, ERING, 2, SLOT])
        down_ring = sb("down_ring", [P, ERING, SLOT])
        wsplit = sb("wsplit", [P, 2, 2, 2, KP * FH], F32R)
        xsplit = sb("xsplit", [P, 2, DC, 2 * WIN], F32R)
        xT = sb("xT", [P, DC, S])
        hT = sb("hT", [P, DC, S])
        cst = sb("cst", [P, C_COLS])
        ones = sb("ones", [P, P])
        mhalf = sb("mhalf", [P, 2])
        last_act = sb("last_act", [P, 1])
        last_dve = sb("last_dve", [P, 1])
        cosT = sb("cosT", [QK, S])
        sinT = sb("sinT", [QK, S])
        bc = sb("bc", [P, S])
        bcs = sb("bcs", [P, S])
        diag = sb("diag", [P, 2, P])
        col = sb("col", [P, len(NORMS), 2, 2])
        vrow = sb("vrow", [VROWS, P])
        crow = sb("crow", [CROWS, P])
        vecT = sb("vecT", [P, VROWS])
        convT = sb("convT", [P, CROWS])
        w_rt = sb("w_rt", [P, DC, NG + NE])
        b_rt = sb("b_rt", [P, TC, NG + NE])
        w_kr = sb("w_kr", [P, DC, QK])
        prow = sb("prow", [P, TC, S])
        pT = sb("pT", [P, 2, S])
        starts = sb("starts", [1, WIDE * NE], I32)
        most = sb("most", [1, 1], I32)
        mx = sb("mx", [P, 2, 2, 3])
        work = sb("work", [P, 12928])
        ps = ctx.enter_context(nc.psum_tensor("ps", [P, 8, 512], F32))

        ident = cst[:, C_ID:C_ID + P]
        upper = cst[:, C_UP:C_UP + P]
        causal = cst[:, C_CAUSAL:C_CAUSAL + P]
        rot = cst[0:QK, C_ROT:C_ROT + QK]
        freq = cst[NOPE:QK, C_FREQ:C_FREQ + 1]
        iota = cst[:, C_IOTA:C_IOTA + PAIRS]

        def area(at, *dims):
            n = 1
            for d in dims:
                n *= d
            v = work[:, at:at + n]
            if len(dims) == 2:
                return v.rearrange("p (a b) -> p a b", a=dims[0])
            if len(dims) == 3:
                return v.rearrange("p (a b c) -> p a b c", a=dims[0], b=dims[1])
            return v

        qn = area(0, 6, S)
        kvn = area(1536, 2, S)
        scu = area(0, SCC, S + KA - 1)
        ya = area(1032, SCC, S)
        qT = area(2056, HEADS, S)
        sq_q = area(2056, 6, S)
        sq_kv = area(2056 + 1536, 2, S)
        merged = area(2056, DC, S)
        kT = area(4104, HEADS, S)
        sq_x = area(4104, DC, S)
        v = area(6152, TC, SC)
        attnT = area(7176, SCC, S)
        rtmp = area(7176, 2, 2, S)
        probs = area(8200, 2, 384)
        probsT = area(8200 + 768, 2, 384)
        upad = area(9736, SCC, S + KC - 1)
        conv = area(10880, SCC, S)
        kr = area(10880, 2, S)
        tmp = area(11904, 2, 512)
        sq_ln = area(11904, SCC, S)
        glu_t = [area(11904, 2, 512), area(8200, 2, 512)]
        gate_t = [area(8200, 3, 512), area(4104, 3, 512)]
        ys = area(0, DC, SLOTS)
        h_tok = area(0, TC, D)
        sel = area(2048, TC, PAIRS)
        sel_t = area(3072, TC, PAIRS)
        xs = area(4608, DC, SLOTS)
        gw = area(9216, TC, PAIRS)
        hhT = area(11264, 2, 2 * WIN)
        hflat = hT[0:WIN, :, :].rearrange("p c n -> p (c n)")
        yrow = hflat[:, 0:D]
        gu = hflat[:, D:D + 2 * FH]
        sg = hflat[:, D + 2 * FH:D + 3 * FH]
        hh = hflat[:, D + 3 * FH:D + 4 * FH]
        gu_low = pT[0:WIN, :, :].rearrange("p a n -> p (a n)")
        y_tok = area(4608, 4, D)
        gwT = area(11776, 4, S)
        route_at = [10240]

        def rt(n):
            route_at[0] += 2 * n
            assert route_at[0] <= 12928
            return area(route_at[0] - 2 * n, 2, n)

        logit, gmax, geq, gval, gmin, gone, gpen = rt(NG + NE), rt(1), rt(NG), rt(NG), rt(1), rt(NG), rt(NG)
        masked, masked2 = rt(NE), rt(NE)
        top, teq, tval, tmin = [rt(1), rt(1)], [rt(NE), rt(NE)], [rt(NE), rt(NE)], [rt(1), rt(1)]
        one = [rt(NE), rt(NE)]
        chosen = rt(NE)
        expd, gsum, dplus, weight = rt(NG + 1), rt(1), rt(1), [rt(1), rt(1)]
        ranks = area(route_at[0], 3 * NE)
        route_at[0] += 3 * NE
        prefix = [rt(24), rt(24)]
        prefix = [f.rearrange("p a b -> p (a b)") for f in prefix]
        base, prod, pos = rt(NE), [rt(NE), rt(NE)], [rt(1), rt(1)]
        off = rt(NE // 2).rearrange("p a b -> p (a b)")
        sq_p = area(0, DC, S)
        ple_t = [area(2048, 512), area(2560, 512)]
        ppt = [area(3072, 512), area(3584, 512)]
        xin = area(0, TC, D)
        gfull = area(8192, D)
        xout = area(9216, TC, D)
        ang = area(8192, 4, S)

        init_loaded = sem("init_loaded")
        small_loaded = sem("small_loaded")
        route_loaded = sem("route_loaded")
        wait_carried = sem("wait_carried")
        chunk_loaded = [sem(f"chunk_loaded{i}") for i in range(RING)]
        gu_loaded = [sem(f"gu_loaded{i}") for i in range(ERING)]
        down_loaded = [sem(f"down_loaded{i}") for i in range(ERING)]
        unit_ready = sem("unit_ready")
        gu_taken = sem("gu_taken")
        down_ready = sem("down_ready")
        layer_over = sem("layer_over")
        x_tr = sem("x_tr")
        x_in = sem("x_in")
        rope_step = sem("rope_step")
        rope_sin = sem("rope_sin")
        const_set = sem("const_set")
        out_stored = sem("out_stored")
        zeroed = []

        def lsem(name):
            zeroed.append(sem(name))
            return zeroed[-1]

        evacuated = [lsem(f"evacuated{i}") for i in range(BANKS)]
        vec_tr = lsem("vec_tr")
        vec_ready = lsem("vec_ready")
        h_ready = lsem("h_ready")
        sq_ready = lsem("sq_ready")
        stat_ready = lsem("stat_ready")
        ms_ready = lsem("ms_ready")
        pow_ready = lsem("pow_ready")
        diag_ready = lsem("diag_ready")
        bcast_ready = lsem("bcast_ready")
        bcast_used = lsem("bcast_used")
        dve_step = lsem("dve_step")
        mean_ready = lsem("mean_ready")
        mask_step = lsem("mask_step")
        short_step = lsem("short_step")
        kvn_ready = lsem("kvn_ready")
        qn_ready = lsem("qn_ready")
        k_ready = lsem("k_ready")
        q_cos = lsem("q_cos")
        q_ready = lsem("q_ready")
        glu_sig = lsem("glu_sig")
        u_ready = lsem("u_ready")
        pad_zero = lsem("pad_zero")
        conv_step = lsem("conv_step")
        score_ready = lsem("score_ready")
        max_ready = lsem("max_ready")
        exp_ready = lsem("exp_ready")
        recip_ready = lsem("recip_ready")
        probs_ready = lsem("probs_ready")
        pT_psum = lsem("pT_psum")
        pT_ready = lsem("pT_ready")
        pv_ready = lsem("pv_ready")
        attn_ready = lsem("attn_ready")
        scu_ready = lsem("scu_ready")
        ya_ready = lsem("ya_ready")
        xc_ready = lsem("xc_ready")
        ln_step = lsem("ln_step")
        ln_sig = lsem("ln_sig")
        yc_ready = lsem("yc_ready")
        gate_sig = lsem("gate_sig")
        merge_step = lsem("merge_step")
        merged_ready = lsem("merged_ready")
        tok_psum = lsem("tok_psum")
        tok_read = [lsem("tok_read_act"), lsem("tok_read_dve")]
        onehot_ready = lsem("onehot_ready")
        top_diff = lsem("top_diff")
        top_exp = lsem("top_exp")
        sel_ready = lsem("sel_ready")
        gw_ready = lsem("gw_ready")
        starts_ready = lsem("starts_ready")
        gather_psum = lsem("gather_psum")
        xs_read = [lsem("xs_read_act"), lsem("xs_read_dve")]
        xs_pad = lsem("xs_pad")
        xw_high = lsem("xw_high")
        xw_ready = lsem("xw_ready")
        piece_high = lsem("piece_high")
        piece_low = lsem("piece_low")
        wide_taken = lsem("wide_taken")
        piece_used = lsem("piece_used")
        low_ready = lsem("low_ready")
        gu_summed = lsem("gu_summed")
        down_half = lsem("down_half")
        wide_down = lsem("wide_down")
        sg_ready = lsem("sg_ready")
        hh_part = lsem("hh_part")
        hh_ready = lsem("hh_ready")
        hh_tr = lsem("hh_tr")
        hhT_ready = lsem("hhT_ready")
        yrow_ready = [lsem("yrow_ready_act"), lsem("yrow_ready_dve")]
        yT_psum = lsem("yT_psum")
        ys_ready = lsem("ys_ready")
        gwT_psum = lsem("gwT_psum")
        gwT_ready = lsem("gwT_ready")
        ytok_psum = lsem("ytok_psum")
        ytok_read = [lsem("ytok_read_act"), lsem("ytok_read_dve")]
        pT_tr = lsem("pT_tr")
        p_ready = lsem("p_ready")
        psig_ready = lsem("psig_ready")
        pmul_ready = lsem("pmul_ready")
        engines_done = lsem("engines_done")

        def begin(eng, layers):
            eng.wait_ge(layer_over, layers)
            eng.sem_inc(wait_carried, 1)

        def unit_value(l, name):
            return NU * (l + 1) + UI[name] + 1

        def wait_unit(eng, l, name):
            eng.wait_ge(unit_ready, unit_value(l, name))

        def bank(name):
            return ps[:, UI[name] % BANKS, :]

        def wait_evacuated(eng, name):
            eng.wait_ge(evacuated[UI[name] % BANKS], UI[name] // BANKS + 1)

        def evacuates(instruction, name):
            instruction.then_inc(evacuated[UI[name] % BANKS], 1)

        def two(ap):
            return ap.rearrange("p (a b) -> p a b", a=2)

        def bc2(n=2):
            return bc[:, :].unsqueeze(1).to_broadcast([P, n, S])

        def vcol(name, i):
            return vecT[:, VEC[name] + i:VEC[name] + i + 1]

        block = ctx.enter_context(nc.Block())

        @block.sync
        def _(sp):
            sp.dma_start(xin, x[0].rearrange("(t q) d -> q t d", q=P)).then_inc(init_loaded, 16)
            sp.dma_start(cst[:, :], consts[:, :]).then_inc(init_loaded, 16)
            sp.dma_start(ang[NOPE:QK, 0, :].bitcast(I32), positions[0].partition_broadcast(ROPE)).then_inc(init_loaded, 16)
            sp.sem_inc(unit_ready, NU)
            sp.sem_inc(gu_taken, NE)
            sp.sem_inc(down_ready, NE)

            gate_flat = w_exp_gate.rearrange("l e d f -> (l e) d f")
            up_flat = w_exp_up.rearrange("l e d f -> (l e) d f")
            down_flat = w_exp_down.rearrange("l e f d -> (l e) f d")

            def cols(w, at, n):
                return w[:, at:at + n].rearrange("(c q) n -> q c n", q=P)

            def source(l, name):
                kind, m = name.rstrip("0123456789"), name[len(name.rstrip("0123456789")):]
                m = int(m) if m else 0
                if kind in ("ga", "gb", "gc"):
                    return [cols(w_in[l], "abc".index(kind[1]) * D + 256 * m, 256)]
                if kind in ("b", "c", "u"):
                    return [cols(w_in[l], OFF_SC + "bcu".index(kind) * SC + 256 * m, 256)]
                if kind == "q":
                    return [cols(w_in[l], OFF_Q + 256 * m, 256)]
                if kind == "kv":
                    return [cols(w_in[l], OFF_KV, 256)]
                if kind == "gv":
                    return [cols(w_in[l], OFF_GV + 256 * m, 256)]
                if kind == "gg":
                    return [cols(w_in[l], OFF_GG + 256 * m, 256)]
                if kind == "ukv":
                    return [cols(w_ukv[l], 0, HEADS * (NOPE + VH))]
                if kind == "uq":
                    return [cols(w_uq[l], 2 * QK * m, 2 * QK)]
                if kind == "yab":
                    return [cols(w_out_a[l], 256 * m, 256), cols(w_out_b[l], 256 * m, 256)]
                if kind == "yc":
                    return [cols(w_out_c[l], 256 * m, 256)]
                if kind == "wo":
                    return [cols(w_o[l], 256 * m, 256)]
                if kind == "pp":
                    return [cols(w_ple[l], 0, D)]
                return [cols(w_ple_gate[l], 256 * m, 256)]

            def load_chunk(l, name):
                n = CI[name]
                if n >= RING:
                    sp.wait_ge(unit_ready, NU * (l + 1) + LAST_UNIT[CHUNKS[n - RING]] + 1)
                else:
                    sp.wait_ge(unit_ready, NU * l + LAST_UNIT[CHUNKS[n - RING]] + 1)
                sp.sem_inc(wait_carried, 1)
                at = 0
                parts = source(l, name)
                for i, src in enumerate(parts):
                    k, w = src.shape[1], src.shape[2]
                    dst = ring[:, n % RING, at:at + k * w].rearrange("p (k n) -> p k n", k=k)
                    at += k * w
                    sp.dma_start(dst, src).then_inc(chunk_loaded[n % RING], 16)

            def load_gate_up(l, e, s):
                sp.wait_ge(gu_taken, NE * (l + 1) + e - ERING + 1)
                sp.dma_start(gu_ring[:, s, 0, :], gate_flat[l * NE + e].rearrange("(q c) f -> q (c f)", q=P)).then_inc(gu_loaded[s], 16)
                sp.dma_start(gu_ring[:, s, 1, :], up_flat[l * NE + e].rearrange("(q c) f -> q (c f)", q=P)).then_inc(gu_loaded[s], 16)

            def load_down(l, e, s):
                sp.wait_ge(down_ready, NE * (l + 1) + e - ERING + 1)
                sp.dma_start(down_ring[:, s, :].rearrange("p (c d) -> p c d", c=2),
                             down_flat[l * NE + e].rearrange("(c q) d -> q c d", q=P)).then_inc(down_loaded[s], 16)

            with sp.Fori(0, DEPTH) as l:
                load_chunk(l, CHUNKS[0])
                sp.wait_ge(unit_ready, NU * l + UI["pp0"] + 1)
                sp.sem_inc(wait_carried, 1)
                for name, w in (("mix", ln_mix_g), ("q", q_norm_g), ("kv", kv_norm_g), ("lng", ln_c_g),
                                ("lnb", ln_c_b), ("ffn", ln_ffn_g), ("ple", ln_ple_g)):
                    n = w.shape[1] // P
                    sp.dma_start(vrow[VEC[name]:VEC[name] + n, :], w[l].rearrange("(c q) -> c q", q=P)).then_inc(small_loaded, 16)
                sp.dma_start(vrow[VEC["ca"]:VEC["ca"] + KA * SCC, :], conv_a_w[l].rearrange("k (c q) -> (k c) q", q=P)).then_inc(small_loaded, 16)
                sp.dma_start(crow[:, :], conv_c_w[l].rearrange("k (c q) -> (k c) q", q=P)).then_inc(small_loaded, 16)
                sp.dma_start(w_kr[:, :, :], cols(w_in[l], OFF_KR - NOPE, QK)).then_inc(small_loaded, 16)
                for c in CHUNKS[1:4]:
                    load_chunk(l, c)
                sp.dma_start(w_rt[:, :, 0:NG], cols(w_route_grp[l], 0, NG)).then_inc(route_loaded, 16)
                sp.dma_start(w_rt[:, :, NG:NG + NE], cols(w_route_exp[l], 0, NE)).then_inc(route_loaded, 16)
                for t in range(TC):
                    sp.dma_start(b_rt[:, t, 0:NG], b_route_grp[l].partition_broadcast(P)).then_inc(route_loaded, 16)
                    sp.dma_start(b_rt[:, t, NG:NG + NE], b_route_exp[l].partition_broadcast(P)).then_inc(route_loaded, 16)
                sp.dma_start(prow[:, :, :], p[l, 0].rearrange("(t q) d -> q t d", q=P)).then_inc(route_loaded, 16)
                for c in CHUNKS[4:16]:
                    load_chunk(l, c)
                for s in range(ERING):
                    load_gate_up(l, s, s)
                    load_down(l, s, s)
                    load_chunk(l, CHUNKS[16 + s])
                for c in CHUNKS[16 + ERING:CI["wo3"] + RING]:
                    load_chunk(l, c)
                load_gate_up(l, ERING, 0)
                with sp.Fori(0, (NE - ERING) // ERING) as it:
                    for i in range(ERING, 2 * ERING):
                        load_gate_up(l, it * ERING + i + 1, (i + 1) % ERING)
                        load_down(l, it * ERING + i, i % ERING)
                for e in range(NE - (NE - ERING) % ERING, NE):
                    if e + 1 < NE:
                        load_gate_up(l, e + 1, (e + 1) % ERING)
                    load_down(l, e, e % ERING)
                for c in CHUNKS[CI["wo3"] + RING:]:
                    load_chunk(l, c)
            sp.wait_ge(layer_over, DEPTH + 1)
            sp.dma_start(gfull, final_norm_g.partition_broadcast(P)).then_inc(init_loaded, 16)
            for t in range(TC):
                sp.wait_ge(pmul_ready, t + 1)
                sp.dma_start(out[0, t * P:(t + 1) * P, :], xout[:, t, :]).then_inc(out_stored, 16)
            sp.wait_ge(out_stored, 16 * TC)

        SMALL = 10
        ROUTES = 2 + 2 * TC + 1

        def wait_last_ys(eng, most_reg, windows, ys_sem):
            with eng.If(most_reg > windows):
                eng.wait_ge(ys_sem, WIDE * NE)
            with eng.Else():
                eng.wait_ge(ys_sem, NE)

        def expert_of(it, k, per):
            return it * BODY + k // per

        def window_of(it, k, per):
            return it * (BODY * per) + k

        def windows_of(eng, per, step):
            for k in range(PEEL * per):
                step(0, k, True, False)
            with eng.Fori(0, NE // BODY) as it:
                for k in range(PEEL * per, (PEEL + BODY) * per):
                    step(it, k, False, False)
            for k in range((PEEL + BODY) * per, (PEEL + BODY) * per + 2):
                step(NE // BODY - 1, k, False, True)

        def loads_of(l, it, k, per, each):
            e = k // per
            of_layer = len(range(e % ERING, NE, ERING))
            return l * (each * of_layer) + it * (each * BODY // ERING) + each * (e // ERING + 1)

        def wait_down(eng, l, it, k, per):
            if k % per == per - 1:
                eng.wait_ge(down_ready, NE * (l + 1) + expert_of(it, k, per) + 1)
            else:
                eng.wait_ge(wide_down, expert_of(it, k, per) * (per - 1) + k % per + 1)

        @block.tensor
        def _(pe):
            def mm(o, lhsT, rhs, first, last):
                return nc.tensor.matmul(o, lhsT, rhs, start=first, stop=last)

            def tr(o, i, n=P):
                return nc.tensor.transpose(o, i, ident[0:n, 0:n])

            pe.wait_ge(init_loaded, 48)
            for c in range(DC):
                for t in range(TC):
                    last = tr(ps[:, c // 2, (c % 2) * S + t * P:(c % 2) * S + (t + 1) * P], xin[:, t, c * P:(c + 1) * P])
                if c % 2:
                    last.then_inc(x_tr, 1)

            def stat(name, tiles, squares):
                n = len(tiles)
                if name != NORMS[0]:
                    pe.wait_ge(bcast_used, after(NORMS, name) - 1)
                for t in range(TC):
                    for c in range(n):
                        if t == 0 and squares[c] is not None:
                            pe.wait_ge(*squares[c])
                        last = mm(ps[:, 3, t:t + 1], tiles[c][:, t * P:(t + 1) * P], ones[:, 0:1], c == 0, c == n - 1)
                last.then_inc(stat_ready, 1)

            def bcast(name):
                pe.wait_ge(diag_ready, after(NORMS, name))
                for t in range(TC):
                    last = mm(ps[:, 3, S + t * P:S + (t + 1) * P], ones[:, :], diag[:, t, :], True, True)
                last.then_inc(bcast_ready, 1)

            def sq_events(name, n):
                return [(sq_ready, after(SQUARES, f"{name}{c // 2}")) for c in range(n)]

            with pe.Fori(0, DEPTH) as l:
                begin(pe, l + 1)

                def wait_chunk(name):
                    n = CI[name]
                    slot = n % RING
                    upto = sum(2 if c[:3] == "yab" else 1 for c in CHUNKS[slot:n + 1:RING])
                    whole = sum(2 if c[:3] == "yab" else 1 for c in CHUNKS[slot::RING])
                    pe.wait_ge(chunk_loaded[slot], l * (16 * whole) + 16 * upto)

                def free_bank(name):
                    if UI[name] >= BANKS:
                        wait_evacuated(pe, UNITS[UI[name] - BANKS])

                def project(name, rhs, k, waits=(), at=0, width=256):
                    wait_chunk(chunk_of(name))
                    free_bank(name)
                    w = ring[:, CI[chunk_of(name)] % RING, at:at + k * width].rearrange("p (k n) -> p k n", k=k)
                    for m in range(2):
                        for c in range(k):
                            if m == 0 and waits:
                                if waits[c] is not None:
                                    pe.wait_ge(*waits[c])
                            last = mm(two(bank(name))[:, m, :], w[:, c, m * P:(m + 1) * P], rhs[:, c, :], c == 0, c == k - 1)
                    last.then_inc(unit_ready, 1)

                def h_events(name):
                    return [(h_ready, DC * ["mix", "ffn", "ple"].index(name) + c + 1) for c in range(DC)]

                pe.wait_ge(small_loaded, l * (16 * SMALL) + 16 * SMALL)
                tr(ps[:, 6, 0:CROWS], crow[:, :], CROWS).then_inc(vec_tr, 1)
                tr(ps[:, 7, 0:VROWS], vrow[:, :], VROWS).then_inc(vec_tr, 1)
                stat("mix", [sq_x[:, c, :] for c in range(DC)], sq_events("mix", DC))
                project("kv", hT, DC, h_events("mix"))
                for c in range(DC):
                    last = mm(bank("kr")[0:QK, 0:S], w_kr[:, c, :], hT[:, c, :], c == 0, c == DC - 1)
                last.then_inc(unit_ready, 1)
                bcast("mix")
                project("q0", hT, DC)
                project("q1", hT, DC)
                stat("kv", [sq_kv[:, c, :] for c in range(2)], [(sq_ready, after(SQUARES, "kv"))] * 2)
                project("q2", hT, DC)
                bcast("kv")
                free_bank("rotk")
                wait_evacuated(pe, "kr")
                mm(bank("rotk")[0:QK, 0:S], rot, kr[0:QK, 0, :], True, True).then_inc(unit_ready, 1)
                wait_chunk("ukv")
                ukv = ring[:, CI["ukv"] % RING, :].rearrange("p (k h n) -> p k h n", k=2, h=HEADS)
                pe.wait_ge(kvn_ready, 2)
                for i in range(4):
                    free_bank(f"kn{i}")
                    for j in range(2):
                        for c in range(2):
                            last = mm(two(bank(f"kn{i}"))[0:NOPE, j, :], ukv[:, c, 2 * i + j, 0:NOPE], kvn[:, c, :], c == 0, c == 1)
                    last.then_inc(unit_ready, 1)
                for t in range(TC):
                    free_bank(f"v{t}")
                    for c in range(2):
                        last = mm(bank(f"v{t}").rearrange("p (h n) -> p h n", h=HEADS), kvn[:, c, t * P:(t + 1) * P],
                                  ukv[:, c, :, NOPE:NOPE + VH], c == 0, c == 1)
                    last.then_inc(unit_ready, 1)
                stat("q", [sq_q[:, c, :] for c in range(6)], sq_events("q", 6))
                bcast("q")

                def queries(i):
                    wait_chunk(f"uq{i}")
                    free_bank(f"uq{i}")
                    w = ring[:, CI[f"uq{i}"] % RING, 0:6 * 2 * QK].rearrange("p (k n) -> p k n", k=6)
                    for j in range(2):
                        for c in range(6):
                            if i == 0 and j == 0:
                                pe.wait_ge(qn_ready, c + 1)
                            last = mm(two(bank(f"uq{i}"))[0:QK, j, :], w[:, c, j * QK:(j + 1) * QK], qn[:, c, :], c == 0, c == 5)
                    last.then_inc(unit_ready, 1)

                def rotate(i):
                    wait_evacuated(pe, f"uq{i}")
                    free_bank(f"rot{i}")
                    mm(bank(f"rot{i}")[0:QK, :], rot, qT[0:QK, 2 * i:2 * i + 2, :], True, True).then_inc(unit_ready, 1)

                queries(0)
                queries(1)
                rotate(0)
                queries(2)
                rotate(1)
                queries(3)
                rotate(2)
                project("gg0", hT, DC)
                rotate(3)
                project("gv0", hT, DC)
                project("gg1", hT, DC)
                project("gv1", hT, DC)

                def scores(h):
                    pe.wait_ge(q_ready, h // 2 + 1)
                    if h == 0:
                        pe.wait_ge(k_ready, 1)
                        for i in range(4):
                            wait_evacuated(pe, f"kn{i}")
                    if h >= 2:
                        pe.wait_ge(exp_ready, 2 * (h - 1))
                    mm(ps[:, 4 + h % 2, 0:P], qT[0:QK, h, 0:P], kT[0:QK, h, 0:P], True, True)
                    mm(ps[:, 4 + h % 2, P:3 * P], qT[0:QK, h, P:S], kT[0:QK, h, :], True, True).then_inc(score_ready, 1)

                def transpose_probs(h):
                    pe.wait_ge(probs_ready, 2 * (h + 1))
                    if h >= 1:
                        pe.wait_ge(pT_ready, h)
                    for i in range(3):
                        last = tr(ps[:, 6, i * P:(i + 1) * P], probs[:, h % 2, i * P:(i + 1) * P])
                    last.then_inc(pT_psum, 1)

                def weigh_values(h):
                    pe.wait_ge(pT_ready, h + 1)
                    if h == 0:
                        wait_evacuated(pe, "v0")
                        wait_evacuated(pe, "v1")
                    if h >= 1:
                        pe.wait_ge(attn_ready, h)
                    o = ps[:, 7, 0:S]
                    mm(o, v[:, 0, (h // 2) * P:(h // 2 + 1) * P], probsT[:, h % 2, 0:S], True, False)
                    mm(o[:, P:S], v[:, 1, (h // 2) * P:(h // 2 + 1) * P], probsT[:, h % 2, S:3 * P], False, True).then_inc(pv_ready, 1)

                scores(0)
                scores(1)
                for h in range(HEADS):
                    transpose_probs(h)
                    if h + 2 < HEADS:
                        scores(h + 2)
                    if h < len(FILL):
                        project(FILL[h], hT, DC)
                    weigh_values(h)

                for m in range(4):
                    project(f"ga{m}", hT, DC)
                    if m == 0:
                        stat("lnm", [conv[:, c, :] for c in range(SCC)], [(conv_step, KC * SCC)] + [None] * 3)
                    project(f"gb{m}", hT, DC)
                    if m == 0:
                        bcast("lnm")
                    project(f"gc{m}", hT, DC)
                    if m == 0:
                        pe.wait_ge(ya_ready, 2)
                    project(f"ya{m}", ya, SCC)
                    if m == 0:
                        stat("lnv", [sq_ln[:, c, :] for c in range(SCC)], [(sq_ready, after(SQUARES, "lnv"))] + [None] * 3)
                        pe.wait_ge(attn_ready, HEADS)
                    project(f"yb{m}", attnT, SCC, at=SLOT // 2)
                    if m == 0:
                        bcast("lnv")
                    project(f"yc{m}", conv, SCC, [(yc_ready, c + 1) for c in range(SCC)])
                for m in range(4):
                    project(f"wo{m}", merged, DC, [(merged_ready, c // 2 + 1) for c in range(DC)])

                stat("ffn", [sq_x[:, c, :] for c in range(DC)], sq_events("ffn", DC))
                bcast("ffn")
                free_bank("lg")
                pe.wait_ge(route_loaded, l * (16 * ROUTES) + 16 * ROUTES)
                lgp = bank("lg")[:, 0:TC * (NG + NE)].rearrange("p (t n) -> p t n", t=TC)
                for t in range(TC):
                    for c in range(DC):
                        if t == 0:
                            pe.wait_ge(h_ready, DC + c + 1)
                        last = mm(lgp[:, t, :], hT[:, c, t * P:(t + 1) * P], w_rt[:, c, :], c == 0, c == DC - 1)
                last.then_inc(unit_ready, 1)
                for i in range(4):
                    for j in range(4):
                        t, c = i // 2, (i % 2) * 4 + j
                        last = tr(ps[:, 4 + i, j * P:(j + 1) * P], hT[:, c, t * P:(t + 1) * P])
                    last.then_inc(tok_psum, 1)
                free_bank("rank")
                pe.wait_ge(onehot_ready, 1)
                a0, a1 = chosen[:, 0, :], chosen[:, 1, :]
                rk = bank("rank")
                mm(rk[:, 0:NE], upper, a0, True, True)
                mm(rk[:, NE:2 * NE], ones[:, :], a0, True, False)
                mm(rk[:, NE:2 * NE], upper, a1, False, True)
                mm(rk[:, 2 * NE:3 * NE], ones[:, :], a0, True, False)
                mm(rk[:, 2 * NE:3 * NE], ones[:, :], a1, False, True).then_inc(unit_ready, 1)
                pe.wait_ge(tok_read[0], 2)
                pe.wait_ge(tok_read[1], 2)
                for c in range(DC):
                    for t in range(TC):
                        if c == 0:
                            pe.wait_ge(sel_ready, t + 1)
                        if t == 0 and c >= 4:
                            pe.wait_ge(xs_read[c % 2], (c - 4) // 2 + 1)
                        last = mm(ps[:, 4 + c % 4, :], h_tok[:, t, :].rearrange("p (q c) -> p c q", c=DC)[:, c, :],
                                  sel[:, t, :], t == 0, t == TC - 1)
                    last.then_inc(gather_psum, 1)

                def experts(per):
                    def gate_up(it, k, q):
                        w, b = window_of(it, k, per), k % 2
                        if q == 0:
                            pe.wait_ge(xw_ready, w + 1)
                        if q < PIECES - 1:
                            pe.wait_ge(piece_low, (PIECES - 1) * w + q + 1)
                        elif k % per == per - 1:
                            pe.wait_ge(gu_taken, NE * (l + 1) + expert_of(it, k, per) + 1)
                        else:
                            pe.wait_ge(wide_taken, expert_of(it, k, per) * (per - 1) + k % per + 1)
                        for c in range(KP):
                            for part in range(2):
                                last = mm(two(ps[:, b, :]), xsplit[:, b, KP * q + c, :], wsplit[:, q % 2, part, :, c * FH:(c + 1) * FH],
                                          q + c + part == 0, q == PIECES - 1 and c + part == KP)
                        last.then_inc(piece_used, 1)

                    def turn_hidden(it, k):
                        pe.wait_ge(hh_ready, window_of(it, k, per) + 1)
                        pe.sem_inc(wait_carried, 1)
                        for c in range(2):
                            last = tr(ps[:, 4 + k % 2, c * WIN:(c + 1) * WIN], hh[:, c * P:(c + 1) * P], WIN)
                        last.then_inc(hh_tr, 1)

                    def down(it, k, n):
                        half, c = n // 2, n % 2
                        w = window_of(it, k, per)
                        if n == 0:
                            if k % per == 0:
                                pe.wait_ge(down_loaded[k // per % ERING], loads_of(l, it, k, per, 16))
                            pe.wait_ge(hhT_ready, w + 1)
                        wd = down_ring[:, k // per % ERING, :].rearrange("p (c n) -> p c n", c=2)
                        last = mm(ps[0:WIN, 6 + half, :], hhT[:, k % 2, c * WIN:(c + 1) * WIN], wd[:, c, half * 512:(half + 1) * 512], c == 0, c == 1)
                        if n == 1:
                            last.then_inc(down_half, 1)
                        if n == 3:
                            last.then_inc(down_ready if k % per == per - 1 else wide_down, 1)

                    def turn_out(it, k, half):
                        w = window_of(it, k, per)
                        pe.wait_ge(yrow_ready[half], w + 1)
                        if half == 0 and k >= 2:
                            pe.wait_ge(ys_ready, w - 1)
                        pe.sem_inc(wait_carried, 1)
                        for c in range(half * 4, half * 4 + 4):
                            last = tr(ps[:, 2 + k % 2, c * WIN:(c + 1) * WIN], yrow[:, c * P:(c + 1) * P], WIN)
                        if half == 1:
                            last.then_inc(yT_psum, 1)

                    def step(it, k, first, ending):
                        one_before = k >= 1 and k <= (PEEL + BODY) * per
                        two_before = k >= 2
                        if not ending:
                            gate_up(it, k, 0)
                        if two_before:
                            down(it, k - 2, 3)
                        if not ending:
                            gate_up(it, k, 1)
                        if one_before:
                            turn_hidden(it, k - 1)
                        if two_before:
                            turn_out(it, k - 2, 0)
                        if not ending:
                            gate_up(it, k, 2)
                        if two_before:
                            turn_out(it, k - 2, 1)
                        if one_before:
                            down(it, k - 1, 0)
                        if not ending:
                            gate_up(it, k, 3)
                        if one_before:
                            down(it, k - 1, 1)
                            down(it, k - 1, 2)

                    windows_of(pe, per, step)

                wait_evacuated(pe, "rank")
                wait_evacuated(pe, "lg")
                pe.wait_ge(starts_ready, 2)
                most_pe = pe.value_load(most[0:1, 0:1], min_val=0, max_val=S)
                with pe.If(most_pe > windows):
                    experts(WIDE)
                with pe.Else():
                    experts(1)

                pe.wait_ge(gw_ready, 2)
                for t in range(TC):
                    for s in range(4):
                        b = 4 + t
                        last = tr(ps[:, b, s * P:(s + 1) * P], gw[:, t, s * P:(s + 1) * P])
                    last.then_inc(gwT_psum, 1)
                for s in range(4):
                    for half in range(2):
                        i = 2 * s + half
                        if i == 0:
                            wait_last_ys(pe, most_pe, windows, ys_ready)
                        if i >= 2:
                            pe.wait_ge(ytok_read[i % 2], (i - 2) // 2 + 1)
                        for j in range(4):
                            last = tr(ps[:, 6 + i % 2, j * P:(j + 1) * P], ys[:, half * 4 + j, s * P:(s + 1) * P])
                        last.then_inc(ytok_psum, 1)
                pe.wait_ge(gwT_ready, 2)
                pe.wait_ge(ytok_read[0], 4)
                pe.wait_ge(ytok_read[1], 4)
                for m in range(4):
                    free_bank(f"cb{m}")
                    for j in range(2):
                        for s in range(4):
                            last = mm(two(bank(f"cb{m}"))[:, j, :], y_tok[:, s, (2 * m + j) * P:(2 * m + j + 1) * P],
                                      gwT[:, s, :], s == 0, s == 3)
                    last.then_inc(unit_ready, 1)

                for i in range(2):
                    for t in range(TC):
                        last = tr(ps[:, 7, i * S + t * P:i * S + (t + 1) * P], prow[:, t, i * P:(i + 1) * P])
                last.then_inc(pT_tr, 1)
                pe.wait_ge(p_ready, 1)

                def embed(m):
                    wait_chunk("pp")
                    free_bank(f"pp{m}")
                    w = ring[:, CI["pp"] % RING, :].rearrange("p (k n) -> p k n", k=2)
                    for j in range(2):
                        for c in range(2):
                            last = mm(two(bank(f"pp{m}"))[:, j, :], w[:, c, (2 * m + j) * P:(2 * m + j + 1) * P],
                                      pT[:, c, :], c == 0, c == 1)
                    last.then_inc(unit_ready, 1)

                embed(0)
                embed(1)
                stat("ple", [sq_p[:, c, :] for c in range(DC)], sq_events("ple", DC))
                project("pg0", hT, DC, h_events("ple"))
                bcast("ple")
                for m in range(1, 4):
                    if m < 3:
                        embed(m + 1)
                    project(f"pg{m}", hT, DC)
                pe.wait_ge(bcast_used, len(NORMS))
                mm(ps[:, 3, 0:1], ones[:, :], ones[:, 0:1], True, True).then_inc(engines_done, 1)
            begin(pe, DEPTH + 1)
            stat("mix", [sq_x[:, c, :] for c in range(DC)], sq_events("mix", DC))
            for i in range(4):
                for j in range(4):
                    t, c = i // 2, (i % 2) * 4 + j
                    last = tr(ps[:, 4 + i, j * P:(j + 1) * P], xT[:, c, t * P:(t + 1) * P])
                last.then_inc(tok_psum, 1)

        @block.scalar
        def _(act):
            def copy(o, i):
                return nc.scalar.activation(o, i, ACT.Copy)

            def squares(name, dst, src, units):
                for i, unit in enumerate(units):
                    if unit:
                        wait_evacuated(act, unit)
                    nc.scalar.activation(dst[:, 2 * i:2 * i + 2, :], src[:, 2 * i:2 * i + 2, :], ACT.Square).then_inc(sq_ready, 1)

            for i in range(2):
                act.wait_ge(x_tr, 2 * i + 1)
                copy(xT[:, 4 * i:4 * i + 2, :], ps[:, 2 * i, :]).then_inc(x_in, 1)
            act.wait_ge(rope_step, ROPE_STEPS)
            act.wait_ge(init_loaded, 48)
            nc.scalar.activation(sinT[NOPE:QK, :], ang[NOPE:QK, 0, :], ACT.Sin).then_inc(rope_sin, 1)
            nc.scalar.activation(cosT[NOPE:QK, :], ang[NOPE:QK, 2, :], ACT.Sin).then_inc(rope_sin, 1)

            def high(l, it, k, q, per):
                n = PIECES * window_of(it, k, per) + q
                s = k // per % ERING
                if q == 0 and k % per == 0:
                    act.wait_ge(gu_loaded[s], loads_of(l, it, k, per, 32))
                if k > 0 or q >= 2:
                    act.wait_ge(piece_used, n - 1)
                copy(wsplit[:, q % 2, 0, :, :], gu_ring[:, s, :, q * KP * FH:(q + 1) * KP * FH]).then_inc(piece_high, 1)

            with act.Fori(0, DEPTH) as l:
                begin(act, l + 1)
                act.wait_ge(x_in, 4)
                squares("mix", sq_x, xT, [None] * 4)
                act.wait_ge(vec_tr, 1)
                copy(convT[:, :], ps[:, 6, 0:CROWS]).then_inc(vec_ready, 1)
                act.wait_ge(vec_tr, 2)
                copy(vecT[:, :], ps[:, 7, 0:VROWS]).then_inc(vec_ready, 1)
                squares("kv", sq_kv, two(tmp[:, 0, :]), ["kv"])
                squares("q", sq_q, qn, [f"q{i}" for i in range(3)])
                for i in range(4):
                    wait_unit(act, l, f"kn{i}")
                    evacuates(copy(kT[0:NOPE, 2 * i:2 * i + 2, :], two(bank(f"kn{i}"))[0:NOPE, :, :]), f"kn{i}")
                for t in range(TC):
                    wait_unit(act, l, f"v{t}")
                    evacuates(copy(v[:, t, :], bank(f"v{t}")), f"v{t}")
                for i in range(4):
                    wait_unit(act, l, f"uq{i}")
                    if i == 0:
                        act.wait_ge(stat_ready, after(NORMS, "q"))
                    evacuates(copy(qT[0:QK, 2 * i:2 * i + 2, :], two(bank(f"uq{i}"))[0:QK, :, :]), f"uq{i}")
                for i in range(2):
                    wait_evacuated(act, f"gg{i}")
                    nc.scalar.activation(glu_t[i][:, 0, :], glu_t[i][:, 0, :], ACT.Sigmoid).then_inc(glu_sig, 1)

                def exponentials(h):
                    act.wait_ge(max_ready, h + 1)
                    if h == 0:
                        act.wait_ge(u_ready, 2)
                    if h >= 2:
                        act.wait_ge(pT_psum, h - 1)
                    for i, (a, b) in enumerate(((0, P), (P, 3 * P))):
                        nc.scalar.activation(probs[:, h % 2, a:b], ps[:, 4 + h % 2, a:b], ACT.Exp,
                                             bias=mx[:, h % 2, i, 1:2], scale=SCALE,
                                             accum_out=mx[:, h % 2, i, 2:3]).then_inc(exp_ready, 1)

                def copy_transposed(h):
                    act.wait_ge(pT_psum, h + 1)
                    if h >= 2:
                        act.wait_ge(pv_ready, h - 1)
                    copy(probsT[:, h % 2, :], ps[:, 6, 0:3 * P]).then_inc(pT_ready, 1)

                def copy_attention(h):
                    act.wait_ge(pv_ready, h + 1)
                    r = (h % 2) * VH
                    if h == 0:
                        act.wait_ge(q_ready, 4)
                    copy(attnT[r:r + VH, h // 2, :], ps[r:r + VH, 7, 0:S]).then_inc(attn_ready, 1)

                exponentials(0)
                exponentials(1)
                for h in range(HEADS):
                    copy_transposed(h)
                    if h + 2 < HEADS:
                        exponentials(h + 2)
                    if h >= 1:
                        copy_attention(h - 1)
                copy_attention(HEADS - 1)

                def gate_sigmoids(m):
                    for i in range(3):
                        wait_evacuated(act, f"g{'abc'[i]}{m}")
                        nc.scalar.activation(gate_t[m % 2][:, i, :], gate_t[m % 2][:, i, :], ACT.Sigmoid).then_inc(gate_sig, 1)

                act.wait_ge(xc_ready, 1)
                nc.scalar.activation(sq_ln, conv, ACT.Square).then_inc(sq_ready, 1)
                gate_sigmoids(0)
                for c in range(SCC):
                    act.wait_ge(ln_step, c + 1)
                    nc.scalar.activation(sq_ln[:, c, :], conv[:, c, :], ACT.Sigmoid, bias=vcol("lnb", c)).then_inc(ln_sig, 1)
                for m in range(1, 4):
                    gate_sigmoids(m)
                act.wait_ge(merged_ready, 4)
                squares("ffn", sq_x, xT, [f"wo{m}" for m in range(4)])
                for i in (0, 2):
                    act.wait_ge(tok_psum, i + 1)
                    copy(h_tok[:, i // 2, (i % 2) * 512:(i % 2 + 1) * 512], ps[:, 4 + i, :]).then_inc(tok_read[0], 1)
                for q in range(2):
                    high(l, 0, 0, q, 1)
                act.wait_ge(top_diff, 1)
                nc.scalar.activation(expd, expd, ACT.Exp).then_inc(top_exp, 1)
                for c in range(0, DC, 2):
                    act.wait_ge(gather_psum, c + 1)
                    copy(xs[:, c, 0:PAIRS], ps[:, 4 + c % 4, :]).then_inc(xs_read[0], 1)

                def experts(per):
                    def sigmoid(it, k):
                        w = window_of(it, k, per)
                        act.wait_ge(gu_summed, w + 1)
                        if k >= 1:
                            act.wait_ge(hh_ready, w)
                        nc.scalar.activation(sg, gu[:, 0:FH], ACT.Sigmoid).then_inc(sg_ready, 1)

                    def take_low(it, k):
                        w = window_of(it, k, per)
                        act.wait_ge(piece_used, PIECES * (w + 1))
                        if k >= 1:
                            act.wait_ge(gu_summed, w)
                        copy(gu_low, ps[WIN:2 * WIN, k % 2, :]).then_inc(low_ready, 1)

                    def place(it, k):
                        w = window_of(it, k, per)
                        at = act.value_load(starts[0:1, bass.ds(expert_of(it, k, per) + k % per * NE, 1)], min_val=0, max_val=PAIRS)
                        act.wait_ge(yT_psum, w + 1)
                        if k > 0:
                            act.wait_ge(ys_ready, w)
                        copy(ys[:, :, bass.ds(at, WIN)], ps[:, 2 + k % 2, :].rearrange("p (m n) -> p m n", m=DC)).then_inc(ys_ready, 1)

                    def take_rows(it, k):
                        act.wait_ge(down_half, window_of(it, k, per) + 1)
                        copy(yrow[:, 0:512], ps[0:WIN, 6, :]).then_inc(yrow_ready[0], 1)

                    def step(it, k, first, ending):
                        one_before = k >= 1 and k <= (PEEL + BODY) * per
                        two_before = k >= 2
                        if not ending and k > 0:
                            high(l, it, k, 0, per)
                        if one_before:
                            take_low(it, k - 1)
                        if not ending and k > 0:
                            high(l, it, k, 1, per)
                        if one_before:
                            sigmoid(it, k - 1)
                        if two_before:
                            take_rows(it, k - 2)
                        if not ending:
                            high(l, it, k, 2, per)
                            high(l, it, k, 3, per)
                        if two_before:
                            place(it, k - 2)

                    windows_of(act, per, step)

                act.wait_ge(starts_ready, 2)
                act.wait_ge(gather_psum, DC)
                most_act = act.value_load(most[0:1, 0:1], min_val=0, max_val=S)
                with act.If(most_act > windows):
                    experts(WIDE)
                with act.Else():
                    experts(1)
                for i in (0, 2, 4, 6):
                    act.wait_ge(ytok_psum, i + 1)
                    copy(y_tok[:, i // 2, 0:512], ps[:, 6, :]).then_inc(ytok_read[0], 1)
                act.wait_ge(pT_tr, 1)
                copy(pT[:, :, :], two(ps[:, 7, :])).then_inc(p_ready, 1)
                squares("ple", sq_p, xT, [f"cb{m}" for m in range(4)])

                def copy_embedding(m):
                    wait_unit(act, l, f"pp{m}")
                    if m >= 2:
                        act.wait_ge(pmul_ready, m - 1)
                    evacuates(copy(ppt[m % 2], bank(f"pp{m}")), f"pp{m}")

                def ple_sigmoid(m):
                    wait_evacuated(act, f"pg{m}")
                    last = nc.scalar.activation(ple_t[m % 2], ple_t[m % 2], ACT.Sigmoid)
                    last.then_inc(psig_ready, 1)

                copy_embedding(0)
                copy_embedding(1)
                for m in range(4):
                    ple_sigmoid(m)
                    if m < 2:
                        copy_embedding(m + 2)
                act.wait_ge(psig_ready, 4)
                copy(last_act[:, :], ones[:, 0:1]).then_inc(engines_done, 1)
            begin(act, DEPTH + 1)
            squares("mix", sq_x, xT, [None] * 4)


        @block.gpsimd
        def _(pool):
            nc.gpsimd.memset(ones[:, :], 1.0).then_inc(const_set, 1)
            nc.gpsimd.memset(mhalf[:, :], -0.5).then_inc(const_set, 1)
            pool.wait_ge(const_set, 2)
            pool.sem_inc(layer_over, 1)

            def power(name):
                i = NORMS.index(name)
                pool.wait_ge(ms_ready, after(POWS, name))
                nc.gpsimd.tensor_tensor(col[:, i, 1, :], col[:, i, 0, :], mhalf[:, :], ALU.pow).then_inc(pow_ready, 1)

            with pool.Fori(0, DEPTH) as l:
                nc.gpsimd.memset(upad[:, :, 0:KC - 1], 0.0).then_inc(pad_zero, 1)
                power("mix")
                power("kv")
                wait_evacuated(pool, "rotk")
                pool.wait_ge(rope_sin, 2)
                nc.gpsimd.tensor_tensor(kr[NOPE:QK, 0, :], kr[NOPE:QK, 0, :], cosT[NOPE:QK, :], ALU.mult).then_inc(q_cos, 1)
                pool.wait_ge(q_cos, 1)
                nc.gpsimd.tensor_tensor(kr[NOPE:QK, 0, :], kr[NOPE:QK, 0, :], kr[NOPE:QK, 1, :], ALU.add).then_inc(q_cos, 1)
                pool.wait_ge(q_cos, 2)
                nc.gpsimd.tensor_copy(kT[NOPE:QK, :, :], kr[NOPE:QK, 0, :].unsqueeze(1).to_broadcast([ROPE, HEADS, S])).then_inc(k_ready, 1)
                pool.wait_ge(k_ready, 1)
                power("q")
                for i in range(4):
                    q2 = qT[NOPE:QK, 2 * i:2 * i + 2, :]
                    wait_evacuated(pool, f"rot{i}")
                    nc.gpsimd.tensor_tensor(q2, q2, cosT[NOPE:QK, :].unsqueeze(1).to_broadcast([ROPE, 2, S]), ALU.mult).then_inc(q_cos, 1)
                    pool.wait_ge(q_cos, i + 3)
                    nc.gpsimd.tensor_tensor(q2, q2, rtmp[NOPE:QK, i % 2, :, :], ALU.add).then_inc(q_ready, 1)
                pool.wait_ge(q_ready, 4)
                for i in range(2):
                    pool.wait_ge(glu_sig, i + 1)
                    wait_evacuated(pool, f"gv{i}")
                    if i == 0:
                        pool.wait_ge(pad_zero, 1)
                    nc.gpsimd.tensor_tensor(upad[:, 2 * i:2 * i + 2, KC - 1:], two(glu_t[i][:, 1, :]), two(glu_t[i][:, 0, :]), ALU.mult).then_inc(u_ready, 1)
                wait_evacuated(pool, "uq3")
                nc.gpsimd.memset(scu[:, :, 0:KA - 1], 0.0).then_inc(pad_zero, 1)
                for h in range(HEADS):
                    pool.wait_ge(recip_ready, h + 1)
                    for i, (a, b) in enumerate(((0, P), (P, 3 * P))):
                        pool.wait_ge(exp_ready, 2 * (h + 1)) if i == 0 else None
                        nc.gpsimd.tensor_scalar(probs[:, h % 2, a:b], probs[:, h % 2, a:b], mx[:, h % 2, i, 0:1], None,
                                                ALU.mult).then_inc(probs_ready, 1)
                    if h in (1, 4):
                        i = h // 3
                        wait_evacuated(pool, f"u{i}")
                        half = scu[:, 2 * i:2 * i + 2, KA - 1:]
                        nc.gpsimd.tensor_tensor(half, half, two(tmp[:, 0, :]), ALU.mult).then_inc(scu_ready, 1)
                power("lnv")
                for m in range(4):
                    g = gate_t[m % 2]
                    wait_evacuated(pool, f"ya{m}")
                    wait_evacuated(pool, f"yb{m}")
                    nc.gpsimd.tensor_tensor(merged[:, 2 * m:2 * m + 2, :], two(g[:, 0, :]), two(g[:, 1, :]), ALU.add).then_inc(merge_step, 1)
                    pool.wait_ge(merge_step, m + 1)
                    wait_evacuated(pool, f"yc{m}")
                    nc.gpsimd.tensor_tensor(merged[:, 2 * m:2 * m + 2, :], merged[:, 2 * m:2 * m + 2, :], two(g[:, 2, :]), ALU.add).then_inc(merged_ready, 1)
                power("ffn")
                pool.wait_ge(stat_ready, after(NORMS, "ffn"))
                nc.gpsimd.memset(xs[:, :, PAIRS:SLOTS], 0.0).then_inc(xs_pad, 1)

                def experts(per):
                    def window(it, k, first, ending):
                        if ending:
                            return
                        w, b = window_of(it, k, per), k % 2
                        at = pool.value_load(starts[0:1, bass.ds(expert_of(it, k, per) + k % per * NE, 1)], min_val=0, max_val=PAIRS)
                        if k >= 2:
                            pool.wait_ge(piece_used, PIECES * (w - 1))
                        nc.gpsimd.tensor_copy(xsplit[:, b, :, 0:WIN], xs[:, :, bass.ds(at, WIN)]).then_inc(xw_high, 1)
                        pool.wait_ge(xw_high, w + 1)
                        pool.sem_inc(wait_carried, 1)
                        nc.gpsimd.tensor_tensor(xsplit[:, b, :, WIN:2 * WIN], xs[:, :, bass.ds(at, WIN)],
                                                xsplit[:, b, :, 0:WIN].bitcast(F32), ALU.subtract).then_inc(xw_ready, 1)

                    windows_of(pool, per, window)

                pool.wait_ge(xs_read[0], 4)
                pool.wait_ge(xs_read[1], 4)
                pool.wait_ge(xs_pad, 1)
                pool.wait_ge(gw_ready, 2)
                pool.wait_ge(starts_ready, 2)
                most_pool = pool.value_load(most[0:1, 0:1], min_val=0, max_val=S)
                with pool.If(most_pool > windows):
                    experts(WIDE)
                with pool.Else():
                    experts(1)
                power("ple")
                for m in range(4):
                    pool.wait_ge(pmul_ready, m + 1)
                    x2 = xT[:, 2 * m:2 * m + 2, :]
                    if m == 0:
                        pool.wait_ge(h_ready, 3 * DC)
                        pool.wait_ge(sq_ready, len(SQUARES))
                    nc.gpsimd.tensor_tensor(x2, x2, two(ple_t[m % 2]), ALU.add).then_inc(merge_step, 1)
                pool.wait_ge(merge_step, 8)
                pool.wait_ge(engines_done, 3)
                pool.sem_clear(range(zeroed[0].num, zeroed[-1].num + 1))
                pool.sem_inc(layer_over, 1)
            power("mix")

        @block.vector
        def _(dve):
            TT, TS, STT = nc.vector.tensor_tensor, nc.vector.tensor_scalar, nc.vector.scalar_tensor_tensor
            for i in range(2):
                dve.wait_ge(x_tr, 2 * i + 2)
                nc.vector.tensor_copy(xT[:, 4 * i + 2:4 * i + 4, :], ps[:, 2 * i + 1, :]).then_inc(x_in, 1)

            rows = slice(NOPE, QK)
            n_rope = [0]

            def rstep(ins):
                n_rope[0] += 1
                ins.then_inc(rope_step, 1)
                dve.wait_ge(rope_step, n_rope[0])

            dve.wait_ge(init_loaded, 48)
            a0, a1, a2 = (ang[rows, i, :] for i in (1, 3, 2))
            A = ang[rows, 0, :]
            rstep(nc.vector.tensor_copy(a0, A.bitcast(I32)))
            rstep(TS(a0, a0, freq, None, ALU.mult))
            rstep(TS(a1, a0, INV_2PI, ROUND, ALU.mult, ALU.add))
            rstep(TS(a1, a1, ROUND, None, ALU.subtract))
            rstep(STT(a0, a1, -TWO_PI[0], a0, ALU.mult, ALU.add))
            rstep(STT(a0, a1, -TWO_PI[1], a0, ALU.mult, ALU.add))
            rstep(STT(a0, a1, -TWO_PI[2], a0, ALU.mult, ALU.add))
            rstep(TS(A, a0, PI_IN, -PI_IN, ALU.min, ALU.max))
            rstep(STT(a2, A, -1.0, A, ALU.mult, ALU.min))
            rstep(TS(a2, a2, HALF_PI, None, ALU.add))

            def mean(name, n):
                i = NORMS.index(name)
                dve.wait_ge(stat_ready, after(NORMS, name))
                if name == "lnm":
                    TS(col[:, i, 1, :], ps[:, 3, 0:TC], 1.0 / n, None, ALU.mult).then_inc(mean_ready, 1)
                else:
                    TS(col[:, i, 0, :], ps[:, 3, 0:TC], 1.0 / n, EPS, ALU.mult, ALU.add).then_inc(ms_ready, 1)

            def diagonal(name):
                i = NORMS.index(name)
                if name == "lnm":
                    dve.wait_ge(mean_ready, 1)
                else:
                    dve.wait_ge(pow_ready, after(POWS, name))
                TS(diag[:, 0, :], ident, col[:, i, 1, 0:1], None, ALU.mult)
                TS(diag[:, 1, :], ident, col[:, i, 1, 1:2], None, ALU.mult).then_inc(diag_ready, 1)

            def take_row(name, dst):
                dve.wait_ge(bcast_ready, after(NORMS, name))
                nc.vector.tensor_copy(dst[:, :], ps[:, 3, S:2 * S]).then_inc(bcast_used, 1)
                dve.wait_ge(bcast_used, after(NORMS, name))

            def low(it, k, q, per):
                s = k // per % ERING
                dve.wait_ge(piece_high, PIECES * window_of(it, k, per) + q + 1)
                ins = TT(wsplit[:, q % 2, 1, :, :], gu_ring[:, s, :, q * KP * FH:(q + 1) * KP * FH],
                         wsplit[:, q % 2, 0, :, :].bitcast(F32), ALU.subtract)
                if q < PIECES - 1:
                    ins.then_inc(piece_low, 1)
                else:
                    ins.then_inc(gu_taken if k % per == per - 1 else wide_taken, 1)

            with dve.Fori(0, DEPTH) as l:
                begin(dve, l + 1)
                dve.wait_ge(x_in, 4)
                dve.wait_ge(vec_ready, 2)
                for c in range(DC):
                    TS(hT[:, c, :], xT[:, c, :], vcol("mix", c), None, ALU.mult).then_inc(h_ready, 1)

                def scale_out(name, dst, n=2):
                    wait_unit(dve, l, name)
                    evacuates(TT(dst, two(bank(name)), bc2(), ALU.mult), name)

                mean("mix", D)
                diagonal("mix")
                take_row("mix", bc)
                scale_out("kv", two(tmp[:, 0, :]))
                wait_unit(dve, l, "kr")
                evacuates(TT(kr[0:QK, 0, :], bank("kr")[0:QK, 0:S], bc[0:QK, :], ALU.mult), "kr")
                scale_out("q0", qn[:, 0:2, :])
                scale_out("q1", qn[:, 2:4, :])
                mean("kv", KVL)
                scale_out("q2", qn[:, 4:6, :])
                diagonal("kv")
                take_row("kv", bcs)
                for c in range(2):
                    STT(kvn[:, c, :], two(tmp[:, 0, :])[:, c, :], vcol("kv", c), bcs[:, :], ALU.mult, ALU.mult).then_inc(kvn_ready, 1)
                wait_unit(dve, l, "rotk")
                dve.wait_ge(rope_sin, 2)
                evacuates(TT(kr[NOPE:QK, 1, :], bank("rotk")[NOPE:QK, 0:S], sinT[NOPE:QK, :], ALU.mult), "rotk")
                mean("q", QL)
                diagonal("q")
                take_row("q", bcs)
                for c in range(6):
                    STT(qn[:, c, :], qn[:, c, :], vcol("q", c), bcs[:, :], ALU.mult, ALU.mult).then_inc(qn_ready, 1)

                def rotated(i):
                    wait_unit(dve, l, f"rot{i}")
                    if i >= 2:
                        dve.wait_ge(q_ready, i - 1)
                    evacuates(TT(rtmp[NOPE:QK, i % 2, :, :], two(bank(f"rot{i}"))[NOPE:QK, :, :],
                                 sinT[NOPE:QK, :].unsqueeze(1).to_broadcast([ROPE, 2, S]), ALU.mult), f"rot{i}")

                rotated(0)
                rotated(1)
                rotated(2)
                scale_out("gg0", two(glu_t[0][:, 0, :]))
                rotated(3)
                scale_out("gv0", two(glu_t[0][:, 1, :]))
                scale_out("gg1", two(glu_t[1][:, 0, :]))
                scale_out("gv1", two(glu_t[1][:, 1, :]))

                def maximum(h):
                    dve.wait_ge(score_ready, h + 1)
                    if h >= 2:
                        dve.wait_ge(probs_ready, 2 * (h - 1))
                    b = 4 + h % 2
                    edge = two(ps[:, b, :])[:, :, 0:P]
                    TT(edge, edge, causal.unsqueeze(1).to_broadcast([P, 2, P]), ALU.add).then_inc(mask_step, 1)
                    dve.wait_ge(mask_step, 2 * h + 1)
                    nc.vector.reduce_max(mx[:, h % 2, 0, 0:1], ps[:, b, 0:P], AX.X)
                    nc.vector.reduce_max(mx[:, h % 2, 1, 0:1], ps[:, b, P:3 * P], AX.X).then_inc(mask_step, 1)
                    dve.wait_ge(mask_step, 2 * h + 2)
                    TS(mx[:, h % 2, :, 1], mx[:, h % 2, :, 0], -SCALE, None, ALU.mult).then_inc(max_ready, 1)

                taps = [(k, c) for k in range(KC) for c in range(SCC)]

                def conv_taps(first, count):
                    for n in range(first, min(first + count, len(taps))):
                        k, c = taps[n]
                        w = convT[:, k * SCC + c:k * SCC + c + 1]
                        if k == 0:
                            TS(conv[:, c, :], upad[:, c, 0:S], w, None, ALU.mult).then_inc(conv_step, 1)
                        else:
                            dve.wait_ge(conv_step, n - SCC + 1)
                            STT(conv[:, c, :], upad[:, c, k:k + S], w, conv[:, c, :], ALU.mult, ALU.add).then_inc(conv_step, 1)

                def short_conv(i):
                    dve.wait_ge(scu_ready, i + 1)
                    t = two(tmp[:, 1, :])
                    for j in range(2):
                        c = 2 * i + j
                        TS(t[:, j, :], scu[:, c, 0:S], vcol("ca", c), None, ALU.mult).then_inc(short_step, 1)
                    for k in range(1, KA):
                        for j in range(2):
                            c = 2 * i + j
                            dve.wait_ge(short_step, 6 * i + 2 * (k - 1) + j + 1)
                            STT(t[:, j, :], scu[:, c, k:k + S], vcol("ca", k * SCC + c), t[:, j, :], ALU.mult, ALU.add).then_inc(short_step, 1)
                    dve.wait_ge(short_step, 6 * (i + 1))
                    y2 = ya[:, 2 * i:2 * i + 2, :]
                    TT(y2, y2, t, ALU.mult).then_inc(ya_ready, 1)

                maximum(0)
                maximum(1)
                dve.wait_ge(u_ready, 2)
                dve.wait_ge(k_ready, 1)
                PER_HEAD = -(-len(taps) // HEADS)
                for h in range(HEADS):
                    dve.wait_ge(exp_ready, 2 * (h + 1))
                    nc.vector.reciprocal(mx[:, h % 2, :, 0], mx[:, h % 2, :, 2]).then_inc(recip_ready, 1)
                    conv_taps(PER_HEAD * h, PER_HEAD)
                    if h + 2 < HEADS:
                        maximum(h + 2)
                    if h < len(FILL):
                        kind, i = FILL[h][0], h // 3
                        if h == 0:
                            dve.wait_ge(pad_zero, 2)
                        if kind == "c":
                            scale_out(FILL[h], scu[:, 2 * i:2 * i + 2, KA - 1:])
                        if kind == "u":
                            if i:
                                dve.wait_ge(scu_ready, 1)
                            scale_out(FILL[h], two(tmp[:, 0, :]))
                        if kind == "b":
                            scale_out(FILL[h], ya[:, 2 * i:2 * i + 2, :])
                            wait_evacuated(dve, FILL[h])
                            short_conv(i)

                def gate_out(x, m):
                    if m == 0:
                        dve.wait_ge(pv_ready, HEADS)
                    if m >= 2:
                        dve.wait_ge(merged_ready, m - 1)
                    scale_out(f"g{x}{m}", two(gate_t[m % 2][:, "abc".index(x), :]))

                def gate_mul(x, m):
                    wait_unit(dve, l, f"y{x}{m}")
                    i = "abc".index(x)
                    dve.wait_ge(gate_sig, 3 * m + i + 1)
                    g = gate_t[m % 2][:, i, :]
                    evacuates(TT(g, g, bank(f"y{x}{m}"), ALU.mult), f"y{x}{m}")

                for m in range(4):
                    gate_out("a", m)
                    if m == 0:
                        mean("lnm", SC)
                        diagonal("lnm")
                    gate_out("b", m)
                    if m == 0:
                        take_row("lnm", bcs)
                        TT(conv, conv, bcs[:, :].unsqueeze(1).to_broadcast([P, SCC, S]), ALU.subtract).then_inc(xc_ready, 1)
                    gate_out("c", m)
                    gate_mul("a", m)
                    if m == 0:
                        mean("lnv", SC)
                    gate_mul("b", m)
                    if m == 0:
                        diagonal("lnv")
                        take_row("lnv", bcs)
                        for c in range(SCC):
                            STT(conv[:, c, :], conv[:, c, :], vcol("lng", c), bcs[:, :], ALU.mult, ALU.mult).then_inc(ln_step, 1)
                        for c in range(SCC):
                            dve.wait_ge(ln_sig, c + 1)
                            STT(conv[:, c, :], conv[:, c, :], vcol("lnb", c), sq_ln[:, c, :], ALU.add, ALU.mult).then_inc(yc_ready, 1)
                    gate_mul("c", m)

                def add_to_x(unit, m):
                    wait_unit(dve, l, unit)
                    x2 = xT[:, 2 * m:2 * m + 2, :]
                    evacuates(TT(x2, two(bank(unit)), x2, ALU.add), unit)

                for m in range(4):
                    add_to_x(f"wo{m}", m)
                mean("ffn", D)
                diagonal("ffn")
                take_row("ffn", bcs)
                for c in range(DC):
                    STT(hT[:, c, :], xT[:, c, :], vcol("ffn", c), bcs[:, :], ALU.mult, ALU.mult).then_inc(h_ready, 1)

                n_step = [0]

                def step(ins):
                    n_step[0] += 1
                    ins.then_inc(dve_step, 1)
                    dve.wait_ge(dve_step, n_step[0])

                def b3(t, n):
                    return t.to_broadcast([P, TC, n])

                def io(n):
                    return iota[:, 0:n].unsqueeze(1).to_broadcast([P, TC, n])

                def first_of_max(x, n, mxt, eq, val, mn, hot):
                    step(nc.vector.reduce_max(mxt, x, AX.X))
                    step(TT(eq, x, b3(mxt, n), ALU.is_equal))
                    step(STT(val, eq, -float(PAIRS), io(n), ALU.mult, ALU.add))
                    step(nc.vector.tensor_reduce(mn, val, AX.X, ALU.min))
                    return TT(hot, val, b3(mn, n), ALU.is_equal)

                wait_unit(dve, l, "lg")
                lgp = bank("lg")[:, 0:TC * (NG + NE)].rearrange("p (t n) -> p t n", t=TC)
                evacuates(TT(logit, lgp, b_rt[:, :, :], ALU.add), "lg")
                wait_evacuated(dve, "lg")
                for i in (1, 3):
                    dve.wait_ge(tok_psum, i + 1)
                    nc.vector.tensor_copy(h_tok[:, i // 2, (i % 2) * 512:(i % 2 + 1) * 512], ps[:, 4 + i, :]).then_inc(tok_read[1], 1)
                step(first_of_max(logit[:, :, 0:NG], NG, gmax, geq, gval, gmin, gone))
                step(TS(gpen, gone, BIG, -BIG, ALU.mult, ALU.add))
                for t in range(TC):
                    last = TT(masked[:, t, :].rearrange("p (g e) -> p g e", g=NG), logit[:, t, NG:].rearrange("p (g e) -> p g e", g=NG),
                              gpen[:, t, :].unsqueeze(2).to_broadcast([P, NG, EPG]), ALU.add)
                step(last)
                step(first_of_max(masked, NE, top[0], teq[0], tval[0], tmin[0], one[0]))
                step(STT(masked2, one[0], -3.0 * BIG, masked, ALU.mult, ALU.add))
                step(first_of_max(masked2, NE, top[1], teq[1], tval[1], tmin[1], one[1]))
                TT(chosen, one[0], one[1], ALU.add).then_inc(onehot_ready, 1)
                TT(expd[:, :, 0:NG], logit[:, :, 0:NG], b3(gmax, NG), ALU.subtract)
                TT(expd[:, :, NG:NG + 1], top[1], top[0], ALU.subtract).then_inc(top_diff, 1)
                for f in prefix:
                    nc.vector.memset(f[:, 0:16], 0.0)
                wait_unit(dve, l, "rank")
                evacuates(nc.vector.tensor_copy(ranks, bank("rank")[:, 0:3 * NE]), "rank")
                wait_evacuated(dve, "rank")
                count = ranks[:, 2 * NE:3 * NE]
                step(nc.vector.tensor_copy(prefix[0][:, 16:48], count))
                for i, sh in enumerate((1, 2, 4, 8, 16)):
                    a, b = prefix[i % 2], prefix[(i + 1) % 2]
                    step(TT(b[:, 16:48], a[:, 16:48], a[:, 16 - sh:48 - sh], ALU.add))
                upto = prefix[1][:, 16:48]
                step(TT(off, upto, count, ALU.subtract))
                step(TT(base, ranks[:, 0:2 * NE].rearrange("p (t n) -> p t n", t=TC), off.unsqueeze(1).to_broadcast([P, TC, NE]), ALU.add))
                TT(prod[0], base, one[0], ALU.mult)
                step(TT(prod[1], base, one[1], ALU.mult))
                nc.vector.reduce_sum(pos[0], prod[0], AX.X)
                step(nc.vector.reduce_sum(pos[1], prod[1], AX.X))
                for t in range(TC):
                    step(TS(sel_t[:, t, :], iota, pos[0][:, t, :], None, ALU.is_equal))
                    STT(sel[:, t, :], iota, pos[1][:, t, :], sel_t[:, t, :], ALU.is_equal, ALU.add).then_inc(sel_ready, 1)
                for j in range(WIDE):
                    last = STT(starts[0:1, j * NE:(j + 1) * NE], off[0:1, :], float(j * WIN), upto[0:1, :], ALU.add, ALU.min)
                last.then_inc(starts_ready, 1)
                nc.vector.reduce_max(most[0:1, 0:1], count[0:1, :], AX.X).then_inc(starts_ready, 1)
                dve.wait_ge(top_exp, 1)
                nc.vector.reduce_sum(gsum, expd[:, :, 0:NG], AX.X)
                step(TS(dplus, expd[:, :, NG:NG + 1], 1.0, None, ALU.add))
                step(TT(gsum, gsum, dplus, ALU.mult))
                step(nc.vector.reciprocal(weight[0], gsum))
                step(TT(weight[1], weight[0], expd[:, :, NG:NG + 1], ALU.mult))
                dve.wait_ge(sel_ready, 2)
                for t in range(TC):
                    TS(gw[:, t, :], iota, pos[0][:, t, :], weight[0][:, t, :], ALU.is_equal, ALU.mult)
                    step(TS(sel_t[:, t, :], iota, pos[1][:, t, :], weight[1][:, t, :], ALU.is_equal, ALU.mult))
                    TT(gw[:, t, :], gw[:, t, :], sel_t[:, t, :], ALU.add).then_inc(gw_ready, 1)
                for c in range(1, DC, 2):
                    dve.wait_ge(gather_psum, c + 1)
                    nc.vector.tensor_copy(xs[:, c, 0:PAIRS], ps[:, 4 + c % 4, :]).then_inc(xs_read[1], 1)

                def experts(per):
                    def sum_up(it, k):
                        dve.wait_ge(low_ready, window_of(it, k, per) + 1)
                        TT(gu, ps[0:WIN, k % 2, :], gu_low, ALU.add).then_inc(gu_summed, 1)

                    def hidden(it, k):
                        w = window_of(it, k, per)
                        dve.wait_ge(sg_ready, w + 1)
                        TT(hh, sg, gu[:, 0:FH], ALU.mult).then_inc(hh_part, 1)
                        dve.wait_ge(hh_part, w + 1)
                        TT(hh, hh, gu[:, FH:2 * FH], ALU.mult).then_inc(hh_ready, 1)

                    def take_hidden(it, k):
                        dve.wait_ge(hh_tr, window_of(it, k, per) + 1)
                        nc.vector.tensor_copy(hhT[:, k % 2, :], ps[:, 4 + k % 2, 0:2 * WIN]).then_inc(hhT_ready, 1)

                    def take_rows(it, k):
                        wait_down(dve, l, it, k, per)
                        nc.vector.tensor_copy(yrow[:, 512:1024], ps[0:WIN, 7, :]).then_inc(yrow_ready[1], 1)

                    def step(it, k, first, ending):
                        one_before = k >= 1 and k <= (PEEL + BODY) * per
                        two_before = k >= 2
                        if not ending and k > 0:
                            low(it, k, 0, per)
                        if one_before:
                            sum_up(it, k - 1)
                        if not ending and k > 0:
                            low(it, k, 1, per)
                        if one_before:
                            hidden(it, k - 1)
                        if not ending:
                            low(it, k, 2, per)
                        if two_before:
                            take_rows(it, k - 2)
                        if one_before:
                            take_hidden(it, k - 1)
                        if not ending:
                            low(it, k, 3, per)

                    windows_of(dve, per, step)

                for q in range(2):
                    low(0, 0, q, 1)
                dve.wait_ge(starts_ready, 2)
                most_dve = dve.value_load(most[0:1, 0:1], min_val=0, max_val=S)
                with dve.If(most_dve > windows):
                    experts(WIDE)
                with dve.Else():
                    experts(1)
                for t in range(TC):
                    dve.wait_ge(gwT_psum, t + 1)
                    nc.vector.tensor_copy(gwT[:, :, t * P:(t + 1) * P], ps[:, 4 + t, :].rearrange("p (s n) -> p s n", s=4)).then_inc(gwT_ready, 1)
                for i in (1, 3, 5, 7):
                    dve.wait_ge(ytok_psum, i + 1)
                    nc.vector.tensor_copy(y_tok[:, i // 2, 512:1024], ps[:, 7, :]).then_inc(ytok_read[1], 1)
                for m in range(4):
                    add_to_x(f"cb{m}", m)
                    wait_evacuated(dve, f"cb{m}")
                    for c in (2 * m, 2 * m + 1):
                        TS(hT[:, c, :], xT[:, c, :], vcol("ple", c), None, ALU.mult).then_inc(h_ready, 1)
                mean("ple", D)
                diagonal("ple")
                take_row("ple", bc)

                def ple_mul(m):
                    dve.wait_ge(psig_ready, m + 1)
                    wait_evacuated(dve, f"pp{m}")
                    TT(ple_t[m % 2], ple_t[m % 2], ppt[m % 2], ALU.mult).then_inc(pmul_ready, 1)

                for m in range(4):
                    if m >= 2:
                        dve.wait_ge(merge_step, 4 + m - 1)
                    scale_out(f"pg{m}", two(ple_t[m % 2]))
                    if m >= 1:
                        ple_mul(m - 1)
                ple_mul(3)
                nc.vector.tensor_copy(last_dve[:, :], ones[:, 0:1]).then_inc(engines_done, 1)
            begin(dve, DEPTH + 1)
            mean("mix", D)
            dve.wait_ge(pow_ready, 1)
            dve.wait_ge(init_loaded, 64)
            for t in range(TC):
                for half in range(2):
                    dve.wait_ge(tok_psum, 2 * t + half + 1)
                    last = STT(xout[:, t, half * 512:(half + 1) * 512], ps[:, 4 + 2 * t + half, :], col[:, 0, 1, t:t + 1],
                               gfull[:, half * 512:(half + 1) * 512], ALU.mult, ALU.mult)
                last.then_inc(pmul_ready, 1)


_INS = ["x", "p", "positions", "ln_mix_g", "w_in", "conv_a_w", "w_out_a", "q_norm_g", "w_uq", "kv_norm_g", "w_ukv",
        "w_out_b", "conv_c_w", "ln_c_g", "ln_c_b", "w_out_c", "w_o", "ln_ffn_g", "w_route_grp", "b_route_grp",
        "w_route_exp", "b_route_exp", "w_exp_gate", "w_exp_up", "w_exp_down", "ln_ple_g", "w_ple_gate", "w_ple",
        "final_norm_g"]


def constants():
    import numpy as np
    c = np.zeros((P, C_COLS), np.float32)
    c[:, C_ID:C_ID + P] = np.eye(P)
    c[:, C_UP:C_UP + P] = np.triu(np.ones((P, P)), 1)
    c[:, C_CAUSAL:C_CAUSAL + P] = np.where(np.tril(np.ones((P, P))) > 0, 0.0, -BIG)
    half = ROPE // 2
    for i in range(half):
        c[NOPE + half + i, C_ROT + NOPE + i] = -1.0
        c[NOPE + i, C_ROT + NOPE + half + i] = 1.0
        f = np.float32(10000.0) ** np.float32(-2.0 * i / ROPE)
        c[NOPE + i, C_FREQ] = c[NOPE + half + i, C_FREQ] = f
    c[:, C_IOTA:C_IOTA + PAIRS] = np.arange(PAIRS)
    return c


def kernel(**inputs):
    import numpy as _np
    import concourse.bacc as _bacc
    from concourse import mybir as _mybir
    from concourse.bass_utils import run_bass_kernel_spmd as _run

    nc = _bacc.Bacc("TRN2", target_bir_lowering=False, num_devices=1)
    arrays, args = {}, []
    for name in _INS:
        a = _np.ascontiguousarray(inputs[name])
        arrays[f"in_{name}_dram"] = a
        args.append(nc.dram_tensor(f"in_{name}_dram", a.shape, _mybir.dt.from_np(a.dtype), kind="ExternalInput").ap())
    c = constants()
    arrays["in_consts_dram"] = c
    args.append(nc.dram_tensor("in_consts_dram", c.shape, _mybir.dt.float32, kind="ExternalInput").ap())
    args.append(nc.dram_tensor("out_0_dram", (1, S, D), _mybir.dt.float32, kind="ExternalOutput").ap())
    program(nc, *args)
    r = _run(nc, [arrays], core_ids=[0])
    return r.results[0]["out_0_dram"]
```

```python
import concourse.bass as bass
from concourse import mybir
from contextlib import ExitStack

F32 = mybir.dt.float32
F32R = mybir.dt.float32r
I32 = mybir.dt.int32
ALU = mybir.AluOpType
ACT = mybir.ActivationFunctionType
AX = mybir.AxisListType

P = 128
DEPTH, S, D = 2, 256, 1024
DC, TC = D // P, S // P
SC, SCC = 512, 4
KA, KC = 3, 31
HEADS, NOPE, ROPE, VH = 8, 64, 32, 64
QK = NOPE + ROPE
QL, KVL = 768, 256
NG, EPG, NE, FH = 4, 8, 32, 256
PAIRS = 2 * S
WIN = 64
WIDE = S // WIN
SLOTS = PAIRS + WIN
ERING = 3
PIECES, KP = 4, 2
BODY = 2 * ERING
PEEL = NE % BODY
EPS = 1e-6
SCALE = float(QK) ** -0.5
BIG = 1e30
OFF_SC = 3 * D
OFF_Q = OFF_SC + 3 * SC
OFF_KV = OFF_Q + QL
OFF_KR = OFF_KV + KVL
OFF_GV = OFF_KR + ROPE
OFF_GG = OFF_GV + SC
INV_2PI = 0.15915494309189535
ROUND = 1.5 * 2.0 ** 23
TWO_PI = (6.28125, 0.001934051513671875, 1.255665914356996e-06)
PI_IN = 3.1415925
HALF_PI = 1.5707963267948966
ROPE_STEPS = 10

C_ID, C_UP, C_CAUSAL, C_ROT, C_FREQ, C_IOTA = 0, P, 2 * P, 3 * P, 3 * P + QK, 3 * P + QK + 1
C_COLS = C_IOTA + PAIRS

VEC = {}
_at = 0
for _name, _n in (("mix", DC), ("q", QL // P), ("kv", KVL // P), ("lng", SCC), ("lnb", SCC),
                  ("ffn", DC), ("ple", DC), ("ca", KA * SCC)):
    VEC[_name] = _at
    _at += _n
VROWS = _at
CROWS = KC * SCC

RING = 2
SLOT = 2048
CHUNKS = (["kv"] + [f"q{i}" for i in range(3)] + ["gg0", "gv0", "gg1", "gv1"] + ["ukv"]
          + [f"uq{i}" for i in range(4)] + ["c0", "u0", "b0", "c1", "u1", "b1"]
          + [f"{x}{m}" for m in range(4) for x in ("ga", "yab", "gb", "gc", "yc")]
          + [f"wo{m}" for m in range(4)] + ["pp"] + [f"pg{m}" for m in range(4)])
CI = {c: i for i, c in enumerate(CHUNKS)}
NC = len(CHUNKS)
assert NC % RING == 0

FILL = ["c0", "u0", "b0", "c1", "u1", "b1"]
UNITS = (["kv", "kr", "q0", "q1", "q2", "rotk", "gg0", "gv0", "gg1", "gv1", "kn0", "kn1", "kn2", "kn3",
          "v0", "v1", "uq0", "uq1", "rot0", "uq2", "rot1", "uq3", "rot2", "rot3"]
         + FILL
         + [f"{x}{m}" for m in range(4) for x in ("ga", "ya", "yb", "gb", "gc", "yc")]
         + [f"wo{m}" for m in range(4)] + ["lg", "rank"] + [f"cb{m}" for m in range(4)]
         + ["pp0", "pp1", "pp2", "pp3", "pg0", "pg1", "pg2", "pg3"])
UI = {u: i for i, u in enumerate(UNITS)}
NU = len(UNITS)
BANKS = 3
TAPS_BEFORE = [50, 13, 13]

SPLITS = (["kv", "q0", "q1", "q2", "gg0", "gv0", "gg1", "gv1"] + FILL + [f"g{x}{m}" for m in range(4) for x in "abc"]
          + [f"wo{m}" for m in range(4)] + [f"pg{m}" for m in range(4)])
SI = {u: i for i, u in enumerate(SPLITS)}
NTILES = 2 * len(SPLITS)
ROWS = ["mix", "wo", "ple"]


def chunk_of(unit):
    if unit in CI:
        return unit
    if unit[:2] == "kn" or unit in ("v0", "v1"):
        return "ukv"
    if unit[:2] in ("ya", "yb"):
        return "yab" + unit[2:]
    if unit[:2] == "pp":
        return "pp"
    return None


LAST_UNIT = {}
for _u in UNITS:
    if chunk_of(_u):
        LAST_UNIT[chunk_of(_u)] = UI[_u]

NORMS = ["mix", "kv", "q", "lnm", "lnv", "ffn", "ple"]
POWS = ["mix", "kv", "q", "lnv", "ffn", "ple"]
SQUARES = ([f"mix{i}" for i in range(4)] + ["kv", "q0", "q1", "q2", "lnv"]
           + [f"ffn{i}" for i in range(4)] + [f"ple{i}" for i in range(4)])


def after(events, name):
    return events.index(name) + 1


def program(nc, x, p, positions, ln_mix_g, w_in, conv_a_w, w_out_a, q_norm_g, w_uq, kv_norm_g, w_ukv,
            w_out_b, conv_c_w, ln_c_g, ln_c_b, w_out_c, w_o, ln_ffn_g, w_route_grp, b_route_grp,
            w_route_exp, b_route_exp, w_exp_gate, w_exp_up, w_exp_down, ln_ple_g, w_ple_gate, w_ple,
            final_norm_g, consts, out, windows=WIN):
    ctx = ExitStack()
    with ctx:
        def sb(name, shape, dt=F32):
            return ctx.enter_context(nc.sbuf_tensor(name, shape, dt))

        def sem(name):
            return ctx.enter_context(nc.semaphore(name))

        ring = sb("ring", [P, RING, SLOT])
        gu_ring = sb("gu_ring", [P, ERING, 2, SLOT])
        down_ring = sb("down_ring", [P, ERING, SLOT])
        wsplit = sb("wsplit", [P, 2, 2, 2, KP * FH], F32R)
        h_high = sb("h_high", [P, DC, S], F32R)
        h_low = sb("h_low", [P, DC, S], F32R)
        xT = sb("xT", [P, DC, S])
        hT = sb("hT", [P, DC, S])
        cst = sb("cst", [P, C_COLS])
        ones = sb("ones", [P, P])
        mhalf = sb("mhalf", [P, 2])
        last_act = sb("last_act", [P, 1])
        last_dve = sb("last_dve", [P, 1])
        cosT = sb("cosT", [QK, S])
        sinT = sb("sinT", [QK, S])
        bc = sb("bc", [P, S])
        bcs = sb("bcs", [P, S])
        diag = sb("diag", [P, 2, P])
        col = sb("col", [P, len(NORMS), 2, 2])
        vrow = sb("vrow", [VROWS, P])
        crow = sb("crow", [CROWS, P])
        vecT = sb("vecT", [P, VROWS])
        convT = sb("convT", [P, CROWS])
        w_rt = sb("w_rt", [P, DC, NG + NE])
        b_rt = sb("b_rt", [P, TC, NG + NE])
        w_kr = sb("w_kr", [P, DC, QK])
        prow = sb("prow", [P, TC, S])
        pT = sb("pT", [P, 2, S])
        starts = sb("starts", [1, WIDE * NE], I32)
        most = sb("most", [1, 1], I32)
        mx = sb("mx", [P, 2, 2, 3])
        work = sb("work", [P, 12928])
        ps = ctx.enter_context(nc.psum_tensor("ps", [P, 8, 512], F32))

        tile_split = wsplit[:, :, :, :, :].rearrange("p b s g (c n) -> p b s (g c) n", n=P)
        xsplit = h_low[:, :, :].rearrange("p (b c) n -> p b (c n)", b=2).rearrange("p b (c n) -> p b c n", n=2 * WIN)

        ident = cst[:, C_ID:C_ID + P]
        upper = cst[:, C_UP:C_UP + P]
        causal = cst[:, C_CAUSAL:C_CAUSAL + P]
        rot = cst[0:QK, C_ROT:C_ROT + QK]
        freq = cst[NOPE:QK, C_FREQ:C_FREQ + 1]
        iota = cst[:, C_IOTA:C_IOTA + PAIRS]

        def area(at, *dims):
            n = 1
            for d in dims:
                n *= d
            v = work[:, at:at + n]
            if len(dims) == 2:
                return v.rearrange("p (a b) -> p a b", a=dims[0])
            if len(dims) == 3:
                return v.rearrange("p (a b c) -> p a b c", a=dims[0], b=dims[1])
            return v

        qn = area(0, 6, S)
        kvn = area(1536, 2, S)
        scu = area(0, SCC, S + KA - 1)
        ya = area(1032, SCC, S)
        qT = area(2056, HEADS, S)
        sq_q = area(2056, 6, S)
        sq_kv = area(2056 + 1536, 2, S)
        merged = area(2056, DC, S)
        kT = area(4104, HEADS, S)
        sq_x = area(4104, DC, S)
        v = area(6152, TC, SC)
        attnT = area(7176, SCC, S)
        rtmp = area(7176, 2, 2, S)
        probs = area(8200, 2, 384)
        probsT = area(8200 + 768, 2, 384)
        upad = area(9736, SCC, S + KC - 1)
        conv = area(10880, SCC, S)
        kr = area(10880, 2, S)
        tmp = area(11904, 2, 512)
        sq_ln = area(11904, SCC, S)
        glu_t = [area(8200, 2, 512), area(11904, 2, 512)]
        gate_t = [area(8200, 3, 512), area(4104, 3, 512)]
        ys = area(0, DC, SLOTS)
        h_tok = [h[:, :, :].rearrange("p c n -> p (c n)").rearrange("p (t d) -> p t d", t=TC) for h in (h_high, h_low)]
        sel = wsplit[:, 1, 0, :, :]
        sel_t = area(3072, TC, PAIRS)
        xs = area(4608, DC, SLOTS)
        gw = area(9216, TC, PAIRS)
        hhT = area(11264, 2, 2 * WIN)
        hflat = hT[0:WIN, :, :].rearrange("p c n -> p (c n)")
        yrow = hflat[:, 0:D]
        gu = hflat[:, D:D + 2 * FH]
        sg = hflat[:, D + 2 * FH:D + 3 * FH]
        hh = hflat[:, D + 3 * FH:D + 4 * FH]
        gu_low = pT[0:WIN, :, :].rearrange("p a n -> p (a n)")
        y_tok = area(4608, 4, D)
        gwT = area(11776, 4, S)
        route_at = [10240]

        def rt(n):
            route_at[0] += 2 * n
            assert route_at[0] <= 12928
            return area(route_at[0] - 2 * n, 2, n)

        logit, gmax, geq, gval, gmin, gone, gpen = rt(NG + NE), rt(1), rt(NG), rt(NG), rt(1), rt(NG), rt(NG)
        masked, masked2 = rt(NE), rt(NE)
        top, teq, tval, tmin = [rt(1), rt(1)], [rt(NE), rt(NE)], [rt(NE), rt(NE)], [rt(1), rt(1)]
        one = [rt(NE), rt(NE)]
        chosen = rt(NE)
        expd, gsum, dplus, weight = rt(NG + 1), rt(1), rt(1), [rt(1), rt(1)]
        ranks = area(route_at[0], 3 * NE)
        route_at[0] += 3 * NE
        prefix = [rt(24), rt(24)]
        prefix = [f.rearrange("p a b -> p (a b)") for f in prefix]
        base, prod, pos = rt(NE), [rt(NE), rt(NE)], [rt(1), rt(1)]
        off = rt(NE // 2).rearrange("p a b -> p (a b)")
        sq_p = area(0, DC, S)
        ple_t = [area(2048, 512), area(2560, 512)]
        ppt = [area(3072, 512), area(3584, 512), area(9216, 512), area(9728, 512)]
        xin = area(0, TC, D)
        gfull = area(8192, D)
        xout = area(9216, TC, D)
        ang = area(8192, 4, S)

        init_loaded = sem("init_loaded")
        small_loaded = sem("small_loaded")
        route_loaded = sem("route_loaded")
        wait_carried = sem("wait_carried")
        chunk_loaded = [sem(f"chunk_loaded{i}") for i in range(RING)]
        gu_loaded = [sem(f"gu_loaded{i}") for i in range(ERING)]
        down_loaded = [sem(f"down_loaded{i}") for i in range(ERING)]
        tile_low = sem("tile_low")
        unit_ready = sem("unit_ready")
        gu_taken = sem("gu_taken")
        down_ready = sem("down_ready")
        layer_over = sem("layer_over")
        x_tr = sem("x_tr")
        x_in = sem("x_in")
        rope_step = sem("rope_step")
        rope_sin = sem("rope_sin")
        const_set = sem("const_set")
        out_stored = sem("out_stored")
        zeroed = []

        def lsem(name):
            zeroed.append(sem(name))
            return zeroed[-1]

        evacuated = [lsem(f"evacuated{i}") for i in range(BANKS)]
        vec_tr = lsem("vec_tr")
        vec_ready = lsem("vec_ready")
        h_ready = lsem("h_ready")
        sq_ready = lsem("sq_ready")
        tile_high = lsem("tile_high")
        high_used = lsem("high_used")
        tile_used = lsem("tile_used")
        rows_high = lsem("rows_high")
        rows_low = lsem("rows_low")
        stat_ready = lsem("stat_ready")
        ms_ready = lsem("ms_ready")
        pow_ready = lsem("pow_ready")
        diag_ready = lsem("diag_ready")
        bcast_ready = lsem("bcast_ready")
        bcast_used = lsem("bcast_used")
        dve_step = lsem("dve_step")
        mean_ready = lsem("mean_ready")
        mask_step = lsem("mask_step")
        short_step = lsem("short_step")
        kvn_ready = lsem("kvn_ready")
        qn_ready = lsem("qn_ready")
        k_ready = lsem("k_ready")
        q_cos = lsem("q_cos")
        q_ready = lsem("q_ready")
        glu_sig = lsem("glu_sig")
        u_ready = lsem("u_ready")
        pad_zero = lsem("pad_zero")
        conv_step = lsem("conv_step")
        score_ready = lsem("score_ready")
        max_ready = lsem("max_ready")
        exp_ready = lsem("exp_ready")
        recip_ready = lsem("recip_ready")
        probs_ready = lsem("probs_ready")
        pT_psum = lsem("pT_psum")
        pT_ready = lsem("pT_ready")
        pv_ready = lsem("pv_ready")
        attn_ready = lsem("attn_ready")
        scu_ready = lsem("scu_ready")
        ya_ready = lsem("ya_ready")
        xc_ready = lsem("xc_ready")
        ln_step = lsem("ln_step")
        ln_sig = lsem("ln_sig")
        yc_ready = lsem("yc_ready")
        gate_sig = lsem("gate_sig")
        merge_step = lsem("merge_step")
        merged_ready = lsem("merged_ready")
        tok_psum = lsem("tok_psum")
        tok_high = lsem("tok_high")
        tok_low = lsem("tok_low")
        onehot_ready = lsem("onehot_ready")
        top_diff = lsem("top_diff")
        top_exp = lsem("top_exp")
        sel_ready = lsem("sel_ready")
        gw_ready = lsem("gw_ready")
        starts_ready = lsem("starts_ready")
        gather_psum = lsem("gather_psum")
        xs_read = [lsem("xs_read_act"), lsem("xs_read_dve")]
        xs_pad = lsem("xs_pad")
        first_high = lsem("first_high")
        first_ready = lsem("first_ready")
        xw_high = lsem("xw_high")
        xw_ready = lsem("xw_ready")
        piece_high = lsem("piece_high")
        piece_low = lsem("piece_low")
        wide_taken = lsem("wide_taken")
        piece_used = lsem("piece_used")
        low_ready = lsem("low_ready")
        gu_summed = lsem("gu_summed")
        down_half = lsem("down_half")
        wide_down = lsem("wide_down")
        sg_ready = lsem("sg_ready")
        hh_part = lsem("hh_part")
        hh_ready = lsem("hh_ready")
        hh_tr = lsem("hh_tr")
        hhT_ready = lsem("hhT_ready")
        yrow_ready = [lsem("yrow_ready_act"), lsem("yrow_ready_dve")]
        yT_psum = lsem("yT_psum")
        ys_ready = lsem("ys_ready")
        gwT_psum = lsem("gwT_psum")
        gwT_ready = lsem("gwT_ready")
        ytok_psum = lsem("ytok_psum")
        ytok_read = [lsem("ytok_read_act"), lsem("ytok_read_dve")]
        pT_tr = lsem("pT_tr")
        p_ready = lsem("p_ready")
        psig_ready = lsem("psig_ready")
        pmul_ready = lsem("pmul_ready")
        engines_done = lsem("engines_done")

        def begin(eng, layers):
            eng.wait_ge(layer_over, layers)
            eng.sem_inc(wait_carried, 1)

        def unit_value(l, name):
            return NU * (l + 1) + UI[name] + 1

        def wait_unit(eng, l, name):
            eng.wait_ge(unit_ready, unit_value(l, name))

        def tile_value(l, name, m):
            return NTILES * (l + 1) + 2 * SI[name] + m + 1

        def wait_chunk(eng, l, name):
            n = CI[name]
            slot = n % RING
            upto = sum(2 if c[:3] == "yab" else 1 for c in CHUNKS[slot:n + 1:RING])
            whole = sum(2 if c[:3] == "yab" else 1 for c in CHUNKS[slot::RING])
            eng.wait_ge(chunk_loaded[slot], l * (16 * whole) + 16 * upto)

        def tile_of(name, m):
            return ring[:, CI[name] % RING, :].rearrange("p (k n) -> p k n", k=DC)[:, :, m * P:(m + 1) * P]

        def bank(name):
            return ps[:, UI[name] % BANKS, :]

        def wait_evacuated(eng, name):
            eng.wait_ge(evacuated[UI[name] % BANKS], UI[name] // BANKS + 1)

        def evacuates(instruction, name):
            instruction.then_inc(evacuated[UI[name] % BANKS], 1)

        def two(ap):
            return ap.rearrange("p (a b) -> p a b", a=2)

        def bc2(n=2):
            return bc[:, :].unsqueeze(1).to_broadcast([P, n, S])

        def vcol(name, i):
            return vecT[:, VEC[name] + i:VEC[name] + i + 1]

        block = ctx.enter_context(nc.Block())

        @block.sync
        def _(sp):
            sp.dma_start(xin, x[0].rearrange("(t q) d -> q t d", q=P)).then_inc(init_loaded, 16)
            sp.dma_start(cst[:, :], consts[:, :]).then_inc(init_loaded, 16)
            sp.dma_start(ang[NOPE:QK, 0, :].bitcast(I32), positions[0].partition_broadcast(ROPE)).then_inc(init_loaded, 16)
            sp.sem_inc(unit_ready, NU)
            sp.sem_inc(tile_low, NTILES)
            sp.sem_inc(gu_taken, NE)
            sp.sem_inc(down_ready, NE)

            gate_flat = w_exp_gate.rearrange("l e d f -> (l e) d f")
            up_flat = w_exp_up.rearrange("l e d f -> (l e) d f")
            down_flat = w_exp_down.rearrange("l e f d -> (l e) f d")

            def cols(w, at, n):
                return w[:, at:at + n].rearrange("(c q) n -> q c n", q=P)

            def source(l, name):
                kind, m = name.rstrip("0123456789"), name[len(name.rstrip("0123456789")):]
                m = int(m) if m else 0
                if kind in ("ga", "gb", "gc"):
                    return [cols(w_in[l], "abc".index(kind[1]) * D + 256 * m, 256)]
                if kind in ("b", "c", "u"):
                    return [cols(w_in[l], OFF_SC + "bcu".index(kind) * SC + 256 * m, 256)]
                if kind == "q":
                    return [cols(w_in[l], OFF_Q + 256 * m, 256)]
                if kind == "kv":
                    return [cols(w_in[l], OFF_KV, 256)]
                if kind == "gv":
                    return [cols(w_in[l], OFF_GV + 256 * m, 256)]
                if kind == "gg":
                    return [cols(w_in[l], OFF_GG + 256 * m, 256)]
                if kind == "ukv":
                    return [cols(w_ukv[l], 0, HEADS * (NOPE + VH))]
                if kind == "uq":
                    return [cols(w_uq[l], 2 * QK * m, 2 * QK)]
                if kind == "yab":
                    return [cols(w_out_a[l], 256 * m, 256), cols(w_out_b[l], 256 * m, 256)]
                if kind == "yc":
                    return [cols(w_out_c[l], 256 * m, 256)]
                if kind == "wo":
                    return [cols(w_o[l], 256 * m, 256)]
                if kind == "pp":
                    return [cols(w_ple[l], 0, D)]
                return [cols(w_ple_gate[l], 256 * m, 256)]

            def load_chunk(l, name):
                n = CI[name]
                before = CHUNKS[n - RING]
                of_layer = l + 1 if n >= RING else l
                if before in SI:
                    sp.wait_ge(tile_low, NTILES * of_layer + 2 * SI[before] + 2)
                else:
                    sp.wait_ge(unit_ready, NU * of_layer + LAST_UNIT[before] + 1)
                sp.sem_inc(wait_carried, 1)
                at = 0
                parts = source(l, name)
                for i, src in enumerate(parts):
                    k, w = src.shape[1], src.shape[2]
                    dst = ring[:, n % RING, at:at + k * w].rearrange("p (k n) -> p k n", k=k)
                    at += k * w
                    sp.dma_start(dst, src).then_inc(chunk_loaded[n % RING], 16)

            def load_gate_up(l, e, s):
                sp.wait_ge(gu_taken, NE * (l + 1) + e - ERING + 1)
                sp.dma_start(gu_ring[:, s, 0, :], gate_flat[l * NE + e].rearrange("(q c) f -> q (c f)", q=P)).then_inc(gu_loaded[s], 16)
                sp.dma_start(gu_ring[:, s, 1, :], up_flat[l * NE + e].rearrange("(q c) f -> q (c f)", q=P)).then_inc(gu_loaded[s], 16)

            def load_down(l, e, s):
                sp.wait_ge(down_ready, NE * (l + 1) + e - ERING + 1)
                sp.dma_start(down_ring[:, s, :].rearrange("p (c d) -> p c d", c=2),
                             down_flat[l * NE + e].rearrange("(c q) d -> q c d", q=P)).then_inc(down_loaded[s], 16)

            with sp.Fori(0, DEPTH) as l:
                load_chunk(l, CHUNKS[0])
                sp.wait_ge(unit_ready, NU * l + UI["pp0"] + 1)
                sp.sem_inc(wait_carried, 1)
                for name, w in (("mix", ln_mix_g), ("q", q_norm_g), ("kv", kv_norm_g), ("lng", ln_c_g),
                                ("lnb", ln_c_b), ("ffn", ln_ffn_g), ("ple", ln_ple_g)):
                    n = w.shape[1] // P
                    sp.dma_start(vrow[VEC[name]:VEC[name] + n, :], w[l].rearrange("(c q) -> c q", q=P)).then_inc(small_loaded, 16)
                sp.dma_start(vrow[VEC["ca"]:VEC["ca"] + KA * SCC, :], conv_a_w[l].rearrange("k (c q) -> (k c) q", q=P)).then_inc(small_loaded, 16)
                sp.dma_start(crow[:, :], conv_c_w[l].rearrange("k (c q) -> (k c) q", q=P)).then_inc(small_loaded, 16)
                sp.dma_start(w_kr[:, :, :], cols(w_in[l], OFF_KR - NOPE, QK)).then_inc(small_loaded, 16)
                for c in CHUNKS[1:4]:
                    load_chunk(l, c)
                sp.dma_start(w_rt[:, :, 0:NG], cols(w_route_grp[l], 0, NG)).then_inc(route_loaded, 16)
                sp.dma_start(w_rt[:, :, NG:NG + NE], cols(w_route_exp[l], 0, NE)).then_inc(route_loaded, 16)
                for t in range(TC):
                    sp.dma_start(b_rt[:, t, 0:NG], b_route_grp[l].partition_broadcast(P)).then_inc(route_loaded, 16)
                    sp.dma_start(b_rt[:, t, NG:NG + NE], b_route_exp[l].partition_broadcast(P)).then_inc(route_loaded, 16)
                sp.dma_start(prow[:, :, :], p[l, 0].rearrange("(t q) d -> q t d", q=P)).then_inc(route_loaded, 16)
                for c in CHUNKS[4:16]:
                    load_chunk(l, c)
                for s in range(ERING):
                    load_gate_up(l, s, s)
                    load_down(l, s, s)
                    load_chunk(l, CHUNKS[16 + s])
                for c in CHUNKS[16 + ERING:CI["wo3"] + RING]:
                    load_chunk(l, c)
                load_gate_up(l, ERING, 0)
                with sp.Fori(0, (NE - ERING) // ERING) as it:
                    for i in range(ERING, 2 * ERING):
                        load_gate_up(l, it * ERING + i + 1, (i + 1) % ERING)
                        load_down(l, it * ERING + i, i % ERING)
                for e in range(NE - (NE - ERING) % ERING, NE):
                    if e + 1 < NE:
                        load_gate_up(l, e + 1, (e + 1) % ERING)
                    load_down(l, e, e % ERING)
                for c in CHUNKS[CI["wo3"] + RING:]:
                    load_chunk(l, c)
            sp.wait_ge(layer_over, DEPTH + 1)
            sp.dma_start(gfull, final_norm_g.partition_broadcast(P)).then_inc(init_loaded, 16)
            for t in range(TC):
                sp.wait_ge(pmul_ready, t + 1)
                sp.dma_start(out[0, t * P:(t + 1) * P, :], xout[:, t, :]).then_inc(out_stored, 16)
            sp.wait_ge(out_stored, 16 * TC)

        SMALL = 10
        ROUTES = 2 + 2 * TC + 1

        def wait_last_ys(eng, most_reg, windows, ys_sem):
            with eng.If(most_reg > windows):
                eng.wait_ge(ys_sem, WIDE * NE)
            with eng.Else():
                eng.wait_ge(ys_sem, NE)

        def expert_of(it, k, per):
            return it * BODY + k // per

        def window_of(it, k, per):
            return it * (BODY * per) + k

        def windows_of(eng, per, step):
            for k in range(PEEL * per):
                step(0, k, True, False)
            with eng.Fori(0, NE // BODY) as it:
                for k in range(PEEL * per, (PEEL + BODY) * per):
                    step(it, k, False, False)
            for k in range((PEEL + BODY) * per, (PEEL + BODY) * per + 2):
                step(NE // BODY - 1, k, False, True)

        def loads_of(l, it, k, per, each):
            e = k // per
            of_layer = len(range(e % ERING, NE, ERING))
            return l * (each * of_layer) + it * (each * BODY // ERING) + each * (e // ERING + 1)

        def wait_down(eng, l, it, k, per):
            if k % per == per - 1:
                eng.wait_ge(down_ready, NE * (l + 1) + expert_of(it, k, per) + 1)
            else:
                eng.wait_ge(wide_down, expert_of(it, k, per) * (per - 1) + k % per + 1)

        @block.tensor
        def _(pe):
            def mm(o, lhsT, rhs, first, last):
                return nc.tensor.matmul(o, lhsT, rhs, start=first, stop=last)

            def tr(o, i, n=P):
                return nc.tensor.transpose(o, i, ident[0:n, 0:n])

            pe.wait_ge(init_loaded, 48)
            for c in range(DC):
                for t in range(TC):
                    last = tr(ps[:, c // 2, (c % 2) * S + t * P:(c % 2) * S + (t + 1) * P], xin[:, t, c * P:(c + 1) * P])
                if c % 2:
                    last.then_inc(x_tr, 1)

            def stat(name, tiles, squares):
                n = len(tiles)
                if name != NORMS[0]:
                    pe.wait_ge(bcast_used, after(NORMS, name) - 1)
                for t in range(TC):
                    for c in range(n):
                        if t == 0 and squares[c] is not None:
                            pe.wait_ge(*squares[c])
                        last = mm(ps[:, 3, t:t + 1], tiles[c][:, t * P:(t + 1) * P], ones[:, 0:1], c == 0, c == n - 1)
                last.then_inc(stat_ready, 1)

            def bcast(name):
                pe.wait_ge(diag_ready, after(NORMS, name))
                for t in range(TC):
                    last = mm(ps[:, 3, S + t * P:S + (t + 1) * P], ones[:, :], diag[:, t, :], True, True)
                last.then_inc(bcast_ready, 1)

            def sq_events(name, n):
                return [(sq_ready, after(SQUARES, f"{name}{c // 2}")) for c in range(n)]

            with pe.Fori(0, DEPTH) as l:
                begin(pe, l + 1)

                def free_bank(name):
                    if UI[name] >= BANKS:
                        wait_evacuated(pe, UNITS[UI[name] - BANKS])

                def project(name, rhs, k, waits=(), at=0, width=256):
                    wait_chunk(pe, l, chunk_of(name))
                    free_bank(name)
                    w = ring[:, CI[chunk_of(name)] % RING, at:at + k * width].rearrange("p (k n) -> p k n", k=k)
                    for m in range(2):
                        for c in range(k):
                            if m == 0 and waits:
                                if waits[c] is not None:
                                    pe.wait_ge(*waits[c])
                            last = mm(two(bank(name))[:, m, :], w[:, c, m * P:(m + 1) * P], rhs[:, c, :], c == 0, c == k - 1)
                    last.then_inc(unit_ready, 1)

                def project_split(name, rows=None, late=0):
                    free_bank(name)
                    early = DC - late

                    def high_part(m, chunks):
                        pe.wait_ge(tile_high, 2 * SI[name] + m + 1)
                        for c in chunks:
                            if rows and m == 0:
                                pe.wait_ge(rows_low, DC // 2 * ROWS.index(rows) + c // 2 + 1)
                            mm(two(bank(name))[:, m, :], tile_split[:, m, 0, c, :], h_high[:, c, :], c == 0, False)
                            last = mm(two(bank(name))[:, m, :], tile_split[:, m, 0, c, :], h_low[:, c, :], False, False)
                        if c == DC - 1:
                            last.then_inc(high_used, 1)

                    def low_part(m, chunks):
                        pe.wait_ge(tile_low, tile_value(l, name, m))
                        for c in chunks:
                            last = mm(two(bank(name))[:, m, :], tile_split[:, m, 1, c, :], h_high[:, c, :], False, c == DC - 1)
                        if c == DC - 1:
                            last.then_inc(tile_used if m == 0 else unit_ready, 1)

                    for m in range(2):
                        if late and m == 0:
                            high_part(m, range(early))
                            low_part(m, range(early))
                            high_part(m, range(early, DC))
                            low_part(m, range(early, DC))
                        else:
                            high_part(m, range(DC))
                            low_part(m, range(DC))

                pe.wait_ge(small_loaded, l * (16 * SMALL) + 16 * SMALL)
                tr(ps[:, 6, 0:CROWS], crow[:, :], CROWS).then_inc(vec_tr, 1)
                tr(ps[:, 7, 0:VROWS], vrow[:, :], VROWS).then_inc(vec_tr, 1)
                stat("mix", [sq_x[:, c, :] for c in range(DC)], sq_events("mix", DC))
                project_split("kv", "mix")
                for c in range(DC):
                    last = mm(bank("kr")[0:QK, 0:S], w_kr[:, c, :], hT[:, c, :], c == 0, c == DC - 1)
                last.then_inc(unit_ready, 1)
                bcast("mix")
                project_split("q0")
                project_split("q1")
                stat("kv", [sq_kv[:, c, :] for c in range(2)], [(sq_ready, after(SQUARES, "kv"))] * 2)
                project_split("q2")
                bcast("kv")
                free_bank("rotk")
                wait_evacuated(pe, "kr")
                mm(bank("rotk")[0:QK, 0:S], rot, kr[0:QK, 0, :], True, True).then_inc(unit_ready, 1)
                project_split("gg0")
                stat("q", [sq_q[:, c, :] for c in range(6)], sq_events("q", 6))
                project_split("gv0")
                bcast("q")
                project_split("gg1")
                project_split("gv1")
                wait_chunk(pe, l, "ukv")
                ukv = ring[:, CI["ukv"] % RING, :].rearrange("p (k h n) -> p k h n", k=2, h=HEADS)
                pe.wait_ge(kvn_ready, 2)
                for i in range(4):
                    free_bank(f"kn{i}")
                    for j in range(2):
                        for c in range(2):
                            last = mm(two(bank(f"kn{i}"))[0:NOPE, j, :], ukv[:, c, 2 * i + j, 0:NOPE], kvn[:, c, :], c == 0, c == 1)
                    last.then_inc(unit_ready, 1)
                for t in range(TC):
                    free_bank(f"v{t}")
                    for c in range(2):
                        last = mm(bank(f"v{t}").rearrange("p (h n) -> p h n", h=HEADS), kvn[:, c, t * P:(t + 1) * P],
                                  ukv[:, c, :, NOPE:NOPE + VH], c == 0, c == 1)
                    last.then_inc(unit_ready, 1)

                def queries(i):
                    wait_chunk(pe, l, f"uq{i}")
                    free_bank(f"uq{i}")
                    w = ring[:, CI[f"uq{i}"] % RING, 0:6 * 2 * QK].rearrange("p (k n) -> p k n", k=6)
                    for j in range(2):
                        for c in range(6):
                            if i == 0 and j == 0:
                                pe.wait_ge(qn_ready, c + 1)
                            last = mm(two(bank(f"uq{i}"))[0:QK, j, :], w[:, c, j * QK:(j + 1) * QK], qn[:, c, :], c == 0, c == 5)
                    last.then_inc(unit_ready, 1)

                def rotate(i):
                    wait_evacuated(pe, f"uq{i}")
                    free_bank(f"rot{i}")
                    mm(bank(f"rot{i}")[0:QK, :], rot, qT[0:QK, 2 * i:2 * i + 2, :], True, True).then_inc(unit_ready, 1)

                def scores(h):
                    pe.wait_ge(q_ready, h // 2 + 1)
                    if h == 0:
                        pe.wait_ge(k_ready, 1)
                        for i in range(4):
                            wait_evacuated(pe, f"kn{i}")
                    if h >= 2:
                        pe.wait_ge(exp_ready, 2 * (h - 1))
                    mm(ps[:, 4 + h % 2, 0:P], qT[0:QK, h, 0:P], kT[0:QK, h, 0:P], True, True)
                    mm(ps[:, 4 + h % 2, P:3 * P], qT[0:QK, h, P:S], kT[0:QK, h, :], True, True).then_inc(score_ready, 1)

                queries(0)
                queries(1)
                rotate(0)
                queries(2)
                rotate(1)
                queries(3)
                scores(0)
                scores(1)
                rotate(2)
                rotate(3)

                def transpose_probs(h):
                    pe.wait_ge(probs_ready, 2 * (h + 1))
                    if h >= 1:
                        pe.wait_ge(pT_ready, h)
                    for i in range(3):
                        last = tr(ps[:, 6, i * P:(i + 1) * P], probs[:, h % 2, i * P:(i + 1) * P])
                    last.then_inc(pT_psum, 1)

                def weigh_values(h):
                    pe.wait_ge(pT_ready, h + 1)
                    if h == 0:
                        wait_evacuated(pe, "v0")
                        wait_evacuated(pe, "v1")
                    if h >= 1:
                        pe.wait_ge(attn_ready, h)
                    o = ps[:, 7, 0:S]
                    mm(o, v[:, 0, (h // 2) * P:(h // 2 + 1) * P], probsT[:, h % 2, 0:S], True, False)
                    mm(o[:, P:S], v[:, 1, (h // 2) * P:(h // 2 + 1) * P], probsT[:, h % 2, S:3 * P], False, True).then_inc(pv_ready, 1)

                project_split(FILL[0])
                for h in range(HEADS):
                    transpose_probs(h)
                    if h + 2 < HEADS:
                        scores(h + 2)
                    if 0 < h < len(FILL):
                        project_split(FILL[h])
                    weigh_values(h)

                for m in range(4):
                    project_split(f"ga{m}")
                    if m == 0:
                        stat("lnm", [conv[:, c, :] for c in range(SCC)], [(conv_step, KC * SCC)] + [None] * 3)
                        pe.wait_ge(ya_ready, 2)
                    project(f"ya{m}", ya, SCC)
                    if m == 0:
                        bcast("lnm")
                        pe.wait_ge(attn_ready, HEADS)
                    project(f"yb{m}", attnT, SCC, at=SLOT // 2)
                    if m == 0:
                        stat("lnv", [sq_ln[:, c, :] for c in range(SCC)], [(sq_ready, after(SQUARES, "lnv"))] + [None] * 3)
                    project_split(f"gb{m}")
                    if m == 0:
                        bcast("lnv")
                    project_split(f"gc{m}")
                    project(f"yc{m}", conv, SCC, [(yc_ready, c + 1) for c in range(SCC)])
                for m in range(4):
                    project_split(f"wo{m}", "wo" if m == 0 else None, late=2 if m == 0 else 0)

                stat("ffn", [sq_x[:, c, :] for c in range(DC)], sq_events("ffn", DC))
                bcast("ffn")
                free_bank("lg")
                pe.wait_ge(route_loaded, l * (16 * ROUTES) + 16 * ROUTES)
                lgp = bank("lg")[:, 0:TC * (NG + NE)].rearrange("p (t n) -> p t n", t=TC)
                for t in range(TC):
                    for c in range(DC):
                        if t == 0:
                            pe.wait_ge(h_ready, DC + c + 1)
                        last = mm(lgp[:, t, :], hT[:, c, t * P:(t + 1) * P], w_rt[:, c, :], c == 0, c == DC - 1)
                last.then_inc(unit_ready, 1)
                for i in range(4):
                    for j in range(4):
                        t, c = i // 2, (i % 2) * 4 + j
                        last = tr(ps[:, 4 + i, j * P:(j + 1) * P], hT[:, c, t * P:(t + 1) * P])
                    last.then_inc(tok_psum, 1)
                free_bank("rank")
                pe.wait_ge(onehot_ready, 1)
                a0, a1 = chosen[:, 0, :], chosen[:, 1, :]
                rk = bank("rank")
                mm(rk[:, 0:NE], upper, a0, True, True)
                mm(rk[:, NE:2 * NE], ones[:, :], a0, True, False)
                mm(rk[:, NE:2 * NE], upper, a1, False, True)
                mm(rk[:, 2 * NE:3 * NE], ones[:, :], a0, True, False)
                mm(rk[:, 2 * NE:3 * NE], ones[:, :], a1, False, True).then_inc(unit_ready, 1)
                pe.wait_ge(tok_low, 4)
                for c in range(DC):
                    for t in range(TC):
                        if c == 0:
                            pe.wait_ge(sel_ready, t + 1)
                        if t == 0 and c >= 4:
                            pe.wait_ge(xs_read[c % 2], (c - 4) // 2 + 1)
                        for part in range(2):
                            last = mm(ps[:, 4 + c % 4, :], h_tok[part][:, t, :].rearrange("p (q c) -> p c q", c=DC)[:, c, :],
                                      sel[:, t, :], t + part == 0, t + part == TC)
                    last.then_inc(gather_psum, 1)

                def experts(per):
                    def gate_up(it, k, q):
                        w, b = window_of(it, k, per), k % 2
                        if q == 0:
                            if k == 0:
                                pe.wait_ge(first_ready, 1)
                            else:
                                pe.wait_ge(xw_ready, w)
                        if q < PIECES - 1:
                            pe.wait_ge(piece_low, (PIECES - 1) * w + q + 1)
                        elif k % per == per - 1:
                            pe.wait_ge(gu_taken, NE * (l + 1) + expert_of(it, k, per) + 1)
                        else:
                            pe.wait_ge(wide_taken, expert_of(it, k, per) * (per - 1) + k % per + 1)
                        for c in range(KP):
                            for part in range(2):
                                last = mm(two(ps[:, b, :]), xsplit[:, b, KP * q + c, :], wsplit[:, q % 2, part, :, c * FH:(c + 1) * FH],
                                          q + c + part == 0, q == PIECES - 1 and c + part == KP)
                        last.then_inc(piece_used, 1)

                    def turn_hidden(it, k):
                        pe.wait_ge(hh_ready, window_of(it, k, per) + 1)
                        pe.sem_inc(wait_carried, 1)
                        for c in range(2):
                            last = tr(ps[:, 4 + k % 2, c * WIN:(c + 1) * WIN], hh[:, c * P:(c + 1) * P], WIN)
                        last.then_inc(hh_tr, 1)

                    def down(it, k, n):
                        half, c = n // 2, n % 2
                        w = window_of(it, k, per)
                        if n == 0:
                            if k % per == 0:
                                pe.wait_ge(down_loaded[k // per % ERING], loads_of(l, it, k, per, 16))
                            pe.wait_ge(hhT_ready, w + 1)
                        wd = down_ring[:, k // per % ERING, :].rearrange("p (c n) -> p c n", c=2)
                        last = mm(ps[0:WIN, 6 + half, :], hhT[:, k % 2, c * WIN:(c + 1) * WIN], wd[:, c, half * 512:(half + 1) * 512], c == 0, c == 1)
                        if n == 1:
                            last.then_inc(down_half, 1)
                        if n == 3:
                            last.then_inc(down_ready if k % per == per - 1 else wide_down, 1)

                    def turn_out(it, k, half):
                        w = window_of(it, k, per)
                        pe.wait_ge(yrow_ready[half], w + 1)
                        if half == 0 and k >= 2:
                            pe.wait_ge(ys_ready, w - 1)
                        pe.sem_inc(wait_carried, 1)
                        for c in range(half * 4, half * 4 + 4):
                            last = tr(ps[:, 2 + k % 2, c * WIN:(c + 1) * WIN], yrow[:, c * P:(c + 1) * P], WIN)
                        if half == 1:
                            last.then_inc(yT_psum, 1)

                    def step(it, k, first, ending):
                        one_before = k >= 1 and k <= (PEEL + BODY) * per
                        two_before = k >= 2
                        if not ending:
                            gate_up(it, k, 0)
                        if two_before:
                            down(it, k - 2, 3)
                        if not ending:
                            gate_up(it, k, 1)
                        if one_before:
                            turn_hidden(it, k - 1)
                        if two_before:
                            turn_out(it, k - 2, 0)
                        if not ending:
                            gate_up(it, k, 2)
                        if two_before:
                            turn_out(it, k - 2, 1)
                        if one_before:
                            down(it, k - 1, 0)
                        if not ending:
                            gate_up(it, k, 3)
                        if one_before:
                            down(it, k - 1, 1)
                            down(it, k - 1, 2)

                    windows_of(pe, per, step)

                wait_evacuated(pe, "rank")
                wait_evacuated(pe, "lg")
                pe.wait_ge(starts_ready, 2)
                most_pe = pe.value_load(most[0:1, 0:1], min_val=0, max_val=S)
                with pe.If(most_pe > windows):
                    experts(WIDE)
                with pe.Else():
                    experts(1)

                pe.wait_ge(gw_ready, 2)
                for t in range(TC):
                    for s in range(4):
                        b = 4 + t
                        last = tr(ps[:, b, s * P:(s + 1) * P], gw[:, t, s * P:(s + 1) * P])
                    last.then_inc(gwT_psum, 1)
                for s in range(4):
                    for half in range(2):
                        i = 2 * s + half
                        if i == 0:
                            wait_last_ys(pe, most_pe, windows, ys_ready)
                        if i >= 2:
                            pe.wait_ge(ytok_read[i % 2], (i - 2) // 2 + 1)
                        for j in range(4):
                            last = tr(ps[:, 6 + i % 2, j * P:(j + 1) * P], ys[:, half * 4 + j, s * P:(s + 1) * P])
                        last.then_inc(ytok_psum, 1)
                pe.wait_ge(gwT_ready, 2)
                pe.wait_ge(ytok_read[0], 4)
                pe.wait_ge(ytok_read[1], 4)
                for m in range(4):
                    free_bank(f"cb{m}")
                    for j in range(2):
                        for s in range(4):
                            last = mm(two(bank(f"cb{m}"))[:, j, :], y_tok[:, s, (2 * m + j) * P:(2 * m + j + 1) * P],
                                      gwT[:, s, :], s == 0, s == 3)
                    last.then_inc(unit_ready, 1)

                for i in range(2):
                    for t in range(TC):
                        last = tr(ps[:, 7, i * S + t * P:i * S + (t + 1) * P], prow[:, t, i * P:(i + 1) * P])
                last.then_inc(pT_tr, 1)
                pe.wait_ge(p_ready, 1)

                def embed(m):
                    wait_chunk(pe, l, "pp")
                    free_bank(f"pp{m}")
                    w = ring[:, CI["pp"] % RING, :].rearrange("p (k n) -> p k n", k=2)
                    for j in range(2):
                        for c in range(2):
                            last = mm(two(bank(f"pp{m}"))[:, j, :], w[:, c, (2 * m + j) * P:(2 * m + j + 1) * P],
                                      pT[:, c, :], c == 0, c == 1)
                    last.then_inc(unit_ready, 1)

                for m in range(4):
                    embed(m)
                stat("ple", [sq_p[:, c, :] for c in range(DC)], sq_events("ple", DC))
                project_split("pg0", "ple")
                bcast("ple")
                for m in range(1, 4):
                    project_split(f"pg{m}")
                pe.wait_ge(bcast_used, len(NORMS))
                mm(ps[:, 3, 0:1], ones[:, :], ones[:, 0:1], True, True).then_inc(engines_done, 1)
            begin(pe, DEPTH + 1)
            stat("mix", [sq_x[:, c, :] for c in range(DC)], sq_events("mix", DC))
            for i in range(4):
                for j in range(4):
                    t, c = i // 2, (i % 2) * 4 + j
                    last = tr(ps[:, 4 + i, j * P:(j + 1) * P], xT[:, c, t * P:(t + 1) * P])
                last.then_inc(tok_psum, 1)

        @block.scalar
        def _(act):
            def copy(o, i):
                return nc.scalar.activation(o, i, ACT.Copy)

            def squares(name, dst, src, units):
                for i, unit in enumerate(units):
                    if unit:
                        wait_evacuated(act, unit)
                    nc.scalar.activation(dst[:, 2 * i:2 * i + 2, :], src[:, 2 * i:2 * i + 2, :], ACT.Square).then_inc(sq_ready, 1)

            for i in range(2):
                act.wait_ge(x_tr, 2 * i + 1)
                copy(xT[:, 4 * i:4 * i + 2, :], ps[:, 2 * i, :]).then_inc(x_in, 1)
            act.wait_ge(rope_step, ROPE_STEPS)
            act.wait_ge(init_loaded, 48)
            nc.scalar.activation(sinT[NOPE:QK, :], ang[NOPE:QK, 0, :], ACT.Sin).then_inc(rope_sin, 1)
            nc.scalar.activation(cosT[NOPE:QK, :], ang[NOPE:QK, 2, :], ACT.Sin).then_inc(rope_sin, 1)

            def high(l, it, k, q, per):
                n = PIECES * window_of(it, k, per) + q
                s = k // per % ERING
                if q == 0 and k % per == 0:
                    act.wait_ge(gu_loaded[s], loads_of(l, it, k, per, 32))
                if k > 0 or q >= 2:
                    act.wait_ge(piece_used, n - 1)
                copy(wsplit[:, q % 2, 0, :, :], gu_ring[:, s, :, q * KP * FH:(q + 1) * KP * FH]).then_inc(piece_high, 1)

            def high_tiles(l, name):
                wait_chunk(act, l, name)
                for m in range(2):
                    n = 2 * SI[name] + m
                    if name not in ("kv", "pg0"):
                        before = SPLITS[SI[name] - 1]
                        act.wait_ge(high_used, n - 1)
                        act.wait_ge(tile_low, tile_value(l, before, m))
                    copy(tile_split[:, m, 0, :, :], tile_of(name, m)).then_inc(tile_high, 1)

            def high_rows(src, events, pairs=range(DC // 2)):
                for i in pairs:
                    act.wait_ge(*events[i])
                    copy(h_high[:, 2 * i:2 * i + 2, :], src[:, 2 * i:2 * i + 2, :]).then_inc(rows_high, 1)

            with act.Fori(0, DEPTH) as l:
                begin(act, l + 1)
                act.wait_ge(x_in, 4)
                squares("mix", sq_x, xT, [None] * 4)
                act.wait_ge(vec_tr, 1)
                copy(convT[:, :], ps[:, 6, 0:CROWS]).then_inc(vec_ready, 1)
                act.wait_ge(vec_tr, 2)
                copy(vecT[:, :], ps[:, 7, 0:VROWS]).then_inc(vec_ready, 1)
                high_tiles(l, "kv")
                high_rows(hT, [(h_ready, 2 * i + 2) for i in range(4)])
                high_tiles(l, "q0")
                squares("kv", sq_kv, two(tmp[:, 0, :]), ["kv"])
                high_tiles(l, "q1")
                high_tiles(l, "q2")
                high_tiles(l, "gg0")
                squares("q", sq_q, qn, [f"q{i}" for i in range(3)])
                for i in range(2):
                    high_tiles(l, f"gv{i}")
                    if i == 0:
                        high_tiles(l, "gg1")
                    wait_evacuated(act, f"gg{i}")
                    nc.scalar.activation(glu_t[i][:, 0, :], glu_t[i][:, 0, :], ACT.Sigmoid).then_inc(glu_sig, 1)
                for i in range(4):
                    wait_unit(act, l, f"kn{i}")
                    evacuates(copy(kT[0:NOPE, 2 * i:2 * i + 2, :], two(bank(f"kn{i}"))[0:NOPE, :, :]), f"kn{i}")
                for t in range(TC):
                    wait_unit(act, l, f"v{t}")
                    evacuates(copy(v[:, t, :], bank(f"v{t}")), f"v{t}")
                for i in range(4):
                    wait_unit(act, l, f"uq{i}")
                    if i == 0:
                        act.wait_ge(stat_ready, after(NORMS, "q"))
                    evacuates(copy(qT[0:QK, 2 * i:2 * i + 2, :], two(bank(f"uq{i}"))[0:QK, :, :]), f"uq{i}")
                def exponentials(h):
                    act.wait_ge(max_ready, h + 1)
                    if h == 0:
                        act.wait_ge(u_ready, 2)
                    if h >= 2:
                        act.wait_ge(pT_psum, h - 1)
                    for i, (a, b) in enumerate(((0, P), (P, 3 * P))):
                        nc.scalar.activation(probs[:, h % 2, a:b], ps[:, 4 + h % 2, a:b], ACT.Exp,
                                             bias=mx[:, h % 2, i, 1:2], scale=SCALE,
                                             accum_out=mx[:, h % 2, i, 2:3]).then_inc(exp_ready, 1)

                def copy_transposed(h):
                    act.wait_ge(pT_psum, h + 1)
                    if h >= 2:
                        act.wait_ge(pv_ready, h - 1)
                    copy(probsT[:, h % 2, :], ps[:, 6, 0:3 * P]).then_inc(pT_ready, 1)

                def copy_attention(h):
                    act.wait_ge(pv_ready, h + 1)
                    r = (h % 2) * VH
                    if h == 0:
                        act.wait_ge(q_ready, 4)
                    copy(attnT[r:r + VH, h // 2, :], ps[r:r + VH, 7, 0:S]).then_inc(attn_ready, 1)

                exponentials(0)
                exponentials(1)
                high_tiles(l, "c0")
                for h in range(HEADS):
                    copy_transposed(h)
                    if h + 2 < HEADS:
                        exponentials(h + 2)
                    if h >= 1:
                        copy_attention(h - 1)
                    if h < len(FILL):
                        high_tiles(l, SPLITS[SI[FILL[h]] + 1])
                copy_attention(HEADS - 1)

                def gate_sigmoids(m, i):
                    u = f"g{'abc'[i]}{m}"
                    if u != "gc3":
                        high_tiles(l, SPLITS[SI[u] + 1])
                    wait_evacuated(act, u)
                    nc.scalar.activation(gate_t[m % 2][:, i, :], gate_t[m % 2][:, i, :], ACT.Sigmoid).then_inc(gate_sig, 1)

                gate_sigmoids(0, 0)
                act.wait_ge(xc_ready, 1)
                nc.scalar.activation(sq_ln, conv, ACT.Square).then_inc(sq_ready, 1)
                gate_sigmoids(0, 1)
                for c in range(SCC):
                    act.wait_ge(ln_step, c + 1)
                    nc.scalar.activation(sq_ln[:, c, :], conv[:, c, :], ACT.Sigmoid, bias=vcol("lnb", c)).then_inc(ln_sig, 1)
                gate_sigmoids(0, 2)
                for m in range(1, 4):
                    for i in range(3):
                        gate_sigmoids(m, i)
                wait_unit(act, l, "gc3")
                high_rows(merged, [(merged_ready, i + 1) for i in range(4)], range(3))
                high_tiles(l, "wo0")
                high_rows(merged, [(merged_ready, i + 1) for i in range(4)], [3])
                for m in range(1, 4):
                    high_tiles(l, f"wo{m}")
                act.wait_ge(merged_ready, 4)
                squares("ffn", sq_x, xT, [f"wo{m}" for m in range(4)])
                for i in range(4):
                    act.wait_ge(tok_psum, i + 1)
                    copy(h_tok[0][:, i // 2, (i % 2) * 512:(i % 2 + 1) * 512], ps[:, 4 + i, :]).then_inc(tok_high, 1)
                wait_unit(act, l, "wo3")
                high(l, 0, 0, 0, 1)
                act.wait_ge(top_diff, 1)
                nc.scalar.activation(expd, expd, ACT.Exp).then_inc(top_exp, 1)
                for c in range(0, DC, 2):
                    act.wait_ge(gather_psum, c + 1)
                    copy(xs[:, c, 0:PAIRS], ps[:, 4 + c % 4, :]).then_inc(xs_read[0], 1)

                def experts(per):
                    def sigmoid(it, k):
                        w = window_of(it, k, per)
                        act.wait_ge(gu_summed, w + 1)
                        if k >= 1:
                            act.wait_ge(hh_ready, w)
                        nc.scalar.activation(sg, gu[:, 0:FH], ACT.Sigmoid).then_inc(sg_ready, 1)

                    def take_low(it, k):
                        w = window_of(it, k, per)
                        act.wait_ge(piece_used, PIECES * (w + 1))
                        if k >= 1:
                            act.wait_ge(gu_summed, w)
                        copy(gu_low, ps[WIN:2 * WIN, k % 2, :]).then_inc(low_ready, 1)

                    def place(it, k):
                        w = window_of(it, k, per)
                        at = act.value_load(starts[0:1, bass.ds(expert_of(it, k, per) + k % per * NE, 1)], min_val=0, max_val=PAIRS)
                        act.wait_ge(yT_psum, w + 1)
                        if k > 0:
                            act.wait_ge(ys_ready, w)
                        copy(ys[:, :, bass.ds(at, WIN)], ps[:, 2 + k % 2, :].rearrange("p (m n) -> p m n", m=DC)).then_inc(ys_ready, 1)

                    def take_rows(it, k):
                        act.wait_ge(down_half, window_of(it, k, per) + 1)
                        copy(yrow[:, 0:512], ps[0:WIN, 6, :]).then_inc(yrow_ready[0], 1)

                    def step(it, k, first, ending):
                        one_before = k >= 1 and k <= (PEEL + BODY) * per
                        two_before = k >= 2
                        if not ending and k > 0:
                            high(l, it, k, 0, per)
                        if one_before:
                            take_low(it, k - 1)
                        if not ending:
                            high(l, it, k, 1, per)
                        if one_before:
                            sigmoid(it, k - 1)
                        if two_before:
                            take_rows(it, k - 2)
                        if not ending:
                            high(l, it, k, 2, per)
                            high(l, it, k, 3, per)
                        if two_before:
                            place(it, k - 2)

                    windows_of(act, per, step)

                act.wait_ge(starts_ready, 2)
                act.wait_ge(gather_psum, DC)
                act.wait_ge(xs_read[1], 4)
                act.wait_ge(xs_read[0], 4)
                copy(xsplit[:, 0, :, 0:WIN], xs[:, :, 0:WIN]).then_inc(first_high, 1)
                most_act = act.value_load(most[0:1, 0:1], min_val=0, max_val=S)
                with act.If(most_act > windows):
                    experts(WIDE)
                with act.Else():
                    experts(1)
                for i in (0, 2, 4, 6):
                    act.wait_ge(ytok_psum, i + 1)
                    copy(y_tok[:, i // 2, 0:512], ps[:, 6, :]).then_inc(ytok_read[0], 1)
                act.wait_ge(pT_tr, 1)
                copy(pT[:, :, :], two(ps[:, 7, :])).then_inc(p_ready, 1)
                high_tiles(l, "pg0")
                squares("ple", sq_p, xT, [f"cb{m}" for m in range(4)])
                for m in range(4):
                    wait_unit(act, l, f"pp{m}")
                    evacuates(copy(ppt[m], bank(f"pp{m}")), f"pp{m}")
                high_rows(hT, [(h_ready, 2 * DC + 2 * i + 2) for i in range(4)])
                for m in range(4):
                    if m < 3:
                        high_tiles(l, f"pg{m + 1}")
                    wait_evacuated(act, f"pg{m}")
                    nc.scalar.activation(ple_t[m % 2], ple_t[m % 2], ACT.Sigmoid).then_inc(psig_ready, 1)
                act.wait_ge(psig_ready, 4)
                nc.scalar.activation(last_act[:, :], ones[:, 0:1], ACT.Square).then_inc(engines_done, 1)
            begin(act, DEPTH + 1)
            squares("mix", sq_x, xT, [None] * 4)


        @block.gpsimd
        def _(pool):
            nc.gpsimd.memset(ones[:, :], 1.0).then_inc(const_set, 1)
            nc.gpsimd.memset(mhalf[:, :], -0.5).then_inc(const_set, 1)
            pool.wait_ge(const_set, 2)
            pool.sem_inc(layer_over, 1)

            def power(name):
                i = NORMS.index(name)
                pool.wait_ge(ms_ready, after(POWS, name))
                nc.gpsimd.tensor_tensor(col[:, i, 1, :], col[:, i, 0, :], mhalf[:, :], ALU.pow).then_inc(pow_ready, 1)

            with pool.Fori(0, DEPTH) as l:
                nc.gpsimd.memset(upad[:, :, 0:KC - 1], 0.0).then_inc(pad_zero, 1)
                power("mix")
                power("kv")
                wait_evacuated(pool, "rotk")
                pool.wait_ge(rope_sin, 2)
                nc.gpsimd.tensor_tensor(kr[NOPE:QK, 0, :], kr[NOPE:QK, 0, :], cosT[NOPE:QK, :], ALU.mult).then_inc(q_cos, 1)
                pool.wait_ge(q_cos, 1)
                nc.gpsimd.tensor_tensor(kr[NOPE:QK, 0, :], kr[NOPE:QK, 0, :], kr[NOPE:QK, 1, :], ALU.add).then_inc(q_cos, 1)
                pool.wait_ge(q_cos, 2)
                nc.gpsimd.tensor_copy(kT[NOPE:QK, :, :], kr[NOPE:QK, 0, :].unsqueeze(1).to_broadcast([ROPE, HEADS, S])).then_inc(k_ready, 1)
                pool.wait_ge(k_ready, 1)
                power("q")
                for i in range(2):
                    pool.wait_ge(glu_sig, i + 1)
                    wait_evacuated(pool, f"gv{i}")
                    if i == 0:
                        pool.wait_ge(pad_zero, 1)
                    nc.gpsimd.tensor_tensor(upad[:, 2 * i:2 * i + 2, KC - 1:], two(glu_t[i][:, 1, :]), two(glu_t[i][:, 0, :]), ALU.mult).then_inc(u_ready, 1)
                pool.wait_ge(u_ready, 2)
                for i in range(4):
                    q2 = qT[NOPE:QK, 2 * i:2 * i + 2, :]
                    wait_evacuated(pool, f"rot{i}")
                    nc.gpsimd.tensor_tensor(q2, q2, cosT[NOPE:QK, :].unsqueeze(1).to_broadcast([ROPE, 2, S]), ALU.mult).then_inc(q_cos, 1)
                    pool.wait_ge(q_cos, i + 3)
                    nc.gpsimd.tensor_tensor(q2, q2, rtmp[NOPE:QK, i % 2, :, :], ALU.add).then_inc(q_ready, 1)
                pool.wait_ge(q_ready, 4)
                wait_evacuated(pool, "uq3")
                nc.gpsimd.memset(scu[:, :, 0:KA - 1], 0.0).then_inc(pad_zero, 1)
                for h in range(HEADS):
                    pool.wait_ge(recip_ready, h + 1)
                    pool.wait_ge(exp_ready, 2 * (h + 1))
                    for i, (a, b) in enumerate(((0, P), (P, 3 * P))):
                        nc.gpsimd.tensor_scalar(probs[:, h % 2, a:b], probs[:, h % 2, a:b], mx[:, h % 2, i, 0:1], None,
                                                ALU.mult).then_inc(probs_ready, 1)
                    if h in (2, 5):
                        i = h // 3
                        wait_evacuated(pool, f"u{i}")
                        half = scu[:, 2 * i:2 * i + 2, KA - 1:]
                        nc.gpsimd.tensor_tensor(half, half, two(tmp[:, 0, :]), ALU.mult).then_inc(scu_ready, 1)
                power("lnv")
                for m in range(4):
                    g = gate_t[m % 2]
                    wait_evacuated(pool, f"ya{m}")
                    wait_evacuated(pool, f"yb{m}")
                    nc.gpsimd.tensor_tensor(merged[:, 2 * m:2 * m + 2, :], two(g[:, 0, :]), two(g[:, 1, :]), ALU.add).then_inc(merge_step, 1)
                    pool.wait_ge(merge_step, m + 1)
                    wait_evacuated(pool, f"yc{m}")
                    nc.gpsimd.tensor_tensor(merged[:, 2 * m:2 * m + 2, :], merged[:, 2 * m:2 * m + 2, :], two(g[:, 2, :]), ALU.add).then_inc(merged_ready, 1)
                power("ffn")
                pool.wait_ge(stat_ready, after(NORMS, "ffn"))
                nc.gpsimd.memset(xs[:, :, PAIRS:SLOTS], 0.0).then_inc(xs_pad, 1)

                def experts(per):
                    def window(it, k, first, ending):
                        if ending or k == 0:
                            return
                        w, b = window_of(it, k, per), k % 2
                        at = pool.value_load(starts[0:1, bass.ds(expert_of(it, k, per) + k % per * NE, 1)], min_val=0, max_val=PAIRS)
                        if k >= 2:
                            pool.wait_ge(piece_used, PIECES * (w - 1))
                        nc.gpsimd.tensor_copy(xsplit[:, b, :, 0:WIN], xs[:, :, bass.ds(at, WIN)]).then_inc(xw_high, 1)
                        pool.wait_ge(xw_high, w)
                        pool.sem_inc(wait_carried, 1)
                        nc.gpsimd.tensor_tensor(xsplit[:, b, :, WIN:2 * WIN], xs[:, :, bass.ds(at, WIN)],
                                                xsplit[:, b, :, 0:WIN].bitcast(F32), ALU.subtract).then_inc(xw_ready, 1)

                    windows_of(pool, per, window)

                pool.wait_ge(xs_read[0], 4)
                pool.wait_ge(xs_read[1], 4)
                pool.wait_ge(xs_pad, 1)
                pool.wait_ge(gw_ready, 2)
                pool.wait_ge(starts_ready, 2)
                most_pool = pool.value_load(most[0:1, 0:1], min_val=0, max_val=S)
                with pool.If(most_pool > windows):
                    experts(WIDE)
                with pool.Else():
                    experts(1)
                power("ple")
                for m in range(3):
                    pool.wait_ge(pmul_ready, m + 1)
                    x2 = xT[:, 2 * m:2 * m + 2, :]
                    if m == 0:
                        pool.wait_ge(h_ready, 3 * DC)
                        pool.wait_ge(sq_ready, len(SQUARES))
                    nc.gpsimd.tensor_tensor(x2, x2, two(ple_t[m % 2]), ALU.add).then_inc(merge_step, 1)
                pool.wait_ge(merge_step, 8)
                pool.wait_ge(engines_done, 3)
                pool.sem_clear(range(zeroed[0].num, zeroed[-1].num + 1))
                pool.sem_inc(layer_over, 1)
            power("mix")

        @block.vector
        def _(dve):
            TT, TS, STT = nc.vector.tensor_tensor, nc.vector.tensor_scalar, nc.vector.scalar_tensor_tensor
            for i in range(2):
                dve.wait_ge(x_tr, 2 * i + 2)
                nc.vector.tensor_copy(xT[:, 4 * i + 2:4 * i + 4, :], ps[:, 2 * i + 1, :]).then_inc(x_in, 1)

            rows = slice(NOPE, QK)
            n_rope = [0]

            def rstep(ins):
                n_rope[0] += 1
                ins.then_inc(rope_step, 1)
                dve.wait_ge(rope_step, n_rope[0])

            dve.wait_ge(init_loaded, 48)
            a0, a1, a2 = (ang[rows, i, :] for i in (1, 3, 2))
            A = ang[rows, 0, :]
            rstep(nc.vector.tensor_copy(a0, A.bitcast(I32)))
            rstep(TS(a0, a0, freq, None, ALU.mult))
            rstep(TS(a1, a0, INV_2PI, ROUND, ALU.mult, ALU.add))
            rstep(TS(a1, a1, ROUND, None, ALU.subtract))
            rstep(STT(a0, a1, -TWO_PI[0], a0, ALU.mult, ALU.add))
            rstep(STT(a0, a1, -TWO_PI[1], a0, ALU.mult, ALU.add))
            rstep(STT(a0, a1, -TWO_PI[2], a0, ALU.mult, ALU.add))
            rstep(TS(A, a0, PI_IN, -PI_IN, ALU.min, ALU.max))
            rstep(STT(a2, A, -1.0, A, ALU.mult, ALU.min))
            rstep(TS(a2, a2, HALF_PI, None, ALU.add))

            def mean(name, n):
                i = NORMS.index(name)
                dve.wait_ge(stat_ready, after(NORMS, name))
                if name == "lnm":
                    TS(col[:, i, 1, :], ps[:, 3, 0:TC], 1.0 / n, None, ALU.mult).then_inc(mean_ready, 1)
                else:
                    TS(col[:, i, 0, :], ps[:, 3, 0:TC], 1.0 / n, EPS, ALU.mult, ALU.add).then_inc(ms_ready, 1)

            def diagonal(name):
                i = NORMS.index(name)
                if name == "lnm":
                    dve.wait_ge(mean_ready, 1)
                else:
                    dve.wait_ge(pow_ready, after(POWS, name))
                TS(diag[:, 0, :], ident, col[:, i, 1, 0:1], None, ALU.mult)
                TS(diag[:, 1, :], ident, col[:, i, 1, 1:2], None, ALU.mult).then_inc(diag_ready, 1)

            def take_row(name, dst):
                dve.wait_ge(bcast_ready, after(NORMS, name))
                nc.vector.tensor_copy(dst[:, :], ps[:, 3, S:2 * S]).then_inc(bcast_used, 1)
                dve.wait_ge(bcast_used, after(NORMS, name))

            def low(it, k, q, per):
                s = k // per % ERING
                dve.wait_ge(piece_high, PIECES * window_of(it, k, per) + q + 1)
                ins = TT(wsplit[:, q % 2, 1, :, :], gu_ring[:, s, :, q * KP * FH:(q + 1) * KP * FH],
                         wsplit[:, q % 2, 0, :, :].bitcast(F32), ALU.subtract)
                if q < PIECES - 1:
                    ins.then_inc(piece_low, 1)
                else:
                    ins.then_inc(gu_taken if k % per == per - 1 else wide_taken, 1)

            def low_tile(l, name, m):
                dve.wait_ge(tile_high, 2 * SI[name] + m + 1)
                if name not in ("kv", "pg0"):
                    if m == 0:
                        dve.wait_ge(tile_used, SI[name])
                    else:
                        wait_unit(dve, l, SPLITS[SI[name] - 1])
                TT(tile_split[:, m, 1, :, :], tile_of(name, m), tile_split[:, m, 0, :, :].bitcast(F32), ALU.subtract).then_inc(tile_low, 1)

            def low_tiles(l, name):
                for m in range(2):
                    low_tile(l, name, m)

            def low_rows(src, rows, pairs=range(DC // 2)):
                for i in pairs:
                    dve.wait_ge(rows_high, DC // 2 * ROWS.index(rows) + i + 1)
                    TT(h_low[:, 2 * i:2 * i + 2, :], src[:, 2 * i:2 * i + 2, :], h_high[:, 2 * i:2 * i + 2, :].bitcast(F32),
                       ALU.subtract).then_inc(rows_low, 1)

            with dve.Fori(0, DEPTH) as l:
                begin(dve, l + 1)
                dve.wait_ge(x_in, 4)
                dve.wait_ge(vec_ready, 2)
                for c in range(DC):
                    TS(hT[:, c, :], xT[:, c, :], vcol("mix", c), None, ALU.mult).then_inc(h_ready, 1)

                def scale_out(name, dst):
                    ahead = name in SI and name not in ("gv1", "gc3", "pg3")
                    if ahead:
                        low_tile(l, SPLITS[SI[name] + 1], 0)
                    wait_unit(dve, l, name)
                    evacuates(TT(dst, two(bank(name)), bc2(), ALU.mult), name)
                    if ahead:
                        low_tile(l, SPLITS[SI[name] + 1], 1)

                low_rows(hT, "mix")
                low_tiles(l, "kv")

                mean("mix", D)
                diagonal("mix")
                take_row("mix", bc)
                scale_out("kv", two(tmp[:, 0, :]))
                wait_unit(dve, l, "kr")
                evacuates(TT(kr[0:QK, 0, :], bank("kr")[0:QK, 0:S], bc[0:QK, :], ALU.mult), "kr")
                scale_out("q0", qn[:, 0:2, :])
                scale_out("q1", qn[:, 2:4, :])
                mean("kv", KVL)
                diagonal("kv")
                scale_out("q2", qn[:, 4:6, :])
                take_row("kv", bcs)
                for c in range(2):
                    STT(kvn[:, c, :], two(tmp[:, 0, :])[:, c, :], vcol("kv", c), bcs[:, :], ALU.mult, ALU.mult).then_inc(kvn_ready, 1)
                wait_unit(dve, l, "rotk")
                dve.wait_ge(rope_sin, 2)
                evacuates(TT(kr[NOPE:QK, 1, :], bank("rotk")[NOPE:QK, 0:S], sinT[NOPE:QK, :], ALU.mult), "rotk")
                scale_out("gg0", two(glu_t[0][:, 0, :]))
                mean("q", QL)
                diagonal("q")
                scale_out("gv0", two(glu_t[0][:, 1, :]))
                take_row("q", bcs)
                for c in range(6):
                    STT(qn[:, c, :], qn[:, c, :], vcol("q", c), bcs[:, :], ALU.mult, ALU.mult).then_inc(qn_ready, 1)
                scale_out("gg1", two(glu_t[1][:, 0, :]))
                scale_out("gv1", two(glu_t[1][:, 1, :]))

                def rotated(i):
                    wait_unit(dve, l, f"rot{i}")
                    if i >= 2:
                        dve.wait_ge(q_ready, i - 1)
                    evacuates(TT(rtmp[NOPE:QK, i % 2, :, :], two(bank(f"rot{i}"))[NOPE:QK, :, :],
                                 sinT[NOPE:QK, :].unsqueeze(1).to_broadcast([ROPE, 2, S]), ALU.mult), f"rot{i}")

                def maximum(h):
                    dve.wait_ge(score_ready, h + 1)
                    if h >= 2:
                        dve.wait_ge(probs_ready, 2 * (h - 1))
                    b = 4 + h % 2
                    edge = two(ps[:, b, :])[:, :, 0:P]
                    TT(edge, edge, causal.unsqueeze(1).to_broadcast([P, 2, P]), ALU.add).then_inc(mask_step, 1)
                    dve.wait_ge(mask_step, 2 * h + 1)
                    nc.vector.reduce_max(mx[:, h % 2, 0, 0:1], ps[:, b, 0:P], AX.X)
                    nc.vector.reduce_max(mx[:, h % 2, 1, 0:1], ps[:, b, P:3 * P], AX.X).then_inc(mask_step, 1)
                    dve.wait_ge(mask_step, 2 * h + 2)
                    TS(mx[:, h % 2, :, 1], mx[:, h % 2, :, 0], -SCALE, None, ALU.mult).then_inc(max_ready, 1)

                taps = [(k, c) for k in range(KC) for c in range(SCC)]

                def conv_taps(first, count):
                    for n in range(first, min(first + count, len(taps))):
                        k, c = taps[n]
                        w = convT[:, k * SCC + c:k * SCC + c + 1]
                        if k == 0:
                            TS(conv[:, c, :], upad[:, c, 0:S], w, None, ALU.mult).then_inc(conv_step, 1)
                        else:
                            dve.wait_ge(conv_step, n - SCC + 1)
                            STT(conv[:, c, :], upad[:, c, k:k + S], w, conv[:, c, :], ALU.mult, ALU.add).then_inc(conv_step, 1)

                def short_conv(i):
                    dve.wait_ge(scu_ready, i + 1)
                    wait_evacuated(dve, f"b{i}")
                    t = two(tmp[:, 1, :])
                    for j in range(2):
                        c = 2 * i + j
                        TS(t[:, j, :], scu[:, c, 0:S], vcol("ca", c), None, ALU.mult).then_inc(short_step, 1)
                    for k in range(1, KA):
                        for j in range(2):
                            c = 2 * i + j
                            dve.wait_ge(short_step, 6 * i + 2 * (k - 1) + j + 1)
                            STT(t[:, j, :], scu[:, c, k:k + S], vcol("ca", k * SCC + c), t[:, j, :], ALU.mult, ALU.add).then_inc(short_step, 1)
                    dve.wait_ge(short_step, 6 * (i + 1))
                    y2 = ya[:, 2 * i:2 * i + 2, :]
                    TT(y2, y2, t, ALU.mult).then_inc(ya_ready, 1)

                def reciprocal(h):
                    dve.wait_ge(exp_ready, 2 * (h + 1))
                    nc.vector.reciprocal(mx[:, h % 2, :, 0], mx[:, h % 2, :, 2]).then_inc(recip_ready, 1)

                dve.wait_ge(u_ready, 2)
                dve.wait_ge(k_ready, 1)
                at = 0
                for i, n in enumerate(TAPS_BEFORE):
                    conv_taps(at, n)
                    at += n
                    if i < 2:
                        rotated(i)
                PER_HEAD = -(-(len(taps) - at) // len(FILL))
                maximum(0)
                maximum(1)
                rotated(2)
                reciprocal(0)
                low_tiles(l, "c0")
                rotated(3)
                for h in range(HEADS):
                    if h < len(FILL):
                        conv_taps(at, PER_HEAD // 2)
                        reciprocal(h + 1)
                        maximum(h + 2)
                        conv_taps(at + PER_HEAD // 2, PER_HEAD - PER_HEAD // 2)
                        at += PER_HEAD
                    if h == len(FILL) - 1:
                        reciprocal(HEADS - 1)
                    if h in (3, 6):
                        short_conv(h // 3 - 1)
                    if h < len(FILL):
                        kind, i = FILL[h][0], h // 3
                        if h == 0:
                            dve.wait_ge(pad_zero, 2)
                        if kind == "c":
                            scale_out(FILL[h], scu[:, 2 * i:2 * i + 2, KA - 1:])
                        if kind == "u":
                            if i:
                                dve.wait_ge(scu_ready, 1)
                            scale_out(FILL[h], two(tmp[:, 0, :]))
                        if kind == "b":
                            scale_out(FILL[h], ya[:, 2 * i:2 * i + 2, :])

                def gate_out(x, m):
                    if m == 0:
                        dve.wait_ge(pv_ready, HEADS)
                    if m >= 2:
                        dve.wait_ge(merged_ready, m - 1)
                    scale_out(f"g{x}{m}", two(gate_t[m % 2][:, "abc".index(x), :]))

                def gate_mul(x, m):
                    wait_unit(dve, l, f"y{x}{m}")
                    i = "abc".index(x)
                    dve.wait_ge(gate_sig, 3 * m + i + 1)
                    g = gate_t[m % 2][:, i, :]
                    evacuates(TT(g, g, bank(f"y{x}{m}"), ALU.mult), f"y{x}{m}")

                for m in range(4):
                    gate_out("a", m)
                    if m == 0:
                        mean("lnm", SC)
                        diagonal("lnm")
                    gate_mul("a", m)
                    if m == 0:
                        take_row("lnm", bcs)
                        TT(conv, conv, bcs[:, :].unsqueeze(1).to_broadcast([P, SCC, S]), ALU.subtract).then_inc(xc_ready, 1)
                        mean("lnv", SC)
                        diagonal("lnv")
                    gate_out("b", m)
                    gate_mul("b", m)
                    if m == 0:
                        take_row("lnv", bcs)
                        for c in range(SCC):
                            STT(conv[:, c, :], conv[:, c, :], vcol("lng", c), bcs[:, :], ALU.mult, ALU.mult).then_inc(ln_step, 1)
                        for c in range(SCC):
                            dve.wait_ge(ln_sig, c + 1)
                            STT(conv[:, c, :], conv[:, c, :], vcol("lnb", c), sq_ln[:, c, :], ALU.add, ALU.mult).then_inc(yc_ready, 1)
                    gate_out("c", m)
                    if m == 3:
                        low_rows(merged, "wo", range(3))
                    gate_mul("c", m)
                low_tiles(l, "wo0")
                low_rows(merged, "wo", [3])

                def add_to_x(unit, m):
                    if unit[:2] == "wo" and m < 3:
                        low_tile(l, f"wo{m + 1}", 0)
                    wait_unit(dve, l, unit)
                    x2 = xT[:, 2 * m:2 * m + 2, :]
                    evacuates(TT(x2, two(bank(unit)), x2, ALU.add), unit)
                    if unit[:2] == "wo" and m < 3:
                        low_tile(l, f"wo{m + 1}", 1)

                for m in range(4):
                    add_to_x(f"wo{m}", m)
                mean("ffn", D)
                diagonal("ffn")
                take_row("ffn", bcs)
                for c in range(DC):
                    STT(hT[:, c, :], xT[:, c, :], vcol("ffn", c), bcs[:, :], ALU.mult, ALU.mult).then_inc(h_ready, 1)

                n_step = [0]

                def step(ins):
                    n_step[0] += 1
                    ins.then_inc(dve_step, 1)
                    dve.wait_ge(dve_step, n_step[0])

                def b3(t, n):
                    return t.to_broadcast([P, TC, n])

                def io(n):
                    return iota[:, 0:n].unsqueeze(1).to_broadcast([P, TC, n])

                def first_of_max(x, n, mxt, eq, val, mn, hot):
                    step(nc.vector.reduce_max(mxt, x, AX.X))
                    step(TT(eq, x, b3(mxt, n), ALU.is_equal))
                    step(STT(val, eq, -float(PAIRS), io(n), ALU.mult, ALU.add))
                    step(nc.vector.tensor_reduce(mn, val, AX.X, ALU.min))
                    return TT(hot, val, b3(mn, n), ALU.is_equal)

                wait_unit(dve, l, "lg")
                lgp = bank("lg")[:, 0:TC * (NG + NE)].rearrange("p (t n) -> p t n", t=TC)
                evacuates(TT(logit, lgp, b_rt[:, :, :], ALU.add), "lg")
                wait_evacuated(dve, "lg")
                step(first_of_max(logit[:, :, 0:NG], NG, gmax, geq, gval, gmin, gone))
                step(TS(gpen, gone, BIG, -BIG, ALU.mult, ALU.add))
                for t in range(TC):
                    last = TT(masked[:, t, :].rearrange("p (g e) -> p g e", g=NG), logit[:, t, NG:].rearrange("p (g e) -> p g e", g=NG),
                              gpen[:, t, :].unsqueeze(2).to_broadcast([P, NG, EPG]), ALU.add)
                step(last)
                step(first_of_max(masked, NE, top[0], teq[0], tval[0], tmin[0], one[0]))
                step(STT(masked2, one[0], -3.0 * BIG, masked, ALU.mult, ALU.add))
                step(first_of_max(masked2, NE, top[1], teq[1], tval[1], tmin[1], one[1]))
                TT(chosen, one[0], one[1], ALU.add).then_inc(onehot_ready, 1)
                TT(expd[:, :, 0:NG], logit[:, :, 0:NG], b3(gmax, NG), ALU.subtract)
                TT(expd[:, :, NG:NG + 1], top[1], top[0], ALU.subtract).then_inc(top_diff, 1)
                for f in prefix:
                    nc.vector.memset(f[:, 0:16], 0.0)
                for i in range(4):
                    dve.wait_ge(tok_high, i + 1)
                    at = slice((i % 2) * 512, (i % 2 + 1) * 512)
                    TT(h_tok[1][:, i // 2, at], ps[:, 4 + i, :], h_tok[0][:, i // 2, at].bitcast(F32), ALU.subtract).then_inc(tok_low, 1)
                wait_unit(dve, l, "rank")
                evacuates(nc.vector.tensor_copy(ranks, bank("rank")[:, 0:3 * NE]), "rank")
                wait_evacuated(dve, "rank")
                count = ranks[:, 2 * NE:3 * NE]
                step(nc.vector.tensor_copy(prefix[0][:, 16:48], count))
                for i, sh in enumerate((1, 2, 4, 8, 16)):
                    a, b = prefix[i % 2], prefix[(i + 1) % 2]
                    step(TT(b[:, 16:48], a[:, 16:48], a[:, 16 - sh:48 - sh], ALU.add))
                upto = prefix[1][:, 16:48]
                step(TT(off, upto, count, ALU.subtract))
                step(TT(base, ranks[:, 0:2 * NE].rearrange("p (t n) -> p t n", t=TC), off.unsqueeze(1).to_broadcast([P, TC, NE]), ALU.add))
                TT(prod[0], base, one[0], ALU.mult)
                step(TT(prod[1], base, one[1], ALU.mult))
                nc.vector.reduce_sum(pos[0], prod[0], AX.X)
                step(nc.vector.reduce_sum(pos[1], prod[1], AX.X))
                for t in range(TC):
                    step(TS(sel_t[:, t, :], iota, pos[0][:, t, :], None, ALU.is_equal))
                    STT(sel[:, t, :], iota, pos[1][:, t, :], sel_t[:, t, :], ALU.is_equal, ALU.add).then_inc(sel_ready, 1)
                for j in range(WIDE):
                    last = STT(starts[0:1, j * NE:(j + 1) * NE], off[0:1, :], float(j * WIN), upto[0:1, :], ALU.add, ALU.min)
                last.then_inc(starts_ready, 1)
                nc.vector.reduce_max(most[0:1, 0:1], count[0:1, :], AX.X).then_inc(starts_ready, 1)
                dve.wait_ge(top_exp, 1)
                nc.vector.reduce_sum(gsum, expd[:, :, 0:NG], AX.X)
                step(TS(dplus, expd[:, :, NG:NG + 1], 1.0, None, ALU.add))
                step(TT(gsum, gsum, dplus, ALU.mult))
                step(nc.vector.reciprocal(weight[0], gsum))
                step(TT(weight[1], weight[0], expd[:, :, NG:NG + 1], ALU.mult))
                dve.wait_ge(sel_ready, 2)
                for t in range(TC):
                    TS(gw[:, t, :], iota, pos[0][:, t, :], weight[0][:, t, :], ALU.is_equal, ALU.mult)
                    step(TS(sel_t[:, t, :], iota, pos[1][:, t, :], weight[1][:, t, :], ALU.is_equal, ALU.mult))
                    TT(gw[:, t, :], gw[:, t, :], sel_t[:, t, :], ALU.add).then_inc(gw_ready, 1)
                for c in range(1, DC, 2):
                    dve.wait_ge(gather_psum, c + 1)
                    nc.vector.tensor_copy(xs[:, c, 0:PAIRS], ps[:, 4 + c % 4, :]).then_inc(xs_read[1], 1)

                def experts(per):
                    def sum_up(it, k):
                        dve.wait_ge(low_ready, window_of(it, k, per) + 1)
                        TT(gu, ps[0:WIN, k % 2, :], gu_low, ALU.add).then_inc(gu_summed, 1)

                    def hidden(it, k):
                        w = window_of(it, k, per)
                        dve.wait_ge(sg_ready, w + 1)
                        TT(hh, sg, gu[:, 0:FH], ALU.mult).then_inc(hh_part, 1)
                        dve.wait_ge(hh_part, w + 1)
                        TT(hh, hh, gu[:, FH:2 * FH], ALU.mult).then_inc(hh_ready, 1)

                    def take_hidden(it, k):
                        dve.wait_ge(hh_tr, window_of(it, k, per) + 1)
                        nc.vector.tensor_copy(hhT[:, k % 2, :], ps[:, 4 + k % 2, 0:2 * WIN]).then_inc(hhT_ready, 1)

                    def take_rows(it, k):
                        wait_down(dve, l, it, k, per)
                        nc.vector.tensor_copy(yrow[:, 512:1024], ps[0:WIN, 7, :]).then_inc(yrow_ready[1], 1)

                    def step(it, k, first, ending):
                        one_before = k >= 1 and k <= (PEEL + BODY) * per
                        two_before = k >= 2
                        if not ending and k > 0:
                            low(it, k, 0, per)
                        if one_before:
                            sum_up(it, k - 1)
                        if not ending:
                            low(it, k, 1, per)
                        if one_before:
                            hidden(it, k - 1)
                        if not ending:
                            low(it, k, 2, per)
                        if two_before:
                            take_rows(it, k - 2)
                        if one_before:
                            take_hidden(it, k - 1)
                        if not ending:
                            low(it, k, 3, per)

                    windows_of(dve, per, step)

                dve.wait_ge(first_high, 1)
                TT(xsplit[:, 0, :, WIN:2 * WIN], xs[:, :, 0:WIN], xsplit[:, 0, :, 0:WIN].bitcast(F32), ALU.subtract).then_inc(first_ready, 1)
                low(0, 0, 0, 1)
                dve.wait_ge(starts_ready, 2)
                most_dve = dve.value_load(most[0:1, 0:1], min_val=0, max_val=S)
                with dve.If(most_dve > windows):
                    experts(WIDE)
                with dve.Else():
                    experts(1)
                for t in range(TC):
                    dve.wait_ge(gwT_psum, t + 1)
                    nc.vector.tensor_copy(gwT[:, :, t * P:(t + 1) * P], ps[:, 4 + t, :].rearrange("p (s n) -> p s n", s=4)).then_inc(gwT_ready, 1)
                for i in (1, 3, 5, 7):
                    dve.wait_ge(ytok_psum, i + 1)
                    nc.vector.tensor_copy(y_tok[:, i // 2, 512:1024], ps[:, 7, :]).then_inc(ytok_read[1], 1)
                for m in range(4):
                    add_to_x(f"cb{m}", m)
                    wait_evacuated(dve, f"cb{m}")
                    for c in (2 * m, 2 * m + 1):
                        TS(hT[:, c, :], xT[:, c, :], vcol("ple", c), None, ALU.mult).then_inc(h_ready, 1)
                low_rows(hT, "ple")
                low_tiles(l, "pg0")
                mean("ple", D)
                diagonal("ple")
                take_row("ple", bc)

                def ple_mul(m):
                    dve.wait_ge(psig_ready, m + 1)
                    wait_evacuated(dve, f"pp{m}")
                    TT(ple_t[m % 2], ple_t[m % 2], ppt[m], ALU.mult).then_inc(pmul_ready, 1)

                for m in range(4):
                    if m >= 2:
                        dve.wait_ge(merge_step, 4 + m - 1)
                    scale_out(f"pg{m}", two(ple_t[m % 2]))
                    if m >= 1:
                        ple_mul(m - 1)
                ple_mul(3)
                dve.wait_ge(pmul_ready, 4)
                TT(xT[:, 6:8, :], xT[:, 6:8, :], two(ple_t[1]), ALU.add).then_inc(merge_step, 1)
                nc.vector.tensor_copy(last_dve[:, :], ones[:, 0:1]).then_inc(engines_done, 1)
            begin(dve, DEPTH + 1)
            mean("mix", D)
            dve.wait_ge(pow_ready, 1)
            dve.wait_ge(init_loaded, 64)
            for t in range(TC):
                for half in range(2):
                    dve.wait_ge(tok_psum, 2 * t + half + 1)
                    last = STT(xout[:, t, half * 512:(half + 1) * 512], ps[:, 4 + 2 * t + half, :], col[:, 0, 1, t:t + 1],
                               gfull[:, half * 512:(half + 1) * 512], ALU.mult, ALU.mult)
                last.then_inc(pmul_ready, 1)


_INS = ["x", "p", "positions", "ln_mix_g", "w_in", "conv_a_w", "w_out_a", "q_norm_g", "w_uq", "kv_norm_g", "w_ukv",
        "w_out_b", "conv_c_w", "ln_c_g", "ln_c_b", "w_out_c", "w_o", "ln_ffn_g", "w_route_grp", "b_route_grp",
        "w_route_exp", "b_route_exp", "w_exp_gate", "w_exp_up", "w_exp_down", "ln_ple_g", "w_ple_gate", "w_ple",
        "final_norm_g"]


def constants():
    import numpy as np
    c = np.zeros((P, C_COLS), np.float32)
    c[:, C_ID:C_ID + P] = np.eye(P)
    c[:, C_UP:C_UP + P] = np.triu(np.ones((P, P)), 1)
    c[:, C_CAUSAL:C_CAUSAL + P] = np.where(np.tril(np.ones((P, P))) > 0, 0.0, -BIG)
    half = ROPE // 2
    for i in range(half):
        c[NOPE + half + i, C_ROT + NOPE + i] = -1.0
        c[NOPE + i, C_ROT + NOPE + half + i] = 1.0
        f = np.float32(10000.0) ** np.float32(-2.0 * i / ROPE)
        c[NOPE + i, C_FREQ] = c[NOPE + half + i, C_FREQ] = f
    c[:, C_IOTA:C_IOTA + PAIRS] = np.arange(PAIRS)
    return c


def kernel(**inputs):
    import numpy as _np
    import concourse.bacc as _bacc
    from concourse import mybir as _mybir
    from concourse.bass_utils import run_bass_kernel_spmd as _run

    nc = _bacc.Bacc("TRN2", target_bir_lowering=False, num_devices=1)
    arrays, args = {}, []
    for name in _INS:
        a = _np.ascontiguousarray(inputs[name])
        arrays[f"in_{name}_dram"] = a
        args.append(nc.dram_tensor(f"in_{name}_dram", a.shape, _mybir.dt.from_np(a.dtype), kind="ExternalInput").ap())
    c = constants()
    arrays["in_consts_dram"] = c
    args.append(nc.dram_tensor("in_consts_dram", c.shape, _mybir.dt.float32, kind="ExternalInput").ap())
    args.append(nc.dram_tensor("out_0_dram", (1, S, D), _mybir.dt.float32, kind="ExternalOutput").ap())
    program(nc, *args)
    r = _run(nc, [arrays], core_ids=[0])
    return r.results[0]["out_0_dram"]
```
